# Optimizing a Trainium2 kernel written in Bass

```python
import math
import jax
import jax.numpy as jnp
from jax import lax
import numpy as np

D_MODEL = 1024
BATCH = 1
SEQ = 256
DEPTH = 2

N_META = 16
EPS = 1e-6

HY_WIDTH = D_MODEL
HY_ORDER = 2
HY_SHORT = 3
HY_BANDS = 16
HY_EMB = 2 * HY_BANDS + 1
HY_FILTER_HIDDEN = 64
HY_DECAY_PCT_SHORT = 0.3
HY_DECAY_PCT_LONG = 1.5
HY_DECAY_TARGET = 1e-2
HY_FILTER_OUT_SCALE = 0.02

LRU_WIDTH = D_MODEL
LRU_BLOCKS = 8
LRU_BLOCK = LRU_WIDTH // LRU_BLOCKS
LRU_CONV = 4
LRU_C = 8.0
LRU_A_MIN = 0.9
LRU_A_MAX = 0.999

RET_HEADS = 4
RET_DK = D_MODEL // RET_HEADS
RET_DV = D_MODEL // RET_HEADS
RET_WIDTH = RET_HEADS * RET_DV
RET_CHUNK = 128
ROPE_BASE = 10000.0

N_BRANCH = 3
BRANCH_WIDTH = D_MODEL

D_FF = ((8 * D_MODEL + 3 * 256 - 1) // (3 * 256)) * 256

OFF_LRU_X = HY_ORDER * HY_WIDTH + HY_WIDTH
OFF_LRU_G = OFF_LRU_X + LRU_WIDTH
OFF_Q = OFF_LRU_G + LRU_WIDTH
OFF_K = OFF_Q + RET_HEADS * RET_DK
OFF_V = OFF_K + RET_HEADS * RET_DK
OFF_G = OFF_V + RET_WIDTH
OFF_MERGE = OFF_G + RET_WIDTH
D_IN = OFF_MERGE + N_BRANCH * D_MODEL

kernel_name = "bidir_hyena_rglru_retention_hybrid"

def rmsnorm(x, g):
    xf = x.astype(jnp.float32)
    y = xf * lax.rsqrt(jnp.mean(xf * xf, axis=-1, keepdims=True) + EPS)
    return (y * g.astype(jnp.float32)).astype(x.dtype)

def depthwise_conv(x, w, b, pad_lo, pad_hi):
    c = x.shape[-1]
    y = lax.conv_general_dilated(
        x, w[:, None, :].astype(x.dtype), window_strides=(1,),
        padding=[(pad_lo, pad_hi)], dimension_numbers=('NWC', 'WIO', 'NWC'),
        feature_group_count=c)
    return y + b.astype(x.dtype)

def hyena_filters(L, w1, b1, w2, b2, w3, b3, freq, wout):
    f32 = jnp.float32
    t = jnp.arange(L, dtype=f32)
    t_norm = t / max(L - 1, 1)
    bands = jnp.linspace(1e-4, HY_BANDS - 1, HY_BANDS, dtype=f32)
    ang = (2.0 * math.pi / L) * t[:, None] * bands[None, :]
    z = jnp.concatenate([t_norm[:, None], jnp.cos(ang), jnp.sin(ang)], axis=-1)
    fr = freq.astype(f32)
    hdn = jnp.sin(fr * (z @ w1.astype(f32) + b1.astype(f32)))
    hdn = jnp.sin(fr * (hdn @ w2.astype(f32) + b2.astype(f32)))
    hdn = jnp.sin(fr * (hdn @ w3.astype(f32) + b3.astype(f32)))
    k = (hdn @ wout.astype(f32)).reshape(L, HY_ORDER, 2, HY_WIDTH)
    max_decay = math.log(HY_DECAY_TARGET) / HY_DECAY_PCT_SHORT
    min_decay = math.log(HY_DECAY_TARGET) / HY_DECAY_PCT_LONG
    deltas = jnp.abs(jnp.linspace(min_decay, max_decay, HY_WIDTH, dtype=f32))
    window = jnp.exp(-t_norm[:, None] * deltas[None, :])
    k = k * window[:, None, None, :]
    kk = jnp.concatenate([k[:, :, 0], jnp.zeros((1, HY_ORDER, HY_WIDTH), f32), k[:0:-1, :, 1]], axis=0)
    return jnp.fft.rfft(kk, axis=0)

def hyena_mixer(proj, conv_w, conv_b, kf, skip):
    L = proj.shape[1]
    uc = depthwise_conv(proj, conv_w, conv_b, HY_SHORT // 2, HY_SHORT // 2)
    x1 = uc[..., :HY_WIDTH]
    x2 = uc[..., HY_WIDTH:2 * HY_WIDTH]
    v = uc[..., 2 * HY_WIDTH:]
    z = v.astype(jnp.float32)
    skf = skip.astype(jnp.float32)
    for o, gate in enumerate((x1, x2)):
        zf = jnp.fft.rfft(z, n=2 * L, axis=1)
        conv = jnp.fft.irfft(zf * kf[None, :, o, :], n=2 * L, axis=1)[:, :L]
        z = gate.astype(jnp.float32) * (conv + z * skf[o])
    return z.astype(proj.dtype)

def linear_scan(a, b, reverse):
    def combine(left, right):
        a_l, b_l = left
        a_r, b_r = right
        return a_l * a_r, a_r * b_l + b_r
    _, h = lax.associative_scan(combine, (a, b), reverse=reverse, axis=1)
    return h

def rglru_mixer(xb, gb, conv_w, conv_b, gate_w, gate_b, lam):
    f32 = jnp.float32
    x = depthwise_conv(xb, conv_w, conv_b, LRU_CONV // 2, LRU_CONV - 1 - LRU_CONV // 2)
    B, T, _ = x.shape
    xblk = x.reshape(B, T, LRU_BLOCKS, LRU_BLOCK)
    gates = jnp.einsum('btnc,dgncm->dgbtnm', xblk, gate_w.astype(x.dtype)).reshape(2, 2, B, T, LRU_WIDTH)
    gates = jax.nn.sigmoid(gates.astype(f32) + gate_b.astype(f32)[:, :, None, None, :])
    r, i = gates[:, 0], gates[:, 1]
    log_a = -LRU_C * r * jax.nn.softplus(-lam.astype(f32))[:, None, None, :]
    a = jnp.exp(log_a)
    b = jnp.sqrt(-jnp.expm1(2.0 * log_a)) * i * x.astype(f32)[None]
    h_f = linear_scan(a[0], b[0], reverse=False)
    h_b = linear_scan(a[1], b[1], reverse=True)
    y = (h_f + h_b) * jax.nn.gelu(gb.astype(f32))
    return y.astype(xb.dtype)

def rotary(x, pos):
    half = x.shape[-1] // 2
    inv = ROPE_BASE ** (-jnp.linspace(0.0, 1.0, half, dtype=jnp.float32))
    ang = pos[:, None] * inv[None, :]
    cos = jnp.cos(ang)[None, :, None, :]
    sin = jnp.sin(ang)[None, :, None, :]
    x1, x2 = x[..., :half], x[..., half:]
    return jnp.concatenate([x1 * cos - x2 * sin, x1 * sin + x2 * cos], axis=-1)

def retention_chunks(q, k, v, log_gamma, strict):
    C = q.shape[2]
    idx = jnp.arange(C, dtype=jnp.float32)
    diff = idx[:, None] - idx[None, :]
    mask = (diff > 0) if strict else (diff >= 0)
    decay_in = jnp.where(mask[None], jnp.exp(jnp.where(mask, diff, 0.0)[None] * log_gamma[:, None, None]), 0.0)
    scores = jnp.einsum('bnchd,bnshd->bnhcs', q, k) * decay_in
    inner = jnp.einsum('bnhcs,bnshe->bnche', scores, v)
    zeta = jnp.exp((C - 1 - idx)[:, None] * log_gamma[None, :])
    kv = jnp.einsum('bnshd,sh,bnshe->nbhde', k, zeta, v)
    chunk_decay = jnp.exp(C * log_gamma)[None, :, None, None]

    def step(state, kv_n):
        return chunk_decay * state + kv_n, state

    _, prev = lax.scan(step, jnp.zeros_like(kv[0]), kv)
    xi = jnp.exp((idx + 1.0)[:, None] * log_gamma[None, :])
    cross = jnp.einsum('bnchd,ch,nbhde->bnche', q, xi, prev)
    return inner + cross

def retention_mixer(q, k, v, g):
    f32 = jnp.float32
    B, T, _ = q.shape
    pos = jnp.arange(T, dtype=f32)
    qh = rotary(q.astype(f32).reshape(B, T, RET_HEADS, RET_DK), pos)
    kh = rotary(k.astype(f32).reshape(B, T, RET_HEADS, RET_DK), pos) * (RET_DK ** -0.5)
    vh = v.astype(f32).reshape(B, T, RET_HEADS, RET_DV)
    pad = RET_CHUNK - N_META
    P = T + pad
    n_chunks = P // RET_CHUNK
    padf = lambda t: jnp.pad(t, ((0, 0), (pad, 0), (0, 0), (0, 0)))
    chunk = lambda t: t.reshape(B, n_chunks, RET_CHUNK, RET_HEADS, t.shape[-1])
    flip = lambda t: jnp.flip(t, axis=1)
    qp, kp, vp = padf(qh), padf(kh), padf(vh)
    log_gamma = jnp.log1p(-(2.0 ** (-5.0 - jnp.arange(RET_HEADS, dtype=f32))))
    y_f = retention_chunks(chunk(qp), chunk(kp), chunk(vp), log_gamma, strict=False)
    y_b = retention_chunks(chunk(flip(qp)), chunk(flip(kp)), chunk(flip(vp)), log_gamma, strict=True)
    y = y_f.reshape(B, P, RET_HEADS, RET_DV) + flip(y_b.reshape(B, P, RET_HEADS, RET_DV))
    y = y[:, pad:]
    mu = jnp.mean(y, axis=-1, keepdims=True)
    var = jnp.mean(jnp.square(y - mu), axis=-1, keepdims=True)
    yn = ((y - mu) * lax.rsqrt(var + EPS)).reshape(B, T, RET_WIDTH)
    return (jax.nn.silu(g.astype(f32)) * yn).astype(q.dtype)

def hybrid_layer(h, norm1_g, w_in, hy_conv_w, hy_conv_b, hy_kf, hy_skip,
                 lru_conv_w, lru_conv_b, lru_gate_w, lru_gate_b, lru_lambda,
                 w_branch, w_out, norm2_g, ffn_w_gu, ffn_w_down):
    B, T, _ = h.shape
    u = rmsnorm(h, norm1_g)
    p = jnp.einsum('btd,de->bte', u, w_in)
    y_hy = hyena_mixer(p[..., :OFF_LRU_X], hy_conv_w, hy_conv_b, hy_kf, hy_skip)
    y_lru = rglru_mixer(p[..., OFF_LRU_X:OFF_LRU_G], p[..., OFF_LRU_G:OFF_Q],
                        lru_conv_w, lru_conv_b, lru_gate_w, lru_gate_b, lru_lambda)
    y_ret = retention_mixer(p[..., OFF_Q:OFF_K], p[..., OFF_K:OFF_V],
                            p[..., OFF_V:OFF_G], p[..., OFF_G:OFF_MERGE])
    gates = jax.nn.sigmoid(p[..., OFF_MERGE:].astype(jnp.float32)).reshape(B, T, N_BRANCH, D_MODEL)
    merged = jnp.zeros((B, T, D_MODEL), jnp.float32)
    for bi, yb in enumerate((y_hy, y_lru, y_ret)):
        proj = jnp.einsum('btc,cd->btd', yb, w_branch[bi]).astype(jnp.float32)
        merged = merged + gates[:, :, bi] * proj
    h = h + jnp.einsum('btd,de->bte', merged.astype(h.dtype), w_out)
    v = rmsnorm(h, norm2_g)
    gu = jnp.einsum('btd,df->btf', v, ffn_w_gu)
    hid = jax.nn.silu(gu[..., :D_FF]) * gu[..., D_FF:]
    h = h + jnp.einsum('btf,fd->btd', hid, ffn_w_down)
    return h

def setup_inputs(seed: int = 0) -> dict:
    key = jax.random.key(seed)
    ks = jax.random.split(key, 32)
    f32 = jnp.float32
    H = HY_FILTER_HIDDEN

    def nrm(k, shape, scale):
        return jax.random.normal(k, shape, f32) * scale

    u = jax.random.uniform(ks[19], (DEPTH, 2, LRU_WIDTH), f32, LRU_A_MIN, LRU_A_MAX)
    s = u ** (1.0 / LRU_C)
    return {
        "x": nrm(ks[0], (BATCH, SEQ, D_MODEL), 1.0),
        "meta_tokens": nrm(ks[1], (N_META, D_MODEL), 1.0),
        "norm1_g": 1.0 + nrm(ks[2], (DEPTH, D_MODEL), 0.02),
        "w_in": nrm(ks[3], (DEPTH, D_MODEL, D_IN), D_MODEL ** -0.5),
        "hy_conv_w": nrm(ks[4], (DEPTH, HY_SHORT, (HY_ORDER + 1) * HY_WIDTH), HY_SHORT ** -0.5),
        "hy_conv_b": nrm(ks[5], (DEPTH, (HY_ORDER + 1) * HY_WIDTH), 0.02),
        "hy_f_w1": nrm(ks[6], (DEPTH, HY_EMB, H), HY_EMB ** -0.5),
        "hy_f_b1": nrm(ks[7], (DEPTH, H), 0.02),
        "hy_f_w2": nrm(ks[8], (DEPTH, H, H), H ** -0.5),
        "hy_f_b2": nrm(ks[9], (DEPTH, H), 0.02),
        "hy_f_w3": nrm(ks[10], (DEPTH, H, H), H ** -0.5),
        "hy_f_b3": nrm(ks[11], (DEPTH, H), 0.02),
        "hy_f_freq": 1.0 + nrm(ks[12], (DEPTH, H), 0.02),
        "hy_f_wout": nrm(ks[13], (DEPTH, H, HY_ORDER * 2 * HY_WIDTH), HY_FILTER_OUT_SCALE * H ** -0.5),
        "hy_skip": nrm(ks[14], (DEPTH, HY_ORDER, HY_WIDTH), 1.0),
        "lru_conv_w": nrm(ks[15], (DEPTH, LRU_CONV, LRU_WIDTH), LRU_CONV ** -0.5),
        "lru_conv_b": nrm(ks[16], (DEPTH, LRU_WIDTH), 0.02),
        "lru_gate_w": nrm(ks[17], (DEPTH, 2, 2, LRU_BLOCKS, LRU_BLOCK, LRU_BLOCK), LRU_BLOCK ** -0.5),
        "lru_gate_b": nrm(ks[18], (DEPTH, 2, 2, LRU_WIDTH), 0.02),
        "lru_lambda": jnp.log(s) - jnp.log1p(-s),
        "w_branch": nrm(ks[20], (DEPTH, N_BRANCH, BRANCH_WIDTH, D_MODEL), BRANCH_WIDTH ** -0.5),
        "w_out": nrm(ks[21], (DEPTH, D_MODEL, D_MODEL), D_MODEL ** -0.5),
        "norm2_g": 1.0 + nrm(ks[22], (DEPTH, D_MODEL), 0.02),
        "ffn_w_gu": nrm(ks[23], (DEPTH, D_MODEL, 2 * D_FF), D_MODEL ** -0.5),
        "ffn_w_down": nrm(ks[24], (DEPTH, D_FF, D_MODEL), D_FF ** -0.5),
        "final_g": 1.0 + nrm(ks[25], (D_MODEL,), 0.02),
    }

def reference(x, meta_tokens, norm1_g, w_in, hy_conv_w, hy_conv_b, hy_f_w1, hy_f_b1,
              hy_f_w2, hy_f_b2, hy_f_w3, hy_f_b3, hy_f_freq, hy_f_wout, hy_skip,
              lru_conv_w, lru_conv_b, lru_gate_w, lru_gate_b, lru_lambda,
              w_branch, w_out, norm2_g, ffn_w_gu, ffn_w_down, final_g):
    B = x.shape[0]
    meta = jnp.broadcast_to(meta_tokens[None].astype(x.dtype), (B, N_META, D_MODEL))
    h = jnp.concatenate([meta, x], axis=1)
    T = h.shape[1]
    for l in range(DEPTH):
        hy_kf = hyena_filters(T, hy_f_w1[l], hy_f_b1[l], hy_f_w2[l], hy_f_b2[l],
                              hy_f_w3[l], hy_f_b3[l], hy_f_freq[l], hy_f_wout[l])
        h = hybrid_layer(h, norm1_g[l], w_in[l], hy_conv_w[l], hy_conv_b[l], hy_kf, hy_skip[l],
                         lru_conv_w[l], lru_conv_b[l], lru_gate_w[l], lru_gate_b[l], lru_lambda[l],
                         w_branch[l], w_out[l], norm2_g[l], ffn_w_gu[l], ffn_w_down[l])
    out = rmsnorm(h, final_g)
    return out[:, N_META:]


_drawn_inputs = setup_inputs


def setup_inputs(seed=0):
    import zlib

    import numpy as np

    out = dict(_drawn_inputs(seed))
    spreads = {}
    factors = {'hy_f_b1': 8.0,
     'hy_f_b2': 8.0,
     'hy_f_b3': 8.0,
     'hy_f_freq': 8.0,
     'lru_gate_b': 8.0,
     'norm2_g': 2.911,
     'final_g': 2.81}
    for name, (base, spread) in spreads.items():
        noise = np.random.default_rng([zlib.crc32(name.encode()), seed]).standard_normal(out[name].shape)
        drawn = base * np.exp(spread * noise) if base else spread * noise
        out[name] = jnp.asarray(drawn.astype(out[name].dtype))
    for name, factor in factors.items():
        out[name] = (out[name] * factor).astype(out[name].dtype)
    return out
```

```python
from contextlib import ExitStack

import numpy as np
import concourse.bass as bass
from concourse import mybir

P = 128
DEPTH = 2
D_MODEL = 1024
SEQ = 256
N_META = 16
T = SEQ + N_META
EPS = 1e-6
KC = D_MODEL // P
HEADS = 4
D_FF = 2816
FT = D_FF // P
HID = 64
EMB = 33
BANDS = 16
CHUNKS = [(0, 96), (96, 96), (192, 80)]
CM = 96
NF = 512
HALF = 4
RAW = 3
SPL = 3
BANKS = 8
SG = 6

F32 = mybir.dt.float32
F32R = mybir.dt.float32r
ALU = mybir.AluOpType
ACT = mybir.ActivationFunctionType

C_N1, C_N2 = 0, 8
C_HW, C_HB = 16, 88
C_SKIP = 112
C_LW, C_LB = 128, 160
C_GB = 168
C_LAM = 200
N_PAR = 216
C_W1, C_W2, C_W3 = 0, 64, 128
C_B1, C_B2, C_B3, C_FR, C_SGN = 256, 257, 258, 259, 260
N_FIL = 261


def schedule():
    s = [("mlp",), ("F", 0, 0), ("norm", 0)]
    hy = lambda a, b: [("hy", i) for i in range(a, b)]
    s += hy(16, 20) + [("T", 0, 0)] + hy(20, 24) + [("W", 0, 0)] + hy(0, 4) + [("I", 0, 0), ("F", 0, 1), ("T", 0, 1)]
    s += hy(4, 8) + [("W", 0, 1)] + hy(8, 12) + [("I", 0, 1), ("F", 1, 0), ("T", 1, 0)] + hy(12, 16)
    s += [("W", 1, 0)] + [("lx", j) for j in range(4)] + [("I", 1, 0), ("F", 1, 1), ("T", 1, 1)]
    s += [("lx", j) for j in range(4, 8)] + [("W", 1, 1)] + [("lg", j) for j in range(8)] + [("I", 1, 1)]
    s += [("G", 0), ("LR", 0)]
    for j in range(4):
        s += [("mg", 0, j), ("mp", 0, j)]
    s += [("G", 1), ("LR", 1)]
    for j in range(4, 8):
        s += [("mg", 0, j), ("mp", 0, j)]
    s += [("mg", 1, j) for j in range(5)]
    for j in range(8):
        s += [("mp", 1, j)]
        if j + 5 < 8:
            s += [("mg", 1, j + 5)]
    s += [("rv", 0), ("rq", 0), ("rk", 0), ("rg", 0)]
    for h in range(HEADS):
        last = h == HEADS - 1
        s += [("RT", h), ("RS", h)]
        s += [("mg", 2, 0), ("mg", 2, 1)] if last else [("rv", h + 1)]
        s += [("RP", h)]
        s += [("mg", 2, 2), ("mg", 2, 3)] if last else [("rq", h + 1)]
        s += [("RM", h)]
        s += [("mg", 2, 4)] if last else [("rk", h + 1)]
        s += [("RV", h)]
        s += [("mg", 2, 5)] if last else [("rg", h + 1)]
    s += [("mp", 2, 0), ("mp", 2, 1), ("mg", 2, 6), ("mg", 2, 7)] + [("mp", 2, j) for j in range(2, 8)]
    s += [("ms",)] + [("wo", j) for j in range(KC)] + [("norm", 1)]
    for i in range(FT):
        s += [("fg", i), ("fu", i)]
    s += [("dn", j) for j in range(KC)]
    return s


def item_slabs(it):
    k = it[0]
    if k == "hy":
        return [("in", it[1])]
    if k == "lx":
        return [("in", 24 + it[1])]
    if k == "lg":
        return [("in", 32 + it[1])]
    if k in ("rq", "rk", "rv", "rg"):
        first = {"rq": 40, "rk": 48, "rv": 56, "rg": 64}[k] + 2 * it[1]
        return [("in", first), ("in", first + 1)]
    if k == "mg":
        return [("in", 72 + 8 * it[1] + it[2])]
    if k == "mp":
        return [("branch", 8 * it[1] + it[2])]
    if k == "G":
        return [("gate", 2 * it[1]), ("gate", 2 * it[1] + 1)]
    if k == "wo":
        return [("out", it[1])]
    if k == "fg":
        return [("gu", it[1])]
    if k == "fu":
        return [("gu", FT + it[1])]
    return []


def item_jobs(it):
    k = it[0]
    if k == "mlp":
        return [(("mlp", i), 1) for i in range(3)]
    if k == "F":
        return [(("sd", *it[1:], c, x), 1) for c in range(3) for x in range(2)] + \
               [(("K", *it[1:], c, x), 1) for c in range(3) for x in range(2)]
    if k == "T":
        return [(("T", *it[1:], c), 1) for c in range(3)]
    if k == "W":
        return [(("W", *it[1:], c, x), 1) for c in range(3) for x in range(2)]
    if k == "I":
        return [(("I", *it[1:], i), 1) for i in range(HALF)]
    if k == "G":
        return [(("G", 4 * it[1] + n, d, g), 1) for n in range(HALF) for d in range(2) for g in range(2)]
    if k in ("rq", "rk", "rv", "rg", "RP"):
        return [(it, 2)]
    if k in ("RT", "RS"):
        return [((k, it[1], c), 1) for c in range(3)]
    if k in ("LR", "ms"):
        return []
    return [(it, 1)]


class Plan:

    def __init__(self):
        self.items = schedule()
        self.slabs, self.first_slab = [], {}
        self.bank, self.nth = {}, {}
        self.jobs = []
        self.before = {}
        self.order = {}
        used, owner, at = [0] * BANKS, [None] * BANKS, 0
        slab_job = []
        for it in self.items:
            self.first_slab[it] = len(self.slabs)
            self.order.setdefault(it[0], []).append(it)
            mine = item_slabs(it)
            self.slabs += mine
            for job, n in item_jobs(it):
                if at + n > BANKS:
                    at = 0
                self.bank[job] = at
                self.before[job] = [owner[b] for b in range(at, at + n) if owner[b] is not None]
                for b in range(at, at + n):
                    owner[b] = job
                used[at + n - 1] += 1
                self.nth[job] = (at + n - 1, used[at + n - 1])
                self.jobs.append(job)
                if job[0] != it[0] or job != it:
                    self.order.setdefault(("job", job[0]), []).append(job)
                at = (at + n) % BANKS
            if it[0] == "G":
                g = [j for j, _ in item_jobs(it)]
                slab_job += [g[7], g[15]]
            elif mine:
                slab_job += [item_jobs(it)[0][0]] * len(mine)
        self.first_down = len(self.slabs)
        self.slabs += [("down", n) for n in range(FT)]
        self.slab_job = slab_job

    def place(self, it):
        return self.order[it[0]].index(it) + 1

    def jplace(self, job):
        return self.order[("job", job[0])].index(job) + 1


PLAN = Plan()
N_SLAB = len(PLAN.slabs)
U = KC * T * 4


def build(nc, h0, slabs, params, filt, wout, fin_g, cfwd, cinv, rope, decay, window, zfeat, ident_in, out):
    plan = PLAN
    sems = []

    with ExitStack() as ctx:
        def sem(name):
            s = ctx.enter_context(nc.semaphore(name))
            sems.append(s)
            return s

        top = [(nc.sbuf_base + 31) // 32 * 32]

        def at(name, shape, offset, dt=F32):
            size = 4 * int(np.prod(shape[1:]))
            assert offset + size <= nc.sbuf_usable_end, (name, offset, size)
            return nc.alloc_sbuf_tensor_at(name, shape, dt, offset=offset)

        def sb(name, shape, dt=F32):
            t = at(name, shape, top[0], dt)
            top[0] += (4 * int(np.prod(shape[1:])) + 31) // 32 * 32
            return t

        h = sb("h", [P, KC, T])
        uh = sb("uh", [P, KC, T], F32R)
        ul = sb("ul", [P, KC, T], F32R)
        raw = sb("raw", [P, RAW, KC * P])
        wh = sb("wh", [P, SPL, KC * P], F32R)
        wl = sb("wl", [P, SPL, KC * P], F32R)
        fwd_h = sb("fwd_h", [CM, 3, 2, T], F32R)
        fwd_l = sb("fwd_l", [CM, 3, 2, T], F32R)
        inv_h = sb("inv_h", [CM, 3, 2, T], F32R)
        inv_l = sb("inv_l", [CM, 3, 2, T], F32R)
        cs = sb("cs", [P, 2, T])
        ones = sb("ones", [P, P])
        ident = sb("ident", [P, P])
        zf = sb("zf", [EMB, T])
        par = sb("par", [P, N_PAR])
        fil = sb("fil", [P, N_FIL])
        c8 = sb("c8", [P, 2, 2 * KC])
        lsp = sb("lsp", [P, 5, 2 * KC])
        hdn_s = sb("hdn_s", [P, T])
        hdn_d = sb("hdn_d", [P, T])
        rstd = sb("rstd", [P, T])
        ms = sb("ms", [P, T])
        finp = sb("finp", [P, KC])
        U0 = top[0]
        utmp = at("utmp", [P, KC, T], U0)
        tmp_b = at("tmp_b", [CM, 4, NF], U0)
        A0 = U0 + U

        oA, oB, oC, oD, oG, oX, oL, oE = (A0 + x for x in (0, U, 2 * U, 3 * U, 3 * U + 12288, 3 * U + 24576,
                                                           4 * U + 24576, 5 * U + 24576))
        oT = oE + 24576
        x1 = at("x1", [P, KC, T], oA)
        x2 = at("x2", [P, KC, T], oB)
        z = at("z", [P, KC, T], oC)
        zt_h = at("zt_h", [CM, 3, NF], oD, F32R)
        zt_l = at("zt_l", [CM, 3, NF], oD + 6144, F32R)
        kf = at("kf", [CM, 3, 2, NF], oG)
        sp_h = at("sp_h", [CM, 3, 2, NF], oE, F32R)
        sp_l = at("sp_l", [CM, 3, 2, NF], oE + 12288, F32R)
        tmp_a = at("tmp_a", [CM, 4, NF], oT)
        win = at("win", [CM, 3, NF], oL)
        wo_t = at("wo_t", [P, NF], oL + 6144)
        marg = at("marg", [P, 3, T], oT)
        mact = at("mact", [P, 2, T], oT + 3264)
        bh = at("bh", [P, KC, T], oA, F32R)
        bl = at("bl", [P, KC, T], oB, F32R)
        xc = at("xc", [P, KC, T], oX)
        gl = at("gl", [P, KC, T], oL)
        lh = at("lh", [P, KC, T], oE, F32R)
        ll = at("ll", [P, KC, T], oE + U, F32R)
        lth = at("lth", [P, 2, HALF, T], oC)
        lr = at("lr", [P, 2, HALF, T], oD)
        li = at("li", [P, 2, HALF, T], oG)
        la2 = at("la2", [P, 2, HALF, T], U0)
        merged = at("merged", [P, KC, T], oT)
        sg = at("sg", [P, SG, T], oE + 2 * U)
        dec = at("dec", [CM, 3, HEADS, T], oC)
        o = oC + 3 * HEADS * T * 4
        qk_h = at("qk_h", [P, 2, 2, T], o, F32R)
        qk_l = at("qk_l", [P, 2, 2, T], o + 4352, F32R)
        rv = at("rv", [P, 2, T], o + 8704)
        vt_h = at("vt_h", [CM, 3, 256], o + 10880, F32R)
        vt_l = at("vt_l", [CM, 3, 256], o + 13952, F32R)
        ra = at("ra", [P, 2, T], o + 17024)
        rb = at("rb", [P, 2, T], o + 19200)
        sc = at("sc", [CM, 2, T], o + 21376)
        sc_h = at("sc_h", [CM, 3, T], o + 23552, F32R)
        sc_l = at("sc_l", [CM, 3, T], o + 26816, F32R)
        ry = at("ry", [P, 2, T], o + 30080)
        rsq = at("rsq", [P, 2, T], o + 32256)
        gs = at("gs", [P, 2, T], o + 34432)
        hh = at("hh", [P, FT, T], oA, F32R)
        hl = at("hl", [P, FT, T], oA + FT * T * 4, F32R)
        craw = at("craw", [CM, 2, 3, 2, T], oA)

        ps = ctx.enter_context(nc.psum_tensor("ps", [P, BANKS, 512], F32))

        full = [sem(f"bank_full{b}") for b in range(BANKS)]
        raw_in = [sem(f"raw_in{r}") for r in range(RAW)]
        slab_hi, slab_lo, down_slab = sem("slab_hi"), sem("slab_lo"), sem("down_slab")
        par_in, win_in, dec_in = sem("par_in"), sem("win_in"), sem("dec_in")
        dve_step, act_step = sem("dve_step"), sem("act_step")
        N = {}
        for name in ("mlp_read mlp_arg mlp_sin hdn sd_win sd_hi sd_lo kf_done zt_hi zt_lo z_prod pq pq_hi pq_lo "
                     "inv_read z_done b_hi b_lo sq_done ms_read ms_rec rstd_done u_f32 u_hi u_lo hy_tap hy_done "
                     "lx_tap lx_done lg_done lx_hi lx_lo gate_done lru_ab lru_th lru_sq lru_y l_hi l_lo "
                     "mg_done mp_done rv_done rope_ab rope_f rope_hi rope_lo rg_done vt_hi vt_lo sc_read sc_hi "
                     "sc_lo y_done mean_done rsq_done var_rec rstd_r yb_done m_hi m_lo wo_done fg_done hid_f32 "
                     "hid_hi hid_lo dn_done lam_exp c8_done").split():
            N[name] = sem(name)

        def wait(eng, name, n):
            eng.wait_ge(N[name], n)

        def inc(ins, name):
            ins.then_inc(N[name], 1)

        def wait_full(eng, job):
            b, n = plan.nth[job]
            eng.wait_ge(full[b], n)

        def freed(job):
            k = job[0]
            jp = plan.jplace if ("job", k) in plan.order else None
            if k == "mlp":
                return "mlp_read", job[1] + 1
            if k == "norm":
                return "ms_read", job[1] + 1
            if k in ("sd", "K", "T", "I", "G", "RT", "RS"):
                return {"sd": "sd_win", "K": "kf_done", "T": "zt_lo", "I": "inv_read", "G": "gate_done",
                        "RT": "vt_lo", "RS": "sc_read"}[k], jp(job)
            if k == "W":
                return "z_prod", (jp(job) + 1) // 2
            if k in ("rq", "rk"):
                return "rope_ab", rope_place(job)
            return {"hy": "hy_done", "lx": "lx_done", "lg": "lg_done", "mg": "mg_done", "mp": "mp_done",
                    "rv": "rv_done", "rg": "rg_done", "RP": "y_done", "RM": "mean_done", "RV": "var_rec",
                    "wo": "wo_done", "fg": "fg_done", "fu": "hid_f32", "dn": "dn_done"}[k], plan.place(job)

        def rope_place(it):
            return [i for i in plan.items if i[0] in ("rq", "rk")].index(it) + 1

        def wait_slab_used(eng, n):
            if n < 0:
                return
            if n < plan.first_down:
                wait_full(eng, plan.slab_job[n])
            else:
                m = n - plan.first_down + 1
                if (8 * m) % FT == 0:
                    wait_full(eng, ("dn", 8 * m // FT - 1))
                else:
                    eng.wait_ge(down_slab, m - m // 11)

        def hy_dst(j):
            return (x1, x2, z)[j // KC][:, j % KC]

        def bank(job, m=P, n=T):
            return ps[0:m, plan.bank[job], 0:n]

        def pair(job):
            b = plan.bank[job]
            return ps[:, b:b + 2, 0:T]

        c_in, c_hi, c_one = sem("c_in"), sem("c_hi"), sem("c_one")
        with nc.Block() as block:
            @block.sync
            def _(sp):
                sp.dma_start(craw[:, 0], cfwd).then_inc(c_in, 16)
                sp.dma_start(craw[:, 1], cinv).then_inc(c_in, 16)
                sp.dma_start(h[:], h0).then_inc(c_in, 16)
                sp.dma_start(cs[:], rope).then_inc(c_in, 16)
                sp.dma_start(ident[:], ident_in).then_inc(c_in, 16)
                sp.dma_start(zf[:], zfeat).then_inc(c_in, 16)
                sp.dma_start(finp[:], fin_g).then_inc(c_in, 16)

            @block.scalar
            def _(act):
                act.wait_ge(c_in, 7 * 16)
                nc.scalar.activation(fwd_h[:], craw[:, 0], ACT.Copy).then_inc(c_hi, 1)
                nc.scalar.activation(inv_h[:], craw[:, 1], ACT.Copy).then_inc(c_hi, 1)

            @block.vector
            def _(dve):
                nc.vector.memset(ones[:], 1.0).then_inc(c_one, 1)
                dve.wait_ge(c_hi, 1)
                nc.vector.tensor_tensor(fwd_l[:], craw[:, 0], fwd_h[:].bitcast(F32), ALU.subtract).then_inc(c_one, 1)
                dve.wait_ge(c_hi, 2)
                nc.vector.tensor_tensor(inv_l[:], craw[:, 1], inv_h[:].bitcast(F32), ALU.subtract).then_inc(c_one, 1)
                dve.wait_ge(c_one, 3)

        def layer_body(layer, block):
            @block.sync
            def _(sp):
                sp.dma_start(par[:], params[bass.ds(layer, 1)].rearrange("a p n -> p (a n)")).then_inc(par_in, 16)
                sp.dma_start(fil[:], filt[bass.ds(layer, 1)].rearrange("a p n -> p (a n)")).then_inc(par_in, 16)
                for n in range(N_SLAB):
                    if n >= RAW:
                        sp.wait_ge(slab_lo, n - RAW + 1)
                    sp.dma_start(raw[:, n % RAW], slabs[bass.ds(layer * N_SLAB + n, 1)].rearrange("a p n -> p (a n)")) \
                      .then_inc(raw_in[n % RAW], 16)

            @block.gpsimd
            def _(pool):
                n = 0
                for it in plan.items:
                    if it[0] == "W":
                        for c, (_, cn) in enumerate(CHUNKS):
                            n += 1
                            t = (tmp_a, tmp_b)[c % 2]
                            wait(pool, "z_prod", n)
                            inc(nc.gpsimd.tensor_tensor(t[0:cn, 0], t[0:cn, 0], t[0:cn, 1], ALU.subtract), "pq")
                            inc(nc.gpsimd.tensor_tensor(t[0:cn, 2], t[0:cn, 2], t[0:cn, 3], ALU.add), "pq")
                    if it[0] in ("rq", "rk"):
                        wait(pool, "rope_ab", rope_place(it))
                        inc(nc.gpsimd.tensor_tensor(ra[:, 0], ra[:, 0], rb[:, 1], ALU.subtract), "rope_f")
                        inc(nc.gpsimd.tensor_tensor(ra[:, 1], ra[:, 1], rb[:, 0], ALU.add), "rope_f")

            @block.scalar
            def _(act):
                steps = [0]
                splits = [0]

                def link(ins):
                    steps[0] += 1
                    ins.then_inc(act_step, 1)
                    act.wait_ge(act_step, steps[0])

                def split_to(n):
                    while splits[0] < min(n, N_SLAB):
                        m = splits[0]
                        act.wait_ge(raw_in[m % RAW], 16 * (m // RAW + 1))
                        wait_slab_used(act, m - SPL)
                        nc.scalar.activation(wh[:, m % SPL], raw[:, m % RAW], ACT.Copy).then_inc(slab_hi, 1)
                        splits[0] += 1

                def rnd(name, dst, src):
                    inc(nc.scalar.activation(dst, src, ACT.Copy), name)

                def load_filter(k):
                    o, f = k // 2, k % 2
                    if k:
                        wait(act, "sd_win", 6 * k)
                        wait_full(act, ("sd", (k - 1) // 2, (k - 1) % 2, 2, 1))
                    act.dma_start(win[:], window[:, :, f * NF:(f + 1) * NF]).then_inc(win_in, 16)
                    act.dma_start(wo_t[:], wout[bass.ds(layer * 4 + k, 1)].rearrange("a p n -> p (a n)")) \
                        .then_inc(win_in, 16)

                load_filter(0)
                act.wait_ge(par_in, 32)
                lam = par[:, C_LAM:C_LAM + 2 * KC]
                link(nc.scalar.activation(lsp[:, 0], lam, ACT.Abs))
                inc(nc.scalar.activation(lsp[:, 1], lsp[:, 0], ACT.Exp, scale=-1.0), "lam_exp")
                wait(act, "lam_exp", 1)
                split_to(SPL)
                c = {}

                def nth(name):
                    c[name] = c.get(name, 0) + 1
                    return c[name]

                for it in plan.items:
                    k = it[0]
                    split_to(plan.first_slab[it] + SPL)
                    if k == "mlp":
                        for i in range(3):
                            wait(act, "mlp_arg", i + 1)
                            d = (mact[0:HID, 0], mact[0:HID, 1], hdn_s[:])[i]
                            s = marg[0:HID, 0] if i < 2 else marg[:, 0]
                            inc(nc.scalar.activation(d, s, ACT.Sin), "mlp_sin")
                    if k == "F":
                        for n in range(6):
                            cc, x = n // 2, n % 2
                            cn = CHUNKS[cc][1]
                            m = nth("sd")
                            wait(act, "sd_win", m)
                            rnd("sd_hi", sp_h[0:cn, cc, x], tmp_a[0:cn, n % 4])
                        for n in range(6):
                            cc, x = n // 2, n % 2
                            cn = CHUNKS[cc][1]
                            job = ("K", it[1], it[2], cc, x)
                            wait_full(act, job)
                            if n == 0 and c.get("W"):
                                wait(act, "z_prod", 3 * c["W"])
                            inc(nc.scalar.copy(kf[0:cn, cc, x], bank(job, cn, NF)), "kf_done")
                    if k == "F" and it[1:] != (1, 1):
                        load_filter(2 * it[1] + it[2] + 1)
                    if it == ("mp", 1, 0):
                        wait(act, "l_lo", 2)
                        act.dma_start(dec[:], decay).then_inc(dec_in, 16)
                    if k == "T":
                        for cc, (_, cn) in enumerate(CHUNKS):
                            job = (*it, cc)
                            wait_full(act, job)
                            rnd("zt_hi", zt_h[0:cn, cc], bank(job, cn, NF))
                    if k == "W":
                        nth("W")
                        for cc, (_, cn) in enumerate(CHUNKS):
                            t = (tmp_a, tmp_b)[cc % 2]
                            for x in range(2):
                                wait(act, "pq", nth("pq"))
                                rnd("pq_hi", sp_h[0:cn, cc, x], t[0:cn, 2 * x])
                    if k == "I" and it[1] == 1:
                        for i in range(HALF):
                            j = HALF * it[2] + i
                            wait(act, "z_done", 8 + j + 1)
                            rnd("b_hi", bh[:, j], z[:, j])
                    if k == "norm":
                        if it[1] == 1:
                            wait(act, "wo_done", KC)
                        for j in range(KC):
                            inc(nc.scalar.activation(utmp[:, j], h[:, j], ACT.Square), "sq_done")
                        wait(act, "ms_rec", it[1] + 1)
                        inc(nc.scalar.activation(rstd[:], ms[:], ACT.Sqrt), "rstd_done")
                        for j in range(KC):
                            wait(act, "u_f32", nth("u"))
                            rnd("u_hi", uh[:, j], utmp[:, j])
                    if k == "hy":
                        j = it[1]
                        wait_full(act, it)
                        inc(nc.scalar.activation(hy_dst(j), bank(it), ACT.Identity,
                                                 bias=par[:, C_HB + j:C_HB + j + 1],
                                                 scale=par[:, C_HW + 24 + j:C_HW + 25 + j]), "hy_tap")
                    if k == "lx":
                        j = it[1]
                        wait_full(act, it)
                        inc(nc.scalar.activation(xc[:, j], bank(it), ACT.Identity,
                                                 bias=par[:, C_LB + j:C_LB + j + 1],
                                                 scale=par[:, C_LW + 16 + j:C_LW + 17 + j]), "lx_tap")
                    if k == "lg":
                        wait_full(act, it)
                        if it[1] == 0:
                            wait(act, "sd_win", 24)
                            wait_full(act, ("sd", 1, 1, 2, 1))
                        inc(nc.scalar.activation(gl[:, it[1]], bank(it), ACT.Gelu_apprx_tanh), "lg_done")
                    if k == "G":
                        f = it[1]
                        if f == 0:
                            wait(act, "lx_done", KC)
                            wait_full(act, ("I", 1, 1, HALF - 1))
                            wait(act, "b_lo", KC)
                        rnd("lx_hi", lh[:, 4 * f:4 * f + 4], xc[:, 4 * f:4 * f + 4])
                        if f == 1:
                            wait(act, "l_lo", 1)
                        for n in range(HALF):
                            for d in range(2):
                                for g in range(2):
                                    job = ("G", 4 * f + n, d, g)
                                    col = C_GB + (2 * d + g) * KC + 4 * f + n
                                    wait_full(act, job)
                                    inc(nc.scalar.activation((lr, li)[g][:, d, n], bank(job), ACT.Sigmoid,
                                                             bias=par[:, col:col + 1]), "gate_done")
                                if n % 2 == 1 and d == 1:
                                    split_to(plan.first_slab[it] + n // 2 + 1 + SPL)
                    if k == "LR":
                        f = it[1]
                        wait(act, "gate_done", 16 * (f + 1))
                        wait(act, "c8_done", 2)
                        for d in range(2):
                            for n in range(HALF):
                                col = d * KC + HALF * f + n
                                nc.scalar.activation(lth[:, d, n], lr[:, d, n], ACT.Tanh,
                                                     scale=c8[:, 0, col:col + 1]).then_inc(act_step, 1)
                                steps[0] += 1
                        act.wait_ge(act_step, steps[0])
                        for d in range(2):
                            for n in range(HALF):
                                col = d * KC + HALF * f + n
                                inc(nc.scalar.activation(lr[:, d, n], lr[:, d, n], ACT.Exp,
                                                         scale=c8[:, 1, col:col + 1]), "lru_ab")
                        wait(act, "lru_th", f + 1)
                        inc(nc.scalar.activation(lth[:], lth[:], ACT.Sqrt), "lru_sq")
                        wait(act, "lru_y", f + 1)
                        rnd("l_hi", lh[:, 4 * f:4 * f + 4], lth[:, 0])
                    if k == "mg":
                        s = (plan.place(it) - 1) % SG
                        wait_full(act, it)
                        if plan.place(it) == 1:
                            wait_full(act, ("I", 1, 1, HALF - 1))
                        if plan.place(it) > SG:
                            wait(act, "mp_done", plan.place(it) - SG)
                        inc(nc.scalar.activation(sg[:, s], bank(it), ACT.Sigmoid), "mg_done")
                    if k == "rv":
                        wait_full(act, it)
                        if it[1] == 0:
                            wait(act, "l_lo", 2)
                        inc(nc.scalar.copy(rv[:], pair(it)), "rv_done")
                    if k in ("rq", "rk"):
                        r = rope_place(it)
                        x = 0 if k == "rq" else 1
                        wait(act, "rope_f", 2 * r)
                        if it[1]:
                            wait_full(act, ("RS", it[1] - 1, 2))
                        rnd("rope_hi", qk_h[:, x], ra[:])
                    if k == "rg":
                        wait_full(act, it)
                        if it[1]:
                            wait(act, "yb_done", it[1])
                        inc(nc.scalar.activation(gs[:], pair(it), ACT.Silu), "rg_done")
                    if k == "RT":
                        for cc, (_, cn) in enumerate(CHUNKS):
                            wait_full(act, (*it, cc))
                            rnd("vt_hi", vt_h[0:cn, cc], bank((*it, cc), cn, 256))
                    if k == "RS":
                        for cc, (_, cn) in enumerate(CHUNKS):
                            wait(act, "sc_read", nth("sc"))
                            rnd("sc_hi", sc_h[0:cn, cc], sc[0:cn, c["sc"] % 2])
                    if k == "RP":
                        wait_full(act, it)
                        if it[1]:
                            wait(act, "b_lo", KC + it[1])
                        inc(nc.scalar.copy(ry[:], pair(it)), "y_done")
                    if k == "RM":
                        wait(act, "mean_done", it[1] + 1)
                        inc(nc.scalar.activation(rsq[:], ry[:], ACT.Square), "rsq_done")
                    if k == "RV":
                        wait(act, "var_rec", it[1] + 1)
                        inc(nc.scalar.activation(rstd[:], ms[:], ACT.Sqrt), "rstd_r")
                        wait(act, "yb_done", it[1] + 1)
                        rnd("b_hi", bh[:, 2 * it[1]:2 * it[1] + 2], ry[:])
                    if k == "ms":
                        for f in range(4):
                            wait(act, "mp_done", 16 + 2 * f + 2)
                            if f == 0:
                                wait_full(act, ("mp", 1, 7))
                            rnd("m_hi", lh[:, 2 * f:2 * f + 2], merged[:, 2 * f:2 * f + 2])
                    if k == "fg":
                        i = it[1]
                        wait_full(act, it)
                        if i >= SG:
                            wait(act, "hid_lo", i - SG + 1)
                        inc(nc.scalar.activation(sg[:, i % SG], bank(it), ACT.Silu), "fg_done")
                    if k == "fu":
                        i = it[1]
                        wait(act, "hid_f32", i + 1)
                        rnd("hid_hi", hh[:, i], sg[:, i % SG])
                    if k == "dn":
                        for m in range(it[1] * FT // KC, (it[1] + 1) * FT // KC):
                            split_to(plan.first_down + m + SPL)

            @block.vector
            def _(dve):
                steps = [0]
                splits = [0]

                def link(ins):
                    steps[0] += 1
                    ins.then_inc(dve_step, 1)
                    dve.wait_ge(dve_step, steps[0])

                def split_to(n):
                    while splits[0] < min(n, N_SLAB):
                        m = splits[0]
                        dve.wait_ge(slab_hi, m + 1)
                        nc.vector.tensor_tensor(wl[:, m % SPL], raw[:, m % RAW], wh[:, m % SPL].bitcast(F32),
                                                ALU.subtract).then_inc(slab_lo, 1)
                        splits[0] += 1

                def rest(name, dst, src, hi):
                    inc(nc.vector.tensor_tensor(dst, src, hi.bitcast(F32), ALU.subtract), name)

                c = {}

                def nth(name):
                    c[name] = c.get(name, 0) + 1
                    return c[name]

                wait(dve, "lam_exp", 1)
                e, s, s2, r = lsp[:, 1], lsp[:, 2], lsp[:, 3], lsp[:, 4]
                link(nc.vector.tensor_scalar(s2, e, 2.0, None, ALU.add))
                link(nc.vector.reciprocal(s, s2))
                link(nc.vector.tensor_tensor(s, e, s, ALU.mult))
                link(nc.vector.tensor_tensor(s2, s, s, ALU.mult))
                link(nc.vector.tensor_scalar(r, s2, 1.0 / 15, None, ALU.mult))
                for q in (13, 11, 9, 7, 5, 3):
                    link(nc.vector.scalar_tensor_tensor(out=r, in0=r, scalar=1.0 / q, in1=s2, op0=ALU.add, op1=ALU.mult))
                link(nc.vector.scalar_tensor_tensor(out=r, in0=r, scalar=1.0, in1=s, op0=ALU.add, op1=ALU.mult))
                link(nc.vector.tensor_scalar(s, par[:, C_LAM:C_LAM + 2 * KC], -1.0, 0.0, ALU.mult, ALU.max))
                link(nc.vector.scalar_tensor_tensor(out=s, in0=r, scalar=2.0, in1=s, op0=ALU.mult, op1=ALU.add))
                inc(nc.vector.tensor_scalar(c8[:, 0], s, 8.0, None, ALU.mult), "c8_done")
                inc(nc.vector.tensor_scalar(c8[:, 1], s, -8.0, None, ALU.mult), "c8_done")
                split_to(SPL)

                TWO_PI = 2 * np.pi
                PI_A = 6.28125
                PI_B = float(np.float32(TWO_PI - PI_A))
                PI_C = float(TWO_PI - PI_A - PI_B)
                PI_LE = 3.1415925
                MAGIC = 1.5 * 2.0 ** 23
                for it in plan.items:
                    k = it[0]
                    split_to(plan.first_slab[it] + SPL)
                    if k == "mlp":
                        for i in range(3):
                            m = HID if i < 2 else P
                            a, b, t = marg[0:m, 0], marg[0:m, 1], marg[0:m, 2]
                            col = (C_B1, C_B2, C_B3)[i]
                            wait_full(dve, ("mlp", i))
                            inc(nc.vector.tensor_scalar(t, bank(("mlp", i), m), fil[0:m, col:col + 1],
                                                        fil[0:m, C_FR:C_FR + 1], ALU.add, ALU.mult), "mlp_read")
                            wait(dve, "mlp_read", i + 1)
                            link(nc.vector.tensor_scalar(b, t, 1 / TWO_PI, MAGIC, ALU.mult, ALU.add))
                            link(nc.vector.tensor_scalar(b, b, MAGIC, None, ALU.subtract))
                            for p_ in (PI_A, PI_B, PI_C):
                                link(nc.vector.scalar_tensor_tensor(out=t, in0=b, scalar=-p_, in1=t,
                                                                    op0=ALU.mult, op1=ALU.add))
                            inc(nc.vector.tensor_scalar(a, t, PI_LE, -PI_LE, ALU.min, ALU.max), "mlp_arg")
                        wait(dve, "mlp_sin", 3)
                        link(nc.vector.memset(hdn_s[HID:P, 0:1], 0.0))
                        inc(nc.vector.tensor_scalar(hdn_d[:], hdn_s[:], fil[:, C_SGN:C_SGN + 1], None, ALU.mult), "hdn")
                    if k == "F":
                        def lo(n):
                            cc, x = n // 2, n % 2
                            cn = CHUNKS[cc][1]
                            wait(dve, "sd_hi", nth("sd_hi"))
                            rest("sd_lo", sp_l[0:cn, cc, x], tmp_a[0:cn, n % 4], sp_h[0:cn, cc, x])
                        nth("F")
                        dve.wait_ge(win_in, 32 * c["F"])
                        if c.get("pq_hi"):
                            wait(dve, "pq_lo", c["pq_hi"])
                            wait(dve, "z_done", 4 * c["F"] - 4)
                        for n in range(6):
                            cc, x = n // 2, n % 2
                            cn = CHUNKS[cc][1]
                            job = ("sd", it[1], it[2], cc, x)
                            wait_full(dve, job)
                            if n >= 4:
                                wait(dve, "sd_lo", 6 * c["F"] - 6 + n - 3)
                            inc(nc.vector.tensor_tensor(tmp_a[0:cn, n % 4], bank(job, cn, NF), win[0:cn, cc], ALU.mult),
                                "sd_win")
                            if n:
                                lo(n - 1)
                        lo(5)
                    if k == "T":
                        for cc, (_, cn) in enumerate(CHUNKS):
                            wait(dve, "zt_hi", nth("zt"))
                            rest("zt_lo", zt_l[0:cn, cc], bank((*it, cc), cn, NF), zt_h[0:cn, cc])
                    if k == "W":
                        nth("W")

                        def lo(cc):
                            cn = CHUNKS[cc][1]
                            for x in range(2):
                                wait(dve, "pq_hi", nth("pq_hi"))
                                rest("pq_lo", sp_l[0:cn, cc, x], (tmp_a, tmp_b)[cc % 2][0:cn, 2 * x], sp_h[0:cn, cc, x])
                        wait(dve, "kf_done", 6 * c["W"])
                        wait(dve, "sd_lo", 6 * c["W"])
                        for cc, (_, cn) in enumerate(CHUNKS):
                            t = (tmp_a, tmp_b)[cc % 2]
                            re, im = (*it, cc, 0), (*it, cc, 1)
                            wait_full(dve, im)
                            wait_full(dve, re)
                            if cc == 2:
                                wait(dve, "pq_lo", 6 * c["W"] - 4)
                            for a, b, d in ((re, 0, 0), (im, 1, 1), (re, 1, 2), (im, 0, 3)):
                                ins = nc.vector.tensor_tensor(t[0:cn, d], bank(a, cn, NF), kf[0:cn, cc, b], ALU.mult)
                            inc(ins, "z_prod")
                            if cc:
                                lo(cc - 1)
                        lo(2)
                    if k == "I":
                        for i in range(HALF):
                            j = HALF * it[2] + i
                            job = (*it, i)
                            wait_full(dve, job)
                            if it[1] == 0:
                                wait(dve, "hy_done", plan.place(("hy", 16 + j)))
                                wait(dve, "hy_done", plan.place(("hy", j)))
                            else:
                                wait(dve, "hy_done", plan.place(("hy", KC + j)))
                            sk = C_SKIP + it[1] * KC + j
                            inc(nc.vector.scalar_tensor_tensor(out=z[:, j], in0=z[:, j], scalar=par[:, sk:sk + 1],
                                                               in1=bank(job), op0=ALU.mult, op1=ALU.add), "inv_read")
                            wait(dve, "inv_read", nth("inv"))
                            inc(nc.vector.tensor_tensor(z[:, j], z[:, j], (x1, x2)[it[1]][:, j], ALU.mult), "z_done")
                        if it[1] == 1:
                            for i in range(HALF):
                                j = HALF * it[2] + i
                                wait(dve, "b_hi", j + 1)
                                rest("b_lo", bl[:, j], z[:, j], bh[:, j])
                    if k == "norm":
                        n = it[1]
                        wait_full(dve, it)
                        inc(nc.vector.tensor_scalar(ms[:], bank(it), 1.0 / D_MODEL, EPS, ALU.mult, ALU.add), "ms_read")
                        wait(dve, "ms_read", n + 1)
                        inc(nc.vector.reciprocal(ms[:], ms[:]), "ms_rec")
                        wait(dve, "rstd_done", n + 1)
                        for j in range(KC + 1):
                            if j < KC:
                                g = (C_N1, C_N2)[n] + j
                                inc(nc.vector.scalar_tensor_tensor(out=utmp[:, j], in0=h[:, j], scalar=par[:, g:g + 1],
                                                                   in1=rstd[:], op0=ALU.mult, op1=ALU.mult), "u_f32")
                            if j:
                                wait(dve, "u_hi", nth("u"))
                                rest("u_lo", ul[:, j - 1], utmp[:, j - 1], uh[:, j - 1])
                    if k == "hy":
                        j = it[1]
                        y, x = hy_dst(j), bank(it)
                        wait(dve, "hy_tap", plan.place(it))
                        col = C_HW + j
                        link(nc.vector.scalar_tensor_tensor(out=y[:, 1:T], in0=x[:, 0:T - 1], scalar=par[:, col:col + 1],
                                                            in1=y[:, 1:T], op0=ALU.mult, op1=ALU.add))
                        col += 48
                        inc(nc.vector.scalar_tensor_tensor(out=y[:, 0:T - 1], in0=x[:, 1:T], scalar=par[:, col:col + 1],
                                                           in1=y[:, 0:T - 1], op0=ALU.mult, op1=ALU.add), "hy_done")
                    if k == "lx":
                        j = it[1]
                        y, x = xc[:, j], bank(it)
                        wait(dve, "lx_tap", j + 1)
                        for i, a, b in ((0, 2, 0), (1, 1, 0), (3, 0, 1)):
                            col = C_LW + i * KC + j
                            n = T - max(a, b)
                            ins = nc.vector.scalar_tensor_tensor(out=y[:, a:a + n], in0=x[:, b:b + n],
                                                                 scalar=par[:, col:col + 1], in1=y[:, a:a + n],
                                                                 op0=ALU.mult, op1=ALU.add)
                            if i < 3:
                                link(ins)
                        inc(ins, "lx_done")
                    if k == "G":
                        f = it[1]
                        wait(dve, "lx_hi", f + 1)
                        rest("lx_lo", ll[:, 4 * f:4 * f + 4], xc[:, 4 * f:4 * f + 4], lh[:, 4 * f:4 * f + 4])
                        split_to(plan.first_slab[it] + 2 + SPL)
                    if k == "LR":
                        f = it[1]
                        flat = lambda t: t.rearrange("p a b t -> p (a b t)")
                        wait(dve, "gate_done", 16 * (f + 1))
                        for d in range(2):
                            ins = nc.vector.tensor_tensor(li[:, d], li[:, d], xc[:, 4 * f:4 * f + 4], ALU.mult)
                            if d == 0:
                                ins.then_inc(dve_step, 1)
                                steps[0] += 1
                        link(ins)
                        wait(dve, "lru_ab", 8 * (f + 1))
                        link(nc.vector.tensor_tensor(la2[:], lr[:], lr[:], ALU.mult))
                        inc(nc.vector.scalar_tensor_tensor(out=flat(lth[:]), in0=flat(la2[:]), scalar=1.0,
                                                           in1=flat(lth[:]), op0=ALU.add, op1=ALU.mult), "lru_th")
                        wait(dve, "lru_sq", f + 1)
                        link(nc.vector.tensor_tensor(li[:], li[:], lth[:], ALU.mult))
                        for n in range(HALF):
                            nc.vector.tensor_tensor_scan(la2[:, 0, n], lr[:, 0, n], li[:, 0, n], 0.0,
                                                         ALU.mult, ALU.add).then_inc(dve_step, 1)
                            nc.vector.tensor_tensor_scan(la2[:, 1, n][:, ::-1], lr[:, 1, n][:, ::-1],
                                                         li[:, 1, n][:, ::-1], 0.0,
                                                         ALU.mult, ALU.add).then_inc(dve_step, 1)
                            steps[0] += 2
                        dve.wait_ge(dve_step, steps[0])
                        link(nc.vector.tensor_tensor(lth[:, 0], la2[:, 0], la2[:, 1], ALU.add))
                        inc(nc.vector.tensor_tensor(lth[:, 0], lth[:, 0], gl[:, 4 * f:4 * f + 4], ALU.mult), "lru_y")
                        wait(dve, "l_hi", f + 1)
                        rest("l_lo", ll[:, 4 * f:4 * f + 4], lth[:, 0], lh[:, 4 * f:4 * f + 4])
                    if k == "mp":
                        b, j = it[1:]
                        g = plan.place(("mg", b, j))
                        s = sg[:, (g - 1) % SG]
                        wait(dve, "mg_done", g)
                        wait_full(dve, it)
                        if b == 0:
                            inc(nc.vector.tensor_tensor(merged[:, j], s, bank(it), ALU.mult), "mp_done")
                        else:
                            wait(dve, "mp_done", 8 * b)
                            link(nc.vector.tensor_tensor(s, s, bank(it), ALU.mult))
                            inc(nc.vector.tensor_tensor(merged[:, j], merged[:, j], s, ALU.add), "mp_done")
                    if k in ("rq", "rk"):
                        r = rope_place(it)
                        x = 0 if k == "rq" else 1
                        wait_full(dve, it)
                        if r > 1:
                            wait(dve, "rope_lo", r - 1)
                        link(nc.vector.tensor_tensor(ra[:], pair(it), cs[:, 0:1].to_broadcast([P, 2, T]), ALU.mult))
                        inc(nc.vector.tensor_tensor(rb[:], pair(it), cs[:, 1:2].to_broadcast([P, 2, T]), ALU.mult),
                            "rope_ab")
                        wait(dve, "rope_hi", r)
                        rest("rope_lo", qk_l[:, x], ra[:], qk_h[:, x])
                    if k == "RT":
                        for cc, (_, cn) in enumerate(CHUNKS):
                            wait(dve, "vt_hi", nth("vt"))
                            rest("vt_lo", vt_l[0:cn, cc], bank((*it, cc), cn, 256), vt_h[0:cn, cc])
                    if k == "RS":
                        def lo(cc):
                            cn = CHUNKS[cc][1]
                            n = nth("sc_lo")
                            wait(dve, "sc_hi", n)
                            rest("sc_lo", sc_l[0:cn, cc], sc[0:cn, n % 2], sc_h[0:cn, cc])
                        dve.wait_ge(dec_in, 16)
                        for cc, (_, cn) in enumerate(CHUNKS):
                            n = nth("sc")
                            wait_full(dve, (*it, cc))
                            if n > 2:
                                wait(dve, "sc_lo", n - 2)
                            inc(nc.vector.tensor_tensor(sc[0:cn, n % 2], bank((*it, cc), cn), dec[0:cn, cc, it[1]],
                                                        ALU.mult), "sc_read")
                            if cc:
                                lo(cc - 1)
                        lo(2)
                    if k == "RM":
                        wait_full(dve, it)
                        for e in range(2):
                            ins = nc.vector.scalar_tensor_tensor(out=ry[:, e], in0=bank(it), scalar=-1.0 / 256,
                                                                 in1=ry[:, e], op0=ALU.mult, op1=ALU.add)
                            if e == 0:
                                link(ins)
                        inc(ins, "mean_done")
                    if k == "RV":
                        n = it[1]
                        wait_full(dve, it)
                        link(nc.vector.tensor_scalar(ms[:], bank(it), 1.0 / 256, EPS, ALU.mult, ALU.add))
                        inc(nc.vector.reciprocal(ms[:], ms[:]), "var_rec")
                        wait(dve, "rstd_r", n + 1)
                        wait(dve, "rg_done", n + 1)
                        link(nc.vector.tensor_tensor(ry[:], ry[:], gs[:], ALU.mult))
                        inc(nc.vector.tensor_tensor(ry[:], ry[:], rstd[:, None, :].to_broadcast([P, 2, T]), ALU.mult),
                            "yb_done")
                        wait(dve, "b_hi", KC + n + 1)
                        rest("b_lo", bl[:, 2 * n:2 * n + 2], ry[:], bh[:, 2 * n:2 * n + 2])
                    if k == "ms":
                        for f in range(4):
                            wait(dve, "m_hi", f + 1)
                            rest("m_lo", ll[:, 2 * f:2 * f + 2], merged[:, 2 * f:2 * f + 2], lh[:, 2 * f:2 * f + 2])
                    if k in ("wo", "dn"):
                        j = it[1]
                        if k == "dn":
                            for m in range(j * FT // KC, (j + 1) * FT // KC):
                                split_to(plan.first_down + m + SPL)
                        wait_full(dve, it)
                        inc(nc.vector.tensor_tensor(h[:, j], h[:, j], bank(it), ALU.add), k + "_done")
                    if k == "fu":
                        i = it[1]
                        s = sg[:, i % SG]
                        wait(dve, "fg_done", i + 1)
                        wait_full(dve, it)
                        inc(nc.vector.tensor_tensor(s, s, bank(it), ALU.mult), "hid_f32")
                        wait(dve, "hid_hi", i + 1)
                        rest("hid_lo", hl[:, i], s, hh[:, i])

            @block.tensor
            def _(pe):
                slab_at = [0]

                def free(job):
                    for j in plan.before[job]:
                        name, n = freed(j)
                        wait(pe, name, n)

                def done(ins, job):
                    ins.then_inc(full[plan.nth[job][0]], 1)

                def passes(dst, tiles):
                    n = len(tiles)
                    for i, (sh, sl, mh, ml) in enumerate(tiles):
                        nc.tensor.matmul(dst, sh, mh, start=(i == 0), stop=False)
                        nc.tensor.matmul(dst, sl, mh, start=False, stop=False)
                        ins = nc.tensor.matmul(dst, sh, ml, start=False, stop=(i == n - 1))
                    return ins

                def weight(slab, t):
                    s = slab % SPL
                    return wh[:, s, t * P:(t + 1) * P], wl[:, s, t * P:(t + 1) * P]

                def project(dst, xh, xl):
                    n = slab_at[0]
                    slab_at[0] += 1
                    pe.wait_ge(slab_lo, n + 1)
                    return passes(dst, [(*weight(n, t), xh[:, t], xl[:, t]) for t in range(KC)])

                def transform(dst, mat_h, mat_l, x, c0, cn, vh, vl):
                    return passes(dst, [(mat_h[0:n, c, x, c0:c0 + cn], mat_l[0:n, c, x, c0:c0 + cn],
                                         vh(c, n), vl(c, n)) for c, (_, n) in enumerate(CHUNKS)])

                for it in plan.items:
                    k = it[0]
                    if k == "mlp":
                        pe.wait_ge(par_in, 32)
                        for i in range(3):
                            job = ("mlp", i)
                            if i == 0:
                                w, x = fil[0:EMB, C_W1:C_W1 + HID], zf[:]
                            else:
                                wait(pe, "mlp_sin", i)
                                w = fil[0:HID, C_W2:C_W2 + HID] if i == 1 else fil[0:HID, C_W3:C_W3 + P]
                                x = mact[0:HID, i - 1]
                            free(job)
                            done(nc.tensor.matmul(bank(job, HID if i < 2 else P), w, x, start=True, stop=True), job)
                    if k == "F":
                        o, f = it[1:]
                        kn = 2 * o + f
                        wait(pe, "hdn", 1)
                        pe.wait_ge(win_in, 32 * (kn + 1))
                        for c, (c0, cn) in enumerate(CHUNKS):
                            for x in range(2):
                                job = ("sd", o, f, c, x)
                                free(job)
                                done(nc.tensor.matmul(bank(job, cn, NF), (hdn_s, hdn_d)[x][:, c0:c0 + cn], wo_t[:],
                                                      start=True, stop=True), job)
                        wait(pe, "sd_lo", 6 * (kn + 1))
                        for c, (c0, cn) in enumerate(CHUNKS):
                            for x in range(2):
                                job = ("K", o, f, c, x)
                                free(job)
                                done(transform(bank(job, cn, NF), fwd_h, fwd_l, x, c0, cn,
                                               lambda q, n: sp_h[0:n, q, x], lambda q, n: sp_l[0:n, q, x]), job)
                    if k == "T":
                        o, f = it[1:]
                        if o == 0:
                            wait(pe, "hy_done", plan.place(("hy", 16 + 4 * f + 3)))
                        else:
                            wait(pe, "z_done", 4 * f + 4)
                        for c, (c0, cn) in enumerate(CHUNKS):
                            job = (*it, c)
                            free(job)
                            for i in range(HALF):
                                ins = nc.tensor.transpose(ps[0:cn, plan.bank[job], i * P:(i + 1) * P],
                                                          z[:, HALF * f + i, c0:c0 + cn], ident[:])
                            done(ins, job)
                    if k == "W":
                        wait(pe, "zt_lo", 3 * plan.place(it))
                        for c, (c0, cn) in enumerate(CHUNKS):
                            for x in range(2):
                                job = (*it, c, x)
                                free(job)
                                done(transform(bank(job, cn, NF), fwd_h, fwd_l, x, c0, cn,
                                               lambda q, n: zt_h[0:n, q], lambda q, n: zt_l[0:n, q]), job)
                    if k == "I":
                        wait(pe, "pq_lo", 6 * plan.place(it))
                        for i in range(HALF):
                            job = (*it, i)
                            free(job)
                            done(passes(bank(job), [(sp_h[0:n, c, x, i * P:(i + 1) * P], sp_l[0:n, c, x, i * P:(i + 1) * P],
                                                     inv_h[0:n, c, x], inv_l[0:n, c, x])
                                                    for c, (_, n) in enumerate(CHUNKS) for x in range(2)]), job)
                    if k == "norm":
                        for j in range(KC):
                            wait(pe, "sq_done", KC * it[1] + j + 1)
                            if j == 0:
                                free(it)
                            ins = nc.tensor.matmul(bank(it), ones[:], utmp[:, j], start=(j == 0), stop=(j == KC - 1))
                        done(ins, it)
                        wait(pe, "u_lo", KC * (it[1] + 1))
                    if k in ("hy", "lx", "lg", "mg", "fg", "fu"):
                        free(it)
                        done(project(bank(it), uh, ul), it)
                    if k in ("rq", "rk", "rv", "rg"):
                        free(it)
                        project(ps[:, plan.bank[it], 0:T], uh, ul)
                        done(project(ps[:, plan.bank[it] + 1, 0:T], uh, ul), it)
                    if k == "mp":
                        if it[1] == 0:
                            wait(pe, "b_lo", KC)
                        elif it[1] == 1:
                            wait(pe, "l_lo", 2)
                        else:
                            wait(pe, "b_lo", KC + HEADS)
                        free(it)
                        done(project(bank(it), *((lh, ll) if it[1] == 1 else (bh, bl))), it)
                    if k == "G":
                        f = it[1]
                        wait(pe, "lx_lo", f + 1)
                        for n in range(HALF):
                            slab = slab_at[0]
                            if n % 2 == 0:
                                pe.wait_ge(slab_lo, slab + 1)
                            for d in range(2):
                                for g in range(2):
                                    job = ("G", HALF * f + n, d, g)
                                    free(job)
                                    done(passes(bank(job), [(*weight(slab, (n % 2) * 4 + 2 * d + g),
                                                             lh[:, HALF * f + n], ll[:, HALF * f + n])]), job)
                            if n % 2 == 1:
                                slab_at[0] += 1
                    if k == "RT":
                        wait(pe, "rv_done", it[1] + 1)
                        for c, (c0, cn) in enumerate(CHUNKS):
                            job = (*it, c)
                            free(job)
                            for e in range(2):
                                ins = nc.tensor.transpose(ps[0:cn, plan.bank[job], e * P:(e + 1) * P],
                                                          rv[:, e, c0:c0 + cn], ident[:])
                            done(ins, job)
                    if k == "RS":
                        wait(pe, "rope_lo", 2 * (it[1] + 1))
                        for c, (c0, cn) in enumerate(CHUNKS):
                            job = (*it, c)
                            free(job)
                            done(passes(bank(job, cn), [(qk_h[:, 1, e, c0:c0 + cn], qk_l[:, 1, e, c0:c0 + cn],
                                                         qk_h[:, 0, e], qk_l[:, 0, e]) for e in range(2)]), job)
                    if k == "RP":
                        wait(pe, "vt_lo", 3 * (it[1] + 1))
                        wait(pe, "sc_lo", 3 * (it[1] + 1))
                        free(it)
                        for e in range(2):
                            ins = passes(ps[:, plan.bank[it] + e, 0:T],
                                         [(vt_h[0:n, c, e * P:(e + 1) * P], vt_l[0:n, c, e * P:(e + 1) * P],
                                           sc_h[0:n, c], sc_l[0:n, c]) for c, (_, n) in enumerate(CHUNKS)])
                        done(ins, it)
                    if k in ("RM", "RV"):
                        wait(pe, "y_done" if k == "RM" else "rsq_done", it[1] + 1)
                        free(it)
                        for e in range(2):
                            ins = nc.tensor.matmul(bank(it), ones[:], (ry if k == "RM" else rsq)[:, e],
                                                   start=(e == 0), stop=(e == 1))
                        done(ins, it)
                    if k == "wo":
                        wait(pe, "m_lo", 4)
                        free(it)
                        done(project(bank(it), lh, ll), it)
                    if k == "dn":
                        j = it[1]
                        wait(pe, "hid_lo", FT)
                        free(it)
                        for i in range(FT):
                            g = FT * j + i
                            m = g // 8
                            slab = plan.first_down + m
                            if g % 8 == 0 or i == 0:
                                pe.wait_ge(slab_lo, slab + 1)
                            a, b = weight(slab, g % 8)
                            nc.tensor.matmul(bank(it), a, hh[:, i], start=(i == 0), stop=False)
                            nc.tensor.matmul(bank(it), b, hh[:, i], start=False, stop=False)
                            ins = nc.tensor.matmul(bank(it), a, hl[:, i], start=False, stop=(i == FT - 1))
                            if g % 8 == 7 and i != FT - 1:
                                ins.then_inc(down_slab, 1)
                        done(ins, it)

        n_layer = len(sems)
        with nc.Fori(0, DEPTH) as layer:
            with nc.Block() as block:
                layer_body(layer, block)
            nc.all_engine_barrier(sems_to_clear=range(sems[0].num, sems[n_layer - 1].num + 1))

        e_sq, e_ms, e_var, e_rstd, e_y, e_out = (sem(n) for n in ("e_sq", "e_ms", "e_var", "e_rstd", "e_y", "e_out"))
        with nc.Block() as block:
            @block.scalar
            def _(act):
                for j in range(KC):
                    nc.scalar.activation(utmp[:, j], h[:, j], ACT.Square).then_inc(e_sq, 1)
                act.wait_ge(e_var, 2)
                nc.scalar.activation(rstd[:], ms[:], ACT.Sqrt).then_inc(e_rstd, 1)

            @block.tensor
            def _(pe):
                for j in range(KC):
                    pe.wait_ge(e_sq, j + 1)
                    ins = nc.tensor.matmul(ps[:, 0, 0:T], ones[:], utmp[:, j], start=(j == 0), stop=(j == KC - 1))
                ins.then_inc(e_ms, 1)

            @block.vector
            def _(dve):
                dve.wait_ge(e_ms, 1)
                nc.vector.tensor_scalar(ms[:], ps[:, 0, 0:T], 1.0 / D_MODEL, EPS, ALU.mult, ALU.add).then_inc(e_var, 1)
                dve.wait_ge(e_var, 1)
                nc.vector.reciprocal(ms[:], ms[:]).then_inc(e_var, 1)
                dve.wait_ge(e_rstd, 1)
                for j in range(KC):
                    nc.vector.scalar_tensor_tensor(out=utmp[:, j, N_META:T], in0=h[:, j, N_META:T],
                                                   scalar=finp[:, j:j + 1], in1=rstd[:, N_META:T],
                                                   op0=ALU.mult, op1=ALU.mult).then_inc(e_y, 1)

            @block.sync
            def _(sp):
                for q in range(4):
                    sp.wait_ge(e_y, 2 * q + 2)
                    sp.dma_start(out[:, 2 * q:2 * q + 2], utmp[:, 2 * q:2 * q + 2, N_META:T]).then_inc(e_out, 16)
                sp.wait_ge(e_out, 64)


def constants():
    n2 = 2 * T
    pos = np.arange(T, dtype=np.float64)
    ang = 2 * np.pi * (pos[:, None] + 0.5) * pos[None, :] / n2

    def chunked(a):
        r = np.zeros((CM, 3, *a.shape[1:]), np.float32)
        for c, (c0, cn) in enumerate(CHUNKS):
            r[:cn, c] = a[c0:c0 + cn]
        return r

    cfwd = chunked(np.stack([np.cos(ang.T), -np.sin(ang.T)], 1))
    cinv = chunked(np.stack([np.cos(ang), -np.sin(ang)], 1) * (2.0 / n2))
    half = 128
    inv = np.power(10000.0, -np.linspace(0.0, 1.0, half, dtype=np.float32).astype(np.float64)).astype(np.float32)
    a = (np.arange(T, dtype=np.float32)[None, :] * inv[:, None]).astype(np.float64)
    rope = np.stack([np.cos(a), np.sin(a)], 1).astype(np.float32)
    dist = np.abs(pos[:, None] - pos[None, :])
    lg = np.log1p(-(2.0 ** (-5.0 - np.arange(HEADS))))
    decay = chunked((np.exp(dist[:, None, :] * lg[None, :, None]) / 16.0))
    tn = (np.arange(T, dtype=np.float32) / np.float32(T - 1)).astype(np.float64)
    lo, hi = np.log(1e-2) / 1.5, np.log(1e-2) / 0.3
    deltas = np.abs(np.linspace(lo, hi, D_MODEL).astype(np.float32)).astype(np.float64)
    window = chunked(np.exp(-tn[:, None] * deltas[None, :]))
    bands = np.linspace(1e-4, BANDS - 1, BANDS).astype(np.float32)
    w = (np.float32(2 * np.pi / T) * np.arange(T, dtype=np.float32)[:, None] * bands[None, :]).astype(np.float64)
    zfeat = np.concatenate([tn[:, None], np.cos(w), np.sin(w)], 1).T.astype(np.float32)
    return {"cfwd": cfwd, "cinv": cinv, "rope": rope, "decay": decay, "window": window,
            "zfeat": np.ascontiguousarray(zfeat), "ident_in": np.eye(P, dtype=np.float32)}


def lay_out(i):
    f32 = np.float32
    hseq = np.concatenate([i["meta_tokens"], i["x"][0]], 0)
    a = {"h0": hseq.T.reshape(KC, P, T).transpose(1, 0, 2)}

    slabs = np.empty((DEPTH * N_SLAB, P, KC, P), f32)
    for l in range(DEPTH):
        tiles = lambda w: w.reshape(w.shape[0] // P, P, w.shape[1] // P, P)
        src = {
            "in": tiles(i["w_in"][l]).transpose(2, 1, 0, 3),
            "branch": np.concatenate([tiles(i["w_branch"][l, b]).transpose(2, 1, 0, 3) for b in range(3)]),
            "out": tiles(i["w_out"][l]).transpose(2, 1, 0, 3),
            "gate": i["lru_gate_w"][l].reshape(4, 4, 2, P, P).transpose(1, 3, 2, 0, 4).reshape(4, P, KC, P),
            "gu": tiles(i["ffn_w_gu"][l]).transpose(2, 1, 0, 3),
            "down": tiles(i["ffn_w_down"][l]).transpose(2, 0, 1, 3).reshape(FT, 8, P, P).transpose(0, 2, 1, 3),
        }
        for n, (kind, at) in enumerate(PLAN.slabs):
            slabs[l * N_SLAB + n] = src[kind][at]
    a["slabs"] = slabs.reshape(DEPTH * N_SLAB, P, KC * P)

    rows = lambda x: x.reshape(-1, P).T
    a["params"] = np.stack([np.concatenate([rows(i[n][l]) for n in (
        "norm1_g", "norm2_g", "hy_conv_w", "hy_conv_b", "hy_skip", "lru_conv_w", "lru_conv_b", "lru_gate_b",
        "lru_lambda")], 1) for l in range(DEPTH)])
    filt = np.zeros((DEPTH, P, N_FIL), f32)
    for l in range(DEPTH):
        filt[l, :EMB, C_W1:C_W1 + HID] = i["hy_f_w1"][l]
        filt[l, :HID, C_W2:C_W2 + HID] = i["hy_f_w2"][l]
        for s in range(2):
            r = slice(s * HID, (s + 1) * HID)
            filt[l, :HID, C_W3 + s * HID:C_W3 + (s + 1) * HID] = i["hy_f_w3"][l]
            for col, n in ((C_B1, "hy_f_b1"), (C_B2, "hy_f_b2"), (C_B3, "hy_f_b3"), (C_FR, "hy_f_freq")):
                filt[l, r, col] = i[n][l]
        filt[l, :HID, C_SGN] = 1.0
        filt[l, HID:, C_SGN] = -1.0
    a["filt"] = filt
    wo = i["hy_f_wout"].reshape(DEPTH, HID, 2, 2, 2, NF).transpose(0, 2, 4, 3, 1, 5)
    a["wout"] = wo.reshape(DEPTH * 4, P, NF)
    a["fin_g"] = rows(i["final_g"])
    a.update(constants())
    return {n: np.ascontiguousarray(v) for n, v in a.items()}


def kernel(**inputs):
    import concourse.bacc as bacc
    from concourse.bass_utils import run_bass_kernel_spmd as run

    arrays = lay_out({n: np.asarray(v) for n, v in inputs.items()})
    nc = bacc.Bacc("TRN2", target_bir_lowering=False, num_devices=1)
    aps = {n: nc.dram_tensor(n, a.shape, F32, kind="ExternalInput").ap() for n, a in arrays.items()}
    out = nc.dram_tensor("out", (P, KC, SEQ), F32, kind="ExternalOutput").ap()
    build(nc, out=out, **aps)
    r = run(nc, [arrays], core_ids=[0])
    got = r.results[0]["out"]
    return np.ascontiguousarray(got.transpose(2, 1, 0)).reshape(1, SEQ, D_MODEL)
```

```python
from contextlib import ExitStack

import numpy as np
import concourse.bass as bass
from concourse import mybir

P = 128
DEPTH = 2
D_MODEL = 1024
SEQ = 256
N_META = 16
T = SEQ + N_META
EPS = 1e-6
KC = D_MODEL // P
HEADS = 4
D_FF = 2816
FT = D_FF // P
HID = 64
EMB = 33
BANDS = 16
CHUNKS = [(0, 96), (96, 96), (192, 80)]
CM = 96
REM = T - 2 * P
TAIL = 32
ROWS = (P, P, 3 * TAIL)
N_PAT = 3
FW = 2 * 2 * P + N_PAT * P
NF = 512
HALF = 4
RAW = 3
SPL = 3
BANKS = 7
SG = 6

F32 = mybir.dt.float32
F32R = mybir.dt.float32r
ALU = mybir.AluOpType
ACT = mybir.ActivationFunctionType

C_N1, C_N2 = 0, 8
C_HW, C_HB = 16, 88
C_SKIP = 112
C_LW, C_LB = 128, 160
C_GB = 168
C_LAM = 200
N_PAR = 216
C_W1, C_W2, C_W3 = 0, 64, 128
C_B1, C_B2, C_B3, C_FR, C_SGN = 256, 257, 258, 259, 260
N_FIL = 261


def schedule():
    hy = lambda *js: [("hy", j) for j in js]
    lx = lambda *js: [("lx", j) for j in js]
    lg = lambda *js: [("lg", j) for j in js]
    s = [("u", 0)] + hy(16) + [("M", 0)] + hy(17, 18) + [("M", 1)] + hy(19, 20) + [("M", 2)] + hy(21, 22)
    s += [("Fs", 0, 0)] + hy(23, 0) + [("FK", 0, 0), ("T", 0, 0)] + hy(1, 2) + [("W", 0, 0)] + hy(3) + [("c8",)] + hy(4)
    s += [("I", 0, 0), ("Fs", 0, 1)] + hy(5) + [("FK", 0, 1), ("T", 0, 1)] + hy(6, 7) + [("W", 0, 1)] + hy(8, 9, 10)
    s += [("I", 0, 1), ("Fs", 1, 0)] + hy(11, 12) + [("FK", 1, 0), ("T", 1, 0)] + hy(13, 14) + [("W", 1, 0)]
    s += hy(15) + lx(0, 1) + [("I", 1, 0), ("Fs", 1, 1)] + lx(2, 3) + [("FK", 1, 1), ("T", 1, 1)] + lx(4, 5)
    s += [("W", 1, 1)] + lx(6, 7) + lg(0) + [("I", 1, 1)] + lg(1, 2, 3, 4) + [("LX", 0)] + lg(5, 6) + [("G", 0)] + lg(7)
    m = [(k, 0, j) for j in range(8) for k in ("mg", "mp")] + [("mg", 1, j) for j in range(6)]
    lru = lambda f: [("La", f), 1, ("Lb", f), 2, ("Lc", f), 2, ("Ld", f), 1, ("Le", f), 1, ("Lf", f), 1, ("Lg", f)]
    chain = lru(0) + [("LX", 1), 2, ("G", 1), 1] + lru(1) + [3]
    for c in chain:
        if isinstance(c, tuple):
            s += [c]
        else:
            s, m = s + m[:c], m[c:]
    assert not m
    for j in range(8):
        s += [("mp", 1, j)]
        if j + 6 < 8:
            s += [("mg", 1, j + 6)]
    s += [("rq", 0), ("rv", 0), ("qlo", 0), ("rk", 0), ("rg", 0), ("klo", 0)]
    for h in range(HEADS):
        last = h == HEADS - 1
        s += [("RT", h), ("RS", h)]
        s += [("mg", 2, 0), ("mg", 2, 1)] if last else [("rv", h + 1)]
        s += [("RP", h)]
        s += [("mg", 2, 2)] if last else [("rq", h + 1)]
        s += [("RM", h)]
        s += [("mg", 2, 3)] if last else [("qlo", h + 1), ("rk", h + 1)]
        s += [("RV", h)]
        s += [("mg", 2, 4), ("mg", 2, 5)] if last else [("klo", h + 1), ("rg", h + 1)]
    s += [("mp", 2, 0), ("mp", 2, 1), ("mg", 2, 6), ("mg", 2, 7), ("mp", 2, 2), ("ms", 0), ("mp", 2, 3), ("mp", 2, 4),
          ("ms", 1), ("mp", 2, 5), ("mp", 2, 6), ("ms", 2), ("mp", 2, 7), ("ms", 3)]
    for k, n in (("wo", 0), ("dn", 1)):
        for j in range(KC):
            s += [(k, j)] + ([("nq", n, j - 1)] if j else [])
        s += [("nq", n, KC - 1), ("nf", n)]
        if n == 0:
            s += [("u", 1)]
            for i in range(FT):
                s += [("fg", i), ("fu", i)]
    return s


def item_slabs(it):
    k = it[0]
    if k == "hy":
        return [("in", it[1])]
    if k == "lx":
        return [("in", 24 + it[1])]
    if k == "lg":
        return [("in", 32 + it[1])]
    if k in ("rq", "rk", "rv", "rg"):
        first = {"rq": 40, "rk": 48, "rv": 56, "rg": 64}[k] + 2 * it[1]
        return [("in", first), ("in", first + 1)]
    if k == "mg":
        return [("in", 72 + 8 * it[1] + it[2])]
    if k == "mp":
        return [("branch", 8 * it[1] + it[2])]
    if k == "G":
        return [("gate", 2 * it[1]), ("gate", 2 * it[1] + 1)]
    if k == "wo":
        return [("out", it[1])]
    if k == "fg":
        return [("gu", it[1])]
    if k == "fu":
        return [("gu", FT + it[1])]
    return []


SPECTRA = [(0, 0), (0, 1), (1, 0), (1, 1), (2, 0)]


def item_jobs(it):
    k = it[0]
    if k == "Fs":
        return [((k, *it[1:], c, x), 1) for c in range(3) for x in range(2)]
    if k in ("FK", "W"):
        return [((k, *it[1:], c, x), 1) for c, x in SPECTRA]
    if k == "T":
        return [(("T", *it[1:], c), 1) for c in range(3)]
    if k == "I":
        return [(("I", *it[1:], i), 1) for i in range(HALF)]
    if k == "G":
        return [(("G", 4 * it[1] + n, d, g), 1) for n in range(HALF) for d in range(2) for g in range(2)]
    if k in ("rq", "rk", "rv", "rg", "RP"):
        return [(it, 2)]
    if k in ("RT", "RS"):
        return [((k, it[1], c), 1) for c in range(3)]
    if k in ("u", "La", "Lb", "Lc", "Ld", "Le", "Lf", "Lg", "LX", "qlo", "klo", "ms", "nq", "nf", "c8"):
        return []
    return [(it, 1)]


class Plan:

    def __init__(self):
        self.items = schedule()
        self.slabs, self.first_slab = [], {}
        self.bank, self.nth = {}, {}
        self.jobs = []
        self.before = {}
        self.order = {}
        used, owner, at = [0] * BANKS, [None] * BANKS, 0
        slab_job, self.pairs = [], 0
        for it in self.items:
            self.first_slab[it] = len(self.slabs) - (not item_jobs(it) and len(self.slabs) > 0)
            self.order.setdefault(it[0], []).append(it)
            mine = item_slabs(it)
            self.slabs += mine
            for job, n in item_jobs(it):
                if at + n > BANKS:
                    at = 0
                self.bank[job] = at
                self.before[job] = [owner[b] for b in range(at, at + n) if owner[b] is not None]
                for b in range(at, at + n):
                    owner[b] = job
                used[at + n - 1] += 1
                self.nth[job] = (at + n - 1, used[at + n - 1])
                self.jobs.append(job)
                if job[0] != it[0] or job != it:
                    self.order.setdefault(("job", job[0]), []).append(job)
                at = (at + n) % BANKS
            if it[0] == "G":
                g = [j for j, _ in item_jobs(it)]
                slab_job += [g[7], g[15]]
            elif len(mine) == 2:
                self.pairs = self.pairs + 1
                slab_job += [self.pairs, it]
            elif mine:
                slab_job += [it]
        self.first_down = len(self.slabs)
        self.slabs += [("down", n) for n in range(FT)]
        self.slab_job = slab_job

    def place(self, it):
        return self.order[it[0]].index(it) + 1

    def jplace(self, job):
        return self.order[("job", job[0])].index(job) + 1


PLAN = Plan()
N_SLAB = len(PLAN.slabs)
U = KC * T * 4


class Signals:

    def __init__(self, sem):
        self.mlp_read = sem("mlp_read")
        self.mlp_arg = sem("mlp_arg")
        self.mlp_sin = sem("mlp_sin")
        self.hdn = sem("hdn")
        self.sd_win = sem("sd_win")
        self.sd_hi = sem("sd_hi")
        self.sd_lo = sem("sd_lo")
        self.kf_done = sem("kf_done")
        self.zt_hi = sem("zt_hi")
        self.zt_lo = sem("zt_lo")
        self.z_prod = sem("z_prod")
        self.pq = sem("pq")
        self.pq_hi = sem("pq_hi")
        self.pq_lo = sem("pq_lo")
        self.inv_read = sem("inv_read")
        self.z_done = sem("z_done")
        self.z_tail = sem("z_tail")
        self.b_hi = sem("b_hi")
        self.b_lo = sem("b_lo")
        self.sq_done = sem("sq_done")
        self.ms_sum = sem("ms_sum")
        self.ms_rec = sem("ms_rec")
        self.rstd_done = sem("rstd_done")
        self.u_f32 = sem("u_f32")
        self.u_hi = sem("u_hi")
        self.u_lo = sem("u_lo")
        self.hy_tap = sem("hy_tap")
        self.hy_done = sem("hy_done")
        self.lx_tap = sem("lx_tap")
        self.lx_done = sem("lx_done")
        self.lg_done = sem("lg_done")
        self.lx_hi = sem("lx_hi")
        self.lx_lo = sem("lx_lo")
        self.gate_done = sem("gate_done")
        self.lru_tanh = sem("lru_tanh")
        self.lru_ab = sem("lru_ab")
        self.lru_ix = sem("lru_ix")
        self.lru_th = sem("lru_th")
        self.lru_sq = sem("lru_sq")
        self.lru_b = sem("lru_b")
        self.lru_scan = sem("lru_scan")
        self.lru_sum = sem("lru_sum")
        self.lru_y = sem("lru_y")
        self.l_hi = sem("l_hi")
        self.l_lo = sem("l_lo")
        self.mg_done = sem("mg_done")
        self.mp_done = sem("mp_done")
        self.rv_done = sem("rv_done")
        self.rope_ab = sem("rope_ab")
        self.rope_f = sem("rope_f")
        self.rope_hi = sem("rope_hi")
        self.rope_lo = sem("rope_lo")
        self.rg_done = sem("rg_done")
        self.vt_hi = sem("vt_hi")
        self.vt_lo = sem("vt_lo")
        self.sc_read = sem("sc_read")
        self.sc_hi = sem("sc_hi")
        self.sc_lo = sem("sc_lo")
        self.y_done = sem("y_done")
        self.mean_done = sem("mean_done")
        self.rsq_done = sem("rsq_done")
        self.var_rec = sem("var_rec")
        self.rstd_r = sem("rstd_r")
        self.yb_done = sem("yb_done")
        self.m_hi = sem("m_hi")
        self.m_lo = sem("m_lo")
        self.wo_done = sem("wo_done")
        self.fg_done = sem("fg_done")
        self.hid_f32 = sem("hid_f32")
        self.hid_hi = sem("hid_hi")
        self.hid_lo = sem("hid_lo")
        self.dn_done = sem("dn_done")
        self.lam_exp = sem("lam_exp")
        self.c8_done = sem("c8_done")
        self.pair_slab = sem("pair_slab")
        self.raw_next = sem("raw_next")
        self.par_next = sem("par_next")
        self.win_next = sem("win_next")


def build(nc, h0, slabs, params, filt, wout, fin_g, cfwd, cinv, cfwd_s, cinv_s, rope, decay, window, zfeat, ident_in, out):
    plan = PLAN
    sems = []

    with ExitStack() as ctx:
        def sem(name):
            s = ctx.enter_context(nc.semaphore(name))
            sems.append(s)
            return s

        top = [(nc.sbuf_base + 31) // 32 * 32]

        def at(name, shape, offset, dt=F32):
            size = 4 * int(np.prod(shape[1:]))
            assert offset + size <= nc.sbuf_usable_end, (name, offset, size)
            return nc.alloc_sbuf_tensor_at(name, shape, dt, offset=offset)

        def sb(name, shape, dt=F32):
            t = at(name, shape, top[0], dt)
            top[0] += (4 * int(np.prod(shape[1:])) + 31) // 32 * 32
            return t

        h = sb("h", [P, KC, T])
        uh = sb("uh", [P, KC, T], F32R)
        ul = sb("ul", [P, KC, T], F32R)
        raw = sb("raw", [P, RAW, KC * P])
        wh = sb("wh", [P, SPL, KC * P], F32R)
        wl = sb("wl", [P, SPL, KC * P], F32R)
        fwd_h = sb("fwd_h", [P, 2, FW], F32R)
        fwd_l = sb("fwd_l", [P, 2, FW], F32R)
        fwd_s = sb("fwd_s", [3 * TAIL, FW], F32R)
        inv_h = sb("inv_h", [P, 2, 2, T], F32R)
        inv_l = sb("inv_l", [P, 2, 2, T], F32R)
        inv_s = sb("inv_s", [P, T], F32R)
        inv_sl = sb("inv_sl", [P // 2, T], F32R)
        cs = sb("cs", [P, 2, T])
        ones = sb("ones", [P, P])
        ident = sb("ident", [P, P])
        zf = sb("zf", [EMB, T])
        par = sb("par", [P, N_PAR])
        fil = sb("fil", [P, N_FIL])
        c8 = sb("c8", [P, 2, 2 * KC])
        hdn_s = sb("hdn_s", [P, T])
        hdn_d = sb("hdn_d", [P, T])
        rstd = sb("rstd", [P, T])
        ms = sb("ms", [P, T])
        finp = sb("finp", [P, KC])
        U0 = top[0]
        utmp = at("utmp", [P, KC, T], U0)
        tmp_b = at("tmp_b", [P, 4, NF], U0)
        A0 = U0 + U

        oA, oB, oC, oD, oG, oX, oL, oE = (A0 + x for x in (0, U, 2 * U, 3 * U, 3 * U + 12288, 3 * U + 24576,
                                                           4 * U + 24576, 5 * U + 24576))
        oT = oE + 24576
        x1 = at("x1", [P, KC, T], oA)
        x2 = at("x2", [P, KC, T], oB)
        z = at("z", [P, KC, T], oC)
        zt_h = at("zt_h", [P, 2, NF], oD, F32R)
        zt_l = at("zt_l", [P, 2, NF], oD + 4096, F32R)
        zt_s = at("zt_s", [3 * TAIL, NF], oD + 8192, F32R)
        hdn_t = at("hdn_t", [P, 2, 3, TAIL], oD + 10240)
        lsp = at("lsp", [P, 5, 2 * KC], oD + 11008)
        kf = at("kf", [P, 2, 2, NF], oG)
        kf_r = at("kf_r", [P, NF], oG + 8192)
        sp_h = at("sp_h", [P, 2, 2, NF], oE, F32R)
        sp_l = at("sp_l", [P, 2, 2, NF], oE + 8192, F32R)
        sd_s = at("sd_s", [3 * TAIL, 2, NF], oE + 16384, F32R)
        sp_s = at("sp_s", [P, NF], oE + 16384, F32R)
        rem = at("rem", [P, NF], oE + 20480)
        z_t = at("z_t", [P, HALF, 3, TAIL], oE + 22528)
        tmp_a = at("tmp_a", [P, 4, NF], oT)
        win = at("win", [P, 3, NF], oL)
        wo_t = at("wo_t", [P, NF], oL + 6144)
        marg = at("marg", [P, 3, T], oT)
        mact = at("mact", [P, 2, T], oT + 3264)
        bh = at("bh", [P, KC, T], oA, F32R)
        bl = at("bl", [P, KC, T], oB, F32R)
        xc = at("xc", [P, KC, T], oX)
        gl = at("gl", [P, KC, T], oL)
        lh = at("lh", [P, KC, T], oE, F32R)
        ll = at("ll", [P, KC, T], oE + U, F32R)
        lth = at("lth", [P, 2, HALF, T], oC)
        lr = at("lr", [P, 2, HALF, T], oD)
        li = at("li", [P, 2, HALF, T], oG)
        la2 = at("la2", [P, 2, HALF, T], U0)
        merged = at("merged", [P, KC, T], oT)
        sg = at("sg", [P, SG, T], oE + 2 * U)
        dec = at("dec", [CM, 3, HEADS, T], oC)
        o = oC + 3 * HEADS * T * 4
        qk_h = at("qk_h", [P, 2, 2, T], o, F32R)
        qk_l = at("qk_l", [P, 2, 2, T], o + 4352, F32R)
        rv = at("rv", [P, 2, T], o + 8704)
        vt_h = at("vt_h", [CM, 3, 256], o + 10880, F32R)
        vt_l = at("vt_l", [CM, 3, 256], o + 13952, F32R)
        rot = [[at(f"rot_{x}{y}", [P, 2, T], base + 2176 * "cs".index(y)) for y in "cs"]
               for x, base in (("q", o + 17024), ("k", U0))]
        sc = at("sc", [CM, 2, T], o + 21376)
        sc_h = at("sc_h", [CM, 3, T], o + 23552, F32R)
        sc_l = at("sc_l", [CM, 3, T], o + 26816, F32R)
        ry = at("ry", [P, 2, T], o + 30080)
        rsq = at("rsq", [P, 2, T], o + 32256)
        gs = at("gs", [P, 2, T], o + 34432)
        hh = at("hh", [P, FT, T], oA, F32R)
        hl = at("hl", [P, FT, T], oA + FT * T * 4, F32R)
        raw_fwd, raw_inv = at("raw_fwd", [P, 2, FW], oA), at("raw_inv", [P, 2, 2, T], oA + 8 * FW)
        raw_fs, raw_is = at("raw_fs", [3 * TAIL, FW], oA + 32768), at("raw_is", [P, T], oA + 32768 + 4 * FW)

        ps = ctx.enter_context(nc.psum_tensor("ps", [P, BANKS + 1, 512], F32))

        full = [sem(f"bank_full{b}") for b in range(BANKS)]
        raw_in = [sem(f"raw_in{r}") for r in range(RAW)]
        slab_hi, slab_lo, down_slab = sem("slab_hi"), sem("slab_lo"), sem("down_slab")
        win_in, dec_in = sem("win_in"), sem("dec_in")
        dve_step, act_step = sem("dve_step"), sem("act_step")
        S = Signals(sem)

        def made(job):
            b, n = plan.nth[job]
            return full[b], n

        def freed(job):
            k = job[0]
            jp = plan.jplace if ("job", k) in plan.order else None
            if k == "M":
                return S.mlp_read, job[1] + 1
            if k in ("Fs", "FK", "T", "I", "G", "RT", "RS"):
                return {"Fs": S.sd_win, "FK": S.kf_done, "T": S.zt_lo, "I": S.inv_read, "G": S.gate_done,
                        "RT": S.vt_lo, "RS": S.sc_read}[k], jp(job)
            if k == "W":
                return S.z_prod, 3 * ((jp(job) - 1) // 5) + job[4 - 1] + 1
            if k in ("rq", "rk"):
                return S.rope_ab, rope_place(job)
            return {"hy": S.hy_done, "lx": S.lx_done, "lg": S.lg_done, "mg": S.mg_done, "mp": S.mp_done,
                    "rv": S.rv_done, "rg": S.rg_done, "RP": S.y_done, "RM": S.mean_done, "RV": S.var_rec,
                    "wo": S.wo_done, "fg": S.fg_done, "fu": S.hid_f32, "dn": S.dn_done}[k], plan.place(job)

        def rope_place(it):
            return [i for i in plan.items if i[0] in ("rq", "rk")].index(it) + 1

        def slab_used(n):
            if n < plan.first_down:
                job = plan.slab_job[n]
                return (S.pair_slab, job) if isinstance(job, int) else made(job)
            m = n - plan.first_down + 1
            if (8 * m) % FT == 0:
                return made(("dn", 8 * m // FT - 1))
            return down_slab, m - m // 11

        def hy_dst(j):
            return (x1, x2, z)[j // KC][:, j % KC]

        def bank(job, m=P, n=T):
            return ps[0:m, plan.bank[job], 0:n]

        def pair(job):
            b = plan.bank[job]
            return ps[:, b:b + 2, 0:T]

        assert N_SLAB % RAW == 0

        def load_params(eng, layer):
            return eng.dma_start(par[:], params[bass.ds(layer, 1)].rearrange("a p n -> p (a n)"))

        def load_fil(eng, layer):
            return eng.dma_start(fil[:], filt[bass.ds(layer, 1)].rearrange("a p n -> p (a n)"))

        def load_window(eng, f):
            return eng.dma_start(win[:], window[:, :, f * NF:(f + 1) * NF])

        def load_wout(eng, k):
            return eng.dma_start(wo_t[:], wout[bass.ds(k, 1)].rearrange("a p n -> p (a n)"))

        c_in, c_hi, c_one = sem("c_in"), sem("c_hi"), sem("c_one")
        c_first, c_sq, c_ms, c_rec = sem("c_first"), sem("c_sq"), sem("c_ms"), sem("c_rec")
        with nc.Block() as block:
            @block.sync
            def _(sp):
                sp.dma_start(raw_fwd[:], cfwd).then_inc(c_in, 16)
                sp.dma_start(raw_inv[:], cinv).then_inc(c_in, 16)
                sp.dma_start(raw_fs[:], cfwd_s).then_inc(c_in, 16)
                sp.dma_start(raw_is[:], cinv_s).then_inc(c_in, 16)
                sp.dma_start(h[:], h0).then_inc(c_in, 16)
                sp.dma_start(cs[:], rope).then_inc(c_in, 16)
                sp.dma_start(ident[:], ident_in).then_inc(c_in, 16)
                sp.dma_start(zf[:], zfeat).then_inc(c_in, 16)
                sp.dma_start(finp[:], fin_g).then_inc(c_in, 16)
                load_params(sp, 0).then_inc(c_first, 16)
                load_fil(sp, 0).then_inc(c_first, 16)
                load_window(sp, 0).then_inc(c_first, 16)
                load_wout(sp, 0).then_inc(c_first, 16)
                for n in range(RAW):
                    sp.dma_start(raw[:, n], slabs[n]).then_inc(c_first, 16)
                sp.wait_ge(c_first, 16 * (4 + RAW))

            @block.scalar
            def _(act):
                act.wait_ge(c_in, 9 * 16)
                nc.scalar.activation(fwd_h[:], raw_fwd[:], ACT.Copy).then_inc(c_hi, 1)
                nc.scalar.activation(inv_h[:], raw_inv[:], ACT.Copy).then_inc(c_hi, 1)
                nc.scalar.activation(fwd_s[:], raw_fs[:], ACT.Copy).then_inc(c_hi, 1)
                nc.scalar.activation(inv_s[:], raw_is[:], ACT.Copy).then_inc(c_hi, 1)
                for j in range(KC):
                    nc.scalar.activation(utmp[:, j], h[:, j], ACT.Square).then_inc(c_sq, 1)
                act.wait_ge(c_rec, 2)
                nc.scalar.activation(rstd[:], ms[:], ACT.Sqrt).then_inc(c_hi, 1)
                act.wait_ge(c_hi, 5)

            @block.tensor
            def _(pe):
                pe.wait_ge(c_one, 1)
                for j in range(KC):
                    pe.wait_ge(c_sq, j + 1)
                    ins = nc.tensor.matmul(ps[:, BANKS, 0:T], ones[:], utmp[:, j], start=(j == 0), stop=(j == KC - 1))
                ins.then_inc(c_ms, 1)

            @block.vector
            def _(dve):
                nc.vector.memset(ones[:], 1.0).then_inc(c_one, 1)
                dve.wait_ge(c_hi, 1)
                nc.vector.tensor_tensor(fwd_l[:], raw_fwd[:], fwd_h[:].bitcast(F32), ALU.subtract).then_inc(c_one, 1)
                dve.wait_ge(c_hi, 2)
                nc.vector.tensor_tensor(inv_l[:], raw_inv[:], inv_h[:].bitcast(F32), ALU.subtract).then_inc(c_one, 1)
                dve.wait_ge(c_hi, 3)
                mid = slice(TAIL, 2 * TAIL)
                nc.vector.tensor_tensor(fwd_s[mid], raw_fs[mid], fwd_s[mid].bitcast(F32), ALU.subtract).then_inc(c_one, 1)
                dve.wait_ge(c_hi, 4)
                nc.vector.tensor_tensor(inv_sl[:], raw_is[0:P // 2], inv_s[0:P // 2].bitcast(F32),
                                        ALU.subtract).then_inc(c_one, 1)
                dve.wait_ge(c_one, 5)
                dve.wait_ge(c_ms, 1)
                nc.vector.tensor_scalar(ms[:], ps[:, BANKS, 0:T], 1.0 / D_MODEL, EPS, ALU.mult, ALU.add).then_inc(c_rec, 1)
                dve.wait_ge(c_rec, 1)
                nc.vector.reciprocal(ms[:], ms[:]).then_inc(c_rec, 1)

        def layer_body(layer, block):
            @block.sync
            def _(sp):
                def load(n):
                    return sp.dma_start(raw[:, n % RAW],
                                        slabs[bass.ds(layer * N_SLAB + n, 1)].rearrange("a p n -> p (a n)"))

                for n in range(RAW, N_SLAB):
                    sp.wait_ge(slab_lo, n - RAW + 1)
                    load(n).then_inc(raw_in[n % RAW], 16)
                    if n == plan.first_slab[("fg", 8)]:
                        sp.wait_ge(S.u_f32, 2 * KC)
                        load_params(sp, layer + 1).then_inc(S.par_next, 16)
                        load_fil(sp, layer + 1).then_inc(S.par_next, 16)
                for n in range(N_SLAB, N_SLAB + RAW):
                    sp.wait_ge(slab_lo, n - RAW + 1)
                    load(n).then_inc(S.raw_next, 16)
                sp.wait_ge(S.raw_next, 16 * RAW)
                sp.wait_ge(S.par_next, 32)

            @block.gpsimd
            def _(pool):
                n = 0
                for it in plan.items:
                    if it[0] == "W":
                        for c in range(2):
                            t = (tmp_a, tmp_b)[c]
                            pool.wait_ge(S.z_prod, 3 * n + c + 1)
                            nc.gpsimd.tensor_tensor(t[:, 0], t[:, 0], t[:, 1], ALU.subtract).then_inc(S.pq, 1)
                            nc.gpsimd.tensor_tensor(t[:, 2], t[:, 2], t[:, 3], ALU.add).then_inc(S.pq, 1)
                        n += 1
                    if it[0] == "La":
                        f = it[1]
                        pool.wait_ge(S.gate_done, 16 * (f + 1))
                        for d in range(2):
                            nc.gpsimd.tensor_tensor(li[:, d], li[:, d], xc[:, 4 * f:4 * f + 4], ALU.mult).then_inc(S.lru_ix, 1)
                    if it[0] in ("rq", "rk"):
                        a, b = rot["qk".index(it[0][1])]
                        pool.wait_ge(S.rope_ab, rope_place(it))
                        nc.gpsimd.tensor_tensor(a[:, 0], a[:, 0], b[:, 1], ALU.subtract).then_inc(S.rope_f, 1)
                        nc.gpsimd.tensor_tensor(a[:, 1], a[:, 1], b[:, 0], ALU.add).then_inc(S.rope_f, 1)

            @block.scalar
            def _(act):
                steps = [0]
                splits = [0]

                def link(ins):
                    steps[0] += 1
                    ins.then_inc(act_step, 1)
                    act.wait_ge(act_step, steps[0])

                def split_to(n):
                    while splits[0] < min(n, N_SLAB):
                        m = splits[0]
                        if m >= RAW:
                            act.wait_ge(raw_in[m % RAW], 16 * (m // RAW))
                        if m >= SPL:
                            act.wait_ge(*slab_used(m - SPL))
                        nc.scalar.activation(wh[:, m % SPL], raw[:, m % RAW], ACT.Copy).then_inc(slab_hi, 1)
                        splits[0] += 1

                def rnd(dst, src):
                    return nc.scalar.activation(dst, src, ACT.Copy)

                def load_filter(k):
                    act.wait_ge(S.sd_win, 6 * k)
                    act.wait_ge(*made(("Fs", (k - 1) // 2, (k - 1) % 2, 2, 1)))
                    load_window(act, k % 2).then_inc(win_in, 16)
                    load_wout(act, layer * 4 + k).then_inc(win_in, 16)

                split_to(SPL)
                c = {}

                def nth(name):
                    c[name] = c.get(name, 0) + 1
                    return c[name]

                for it in plan.items:
                    k = it[0]
                    split_to(plan.first_slab[it] + SPL)
                    if k == "M":
                        i = it[1]
                        act.wait_ge(S.mlp_arg, i + 1)
                        d = (mact[0:HID, 0], mact[0:HID, 1], hdn_s[:])[i]
                        nc.scalar.activation(d, marg[0:HID, 0] if i < 2 else marg[:, 0], ACT.Sin).then_inc(S.mlp_sin, 1)
                    if k == "Fs":
                        for n in range(6):
                            cc, x = n // 2, n % 2
                            cn = ROWS[cc]
                            act.wait_ge(S.sd_win, nth("sd"))
                            rnd(sp_h[:, cc, x] if cc < 2 else sd_s[:, x], tmp_a[0:cn, n % 4]).then_inc(S.sd_hi, 1)
                    if k == "FK":
                        for cc, x in SPECTRA:
                            job = ("FK", it[1], it[2], cc, x)
                            act.wait_ge(*made(job))
                            if (cc, x) == (0, 0) and c.get("W"):
                                act.wait_ge(S.z_prod, 3 * c["W"])
                            nc.scalar.copy(kf[:, cc, x] if cc < 2 else kf_r[:], bank(job, P, NF)).then_inc(S.kf_done, 1)
                    if k == "FK" and it[1:] != (1, 1):
                        load_filter(2 * it[1] + it[2] + 1)
                    if k == "c8":
                        lam = par[:, C_LAM:C_LAM + 2 * KC]
                        link(nc.scalar.activation(lsp[:, 0], lam, ACT.Abs))
                        nc.scalar.activation(lsp[:, 1], lsp[:, 0], ACT.Exp, scale=-1.0).then_inc(S.lam_exp, 1)
                    if it == ("fg", 4):
                        load_window(act, 0).then_inc(S.win_next, 16)
                        load_wout(act, (layer + 1) * 4).then_inc(S.win_next, 16)
                    if it == ("nf", 1):
                        act.wait_ge(S.win_next, 32)
                    if it == ("mp", 1, 0):
                        act.wait_ge(S.l_lo, 2)
                        act.dma_start(dec[:], decay).then_inc(dec_in, 16)
                    if k == "T":
                        for cc in range(3):
                            job = (*it, cc)
                            act.wait_ge(*made(job))
                            rnd(zt_h[:, cc] if cc < 2 else zt_s[:], bank(job, ROWS[cc], NF)).then_inc(S.zt_hi, 1)
                    if k == "W":
                        nth("W")
                        for cc in range(2):
                            for x in range(2):
                                act.wait_ge(S.pq, nth("pq"))
                                rnd(sp_h[:, cc, x], (tmp_a, tmp_b)[cc][:, 2 * x]).then_inc(S.pq_hi, 1)
                        act.wait_ge(S.z_prod, 3 * c["W"])
                        rnd(sp_s[:], rem[:]).then_inc(S.pq_hi, 1)
                    if k == "I" and it[1] == 1:
                        for i in range(HALF):
                            j = HALF * it[2] + i
                            act.wait_ge(S.z_done, 8 + j + 1)
                            rnd(bh[:, j], z[:, j]).then_inc(S.b_hi, 1)
                    if k == "nq":
                        n, j = it[1:]
                        act.wait_ge((S.wo_done, S.dn_done)[n], j + 1)
                        nc.scalar.activation(utmp[:, j], h[:, j], ACT.Square).then_inc(S.sq_done, 1)
                    if k == "nf":
                        act.wait_ge(S.ms_rec, it[1] + 1)
                        nc.scalar.activation(rstd[:], ms[:], ACT.Sqrt).then_inc(S.rstd_done, 1)
                    if k == "u":
                        for j in range(KC):
                            act.wait_ge(S.u_f32, nth("u"))
                            rnd(uh[:, j], utmp[:, j]).then_inc(S.u_hi, 1)
                    if k == "hy":
                        j = it[1]
                        act.wait_ge(*made(it))
                        nc.scalar.activation(hy_dst(j), bank(it), ACT.Identity,
                                                 bias=par[:, C_HB + j:C_HB + j + 1],
                                                 scale=par[:, C_HW + 24 + j:C_HW + 25 + j]).then_inc(S.hy_tap, 1)
                    if k == "lx":
                        j = it[1]
                        act.wait_ge(*made(it))
                        nc.scalar.activation(xc[:, j], bank(it), ACT.Identity,
                                                 bias=par[:, C_LB + j:C_LB + j + 1],
                                                 scale=par[:, C_LW + 16 + j:C_LW + 17 + j]).then_inc(S.lx_tap, 1)
                    if k == "lg":
                        act.wait_ge(*made(it))
                        if it[1] == 0:
                            act.wait_ge(S.sd_win, 24)
                            act.wait_ge(*made(("Fs", 1, 1, 2, 1)))
                        nc.scalar.activation(gl[:, it[1]], bank(it), ACT.Gelu_apprx_tanh).then_inc(S.lg_done, 1)
                    if k == "LX":
                        f = it[1]
                        if f == 0:
                            act.wait_ge(S.lx_done, KC)
                            act.wait_ge(*made(("I", 1, 1, HALF - 1)))
                        rnd(lh[:, 4 * f:4 * f + 4], xc[:, 4 * f:4 * f + 4]).then_inc(S.lx_hi, 1)
                    if k == "G":
                        f = it[1]
                        if f == 1:
                            act.wait_ge(S.lru_scan, 2)
                        else:
                            act.wait_ge(S.b_lo, KC)
                        for n in range(HALF):
                            for d in range(2):
                                for g in range(2):
                                    job = ("G", 4 * f + n, d, g)
                                    col = C_GB + (2 * d + g) * KC + 4 * f + n
                                    act.wait_ge(*made(job))
                                    nc.scalar.activation((lr, li)[g][:, d, n], bank(job), ACT.Sigmoid,
                                                             bias=par[:, col:col + 1]).then_inc(S.gate_done, 1)
                                if n % 2 == 1 and d == 1:
                                    split_to(plan.first_slab[it] + n // 2 + 1 + SPL)
                    if k in ("La", "Lb"):
                        f = it[1]
                        if k == "La":
                            act.wait_ge(S.gate_done, 16 * (f + 1))
                            act.wait_ge(S.c8_done, 2)
                        else:
                            act.wait_ge(S.lru_tanh, 8 * (f + 1))
                        for d in range(2):
                            for n in range(HALF):
                                col = d * KC + HALF * f + n
                                if k == "La":
                                    nc.scalar.activation(lth[:, d, n], lr[:, d, n], ACT.Tanh,
                                                             scale=c8[:, 0, col:col + 1]).then_inc(S.lru_tanh, 1)
                                else:
                                    nc.scalar.activation(lr[:, d, n], lr[:, d, n], ACT.Exp,
                                                             scale=c8[:, 1, col:col + 1]).then_inc(S.lru_ab, 1)
                    if k == "Ld":
                        act.wait_ge(S.lru_th, it[1] + 1)
                        nc.scalar.activation(lth[:], lth[:], ACT.Sqrt).then_inc(S.lru_sq, 1)
                    if k == "Lg":
                        f = it[1]
                        act.wait_ge(S.lru_y, f + 1)
                        rnd(lh[:, 4 * f:4 * f + 4], lth[:, 0]).then_inc(S.l_hi, 1)
                    if k == "mg":
                        s = (plan.place(it) - 1) % SG
                        act.wait_ge(*made(it))
                        if plan.place(it) == 1:
                            act.wait_ge(*made(("I", 1, 1, HALF - 1)))
                        if plan.place(it) > SG:
                            act.wait_ge(S.mp_done, plan.place(it) - SG)
                        nc.scalar.activation(sg[:, s], bank(it), ACT.Sigmoid).then_inc(S.mg_done, 1)
                    if k == "rv":
                        split_to(plan.first_slab[it] + 1 + SPL)
                        act.wait_ge(*made(it))
                        if it[1] == 0:
                            act.wait_ge(S.l_lo, 2)
                        nc.scalar.copy(rv[:], pair(it)).then_inc(S.rv_done, 1)
                    if k in ("rq", "rk"):
                        split_to(plan.first_slab[it] + 1 + SPL)
                    if k in ("qlo", "klo"):
                        x = "qk".index(k[0])
                        act.wait_ge(S.rope_f, 2 * (2 * it[1] + x + 1))
                        if it[1]:
                            act.wait_ge(*made(("RS", it[1] - 1, 2)))
                        rnd(qk_h[:, x], rot[x][0][:]).then_inc(S.rope_hi, 1)
                    if k == "rg":
                        split_to(plan.first_slab[it] + 1 + SPL)
                        act.wait_ge(*made(it))
                        if it[1]:
                            act.wait_ge(S.yb_done, it[1])
                        nc.scalar.activation(gs[:], pair(it), ACT.Silu).then_inc(S.rg_done, 1)
                    if k == "RT":
                        for cc, (_, cn) in enumerate(CHUNKS):
                            act.wait_ge(*made((*it, cc)))
                            rnd(vt_h[0:cn, cc], bank((*it, cc), cn, 256)).then_inc(S.vt_hi, 1)
                    if k == "RS":
                        for cc, (_, cn) in enumerate(CHUNKS):
                            act.wait_ge(S.sc_read, nth("sc"))
                            rnd(sc_h[0:cn, cc], sc[0:cn, c["sc"] % 2]).then_inc(S.sc_hi, 1)
                    if k == "RP":
                        act.wait_ge(*made(it))
                        if it[1]:
                            act.wait_ge(S.b_lo, KC + it[1])
                        nc.scalar.copy(ry[:], pair(it)).then_inc(S.y_done, 1)
                    if k == "RM":
                        act.wait_ge(S.mean_done, it[1] + 1)
                        nc.scalar.activation(rsq[:], ry[:], ACT.Square).then_inc(S.rsq_done, 1)
                    if k == "RV":
                        act.wait_ge(S.var_rec, it[1] + 1)
                        nc.scalar.activation(rstd[:], ms[:], ACT.Sqrt).then_inc(S.rstd_r, 1)
                        act.wait_ge(S.yb_done, it[1] + 1)
                        rnd(bh[:, 2 * it[1]:2 * it[1] + 2], ry[:]).then_inc(S.b_hi, 1)
                    if k == "ms":
                        f = it[1]
                        act.wait_ge(S.mp_done, 16 + 2 * f + 2)
                        if f == 0:
                            act.wait_ge(*made(("mp", 1, 7)))
                        rnd(lh[:, 2 * f:2 * f + 2], merged[:, 2 * f:2 * f + 2]).then_inc(S.m_hi, 1)
                    if k == "fg":
                        i = it[1]
                        act.wait_ge(*made(it))
                        if i >= SG:
                            act.wait_ge(S.hid_lo, i - SG + 1)
                        nc.scalar.activation(sg[:, i % SG], bank(it), ACT.Silu).then_inc(S.fg_done, 1)
                    if k == "fu":
                        i = it[1]
                        act.wait_ge(S.hid_f32, i + 1)
                        rnd(hh[:, i], sg[:, i % SG]).then_inc(S.hid_hi, 1)
                    if k == "dn":
                        for m in range(it[1] * FT // KC, (it[1] + 1) * FT // KC):
                            split_to(plan.first_down + m + SPL)

            @block.vector
            def _(dve):
                steps = [0]
                splits = [0]

                def link(ins):
                    steps[0] += 1
                    ins.then_inc(dve_step, 1)
                    dve.wait_ge(dve_step, steps[0])

                def split_to(n):
                    while splits[0] < min(n, N_SLAB):
                        m = splits[0]
                        dve.wait_ge(slab_hi, m + 1)
                        nc.vector.tensor_tensor(wl[:, m % SPL], raw[:, m % RAW], wh[:, m % SPL].bitcast(F32),
                                                ALU.subtract).then_inc(slab_lo, 1)
                        splits[0] += 1

                def rest(dst, src, hi):
                    return nc.vector.tensor_tensor(dst, src, hi.bitcast(F32), ALU.subtract)

                c = {}

                def nth(name):
                    c[name] = c.get(name, 0) + 1
                    return c[name]

                split_to(SPL)

                last3 = slice(2 * TAIL, 3 * TAIL)
                TWO_PI = 2 * np.pi
                PI_A = 6.28125
                PI_B = float(np.float32(TWO_PI - PI_A))
                PI_C = float(TWO_PI - PI_A - PI_B)
                PI_LE = 3.1415925
                MAGIC = 1.5 * 2.0 ** 23
                for it in plan.items:
                    k = it[0]
                    split_to(plan.first_slab[it] + SPL)
                    if k == "c8":
                        dve.wait_ge(S.lam_exp, 1)
                        e, s, s2, r = lsp[:, 1], lsp[:, 2], lsp[:, 3], lsp[:, 4]
                        link(nc.vector.tensor_scalar(s2, e, 2.0, None, ALU.add))
                        link(nc.vector.reciprocal(s, s2))
                        link(nc.vector.tensor_tensor(s, e, s, ALU.mult))
                        link(nc.vector.tensor_tensor(s2, s, s, ALU.mult))
                        link(nc.vector.tensor_scalar(r, s2, 1.0 / 15, None, ALU.mult))
                        for q in (13, 11, 9, 7, 5, 3):
                            link(nc.vector.scalar_tensor_tensor(out=r, in0=r, scalar=1.0 / q, in1=s2, op0=ALU.add, op1=ALU.mult))
                        link(nc.vector.scalar_tensor_tensor(out=r, in0=r, scalar=1.0, in1=s, op0=ALU.add, op1=ALU.mult))
                        link(nc.vector.tensor_scalar(s, par[:, C_LAM:C_LAM + 2 * KC], -1.0, 0.0, ALU.mult, ALU.max))
                        link(nc.vector.scalar_tensor_tensor(out=s, in0=r, scalar=2.0, in1=s, op0=ALU.mult, op1=ALU.add))
                        nc.vector.tensor_scalar(c8[:, 0], s, 8.0, None, ALU.mult).then_inc(S.c8_done, 1)
                        nc.vector.tensor_scalar(c8[:, 1], s, -8.0, None, ALU.mult).then_inc(S.c8_done, 1)
                    if k == "M":
                        i = it[1]
                        m = HID if i < 2 else P
                        a, b, t = marg[0:m, 0], marg[0:m, 1], marg[0:m, 2]
                        col = (C_B1, C_B2, C_B3)[i]
                        dve.wait_ge(*made(it))
                        nc.vector.tensor_scalar(t, bank(it, m), fil[0:m, col:col + 1],
                                                    fil[0:m, C_FR:C_FR + 1], ALU.add, ALU.mult).then_inc(S.mlp_read, 1)
                        dve.wait_ge(S.mlp_read, i + 1)
                        link(nc.vector.tensor_scalar(b, t, 1 / TWO_PI, MAGIC, ALU.mult, ALU.add))
                        link(nc.vector.tensor_scalar(b, b, MAGIC, None, ALU.subtract))
                        for p_ in (PI_A, PI_B, PI_C):
                            link(nc.vector.scalar_tensor_tensor(out=t, in0=b, scalar=-p_, in1=t,
                                                                op0=ALU.mult, op1=ALU.add))
                        nc.vector.tensor_scalar(a, t, PI_LE, -PI_LE, ALU.min, ALU.max).then_inc(S.mlp_arg, 1)
                    if it == ("Fs", 0, 0):
                        dve.wait_ge(S.mlp_sin, 3)
                        link(nc.vector.memset(hdn_s[HID:P, 0:1], 0.0))
                        nc.vector.tensor_scalar(hdn_d[:], hdn_s[:], fil[:, C_SGN:C_SGN + 1], None, ALU.mult).then_inc(S.hdn, 1)
                        dve.wait_ge(S.hdn, 1)
                        for x in range(2):
                            nc.vector.tensor_copy(hdn_t[:, x], (hdn_s, hdn_d)[x][:, None, T - TAIL:T].to_broadcast([P, 3, TAIL])) \
                                .then_inc(S.hdn, 1)
                    if k == "Fs":
                        def lo(n):
                            cc, x = n // 2, n % 2
                            dve.wait_ge(S.sd_hi, nth("sd_hi"))
                            if cc < 2:
                                rest(sp_l[:, cc, x], tmp_a[:, n % 4], sp_h[:, cc, x]).then_inc(S.sd_lo, 1)
                            else:
                                rest(sd_s[last3, x], tmp_a[last3, n % 4], sd_s[last3, x]).then_inc(S.sd_lo, 1)
                        nth("F")
                        if c["F"] > 1:
                            dve.wait_ge(win_in, 32 * (c["F"] - 1))
                        if c.get("pq_hi"):
                            dve.wait_ge(S.pq_lo, c["pq_hi"])
                            dve.wait_ge(S.z_done, 4 * c["F"] - 4)
                        for n in range(6):
                            cc, x = n // 2, n % 2
                            cn = ROWS[cc]
                            job = ("Fs", it[1], it[2], cc, x)
                            dve.wait_ge(*made(job))
                            if n >= 4:
                                dve.wait_ge(S.sd_lo, 6 * c["F"] - 6 + n - 3)
                            nc.vector.tensor_tensor(tmp_a[0:cn, n % 4], bank(job, cn, NF), win[0:cn, cc], ALU.mult).then_inc(S.sd_win, 1)
                            if n:
                                lo(n - 1)
                        lo(5)
                    if k == "T":
                        o, f = it[1:]
                        if o == 0:
                            dve.wait_ge(S.hy_done, plan.place(("hy", 16 + 4 * f + 3)))
                        else:
                            dve.wait_ge(S.z_done, 4 * f + 4)
                        if plan.place(it) > 1:
                            dve.wait_ge(*made((*plan.order["T"][plan.place(it) - 2], 2)))
                        nc.vector.tensor_copy(z_t[:], z[:, HALF * f:HALF * (f + 1), None, T - TAIL:T]
                                              .to_broadcast([P, HALF, 3, TAIL])).then_inc(S.z_tail, 1)
                        for cc in range(3):
                            dve.wait_ge(S.zt_hi, nth("zt"))
                            if cc < 2:
                                rest(zt_l[:, cc], bank((*it, cc), P, NF), zt_h[:, cc]).then_inc(S.zt_lo, 1)
                            else:
                                rest(zt_s[last3], ps[last3, plan.bank[(*it, cc)], 0:NF], zt_s[last3]).then_inc(S.zt_lo, 1)
                    if k == "W":
                        nth("W")

                        def lo(cc):
                            for x in range(2):
                                dve.wait_ge(S.pq_hi, nth("pq_hi"))
                                rest(sp_l[:, cc, x], (tmp_a, tmp_b)[cc][:, 2 * x], sp_h[:, cc, x]).then_inc(S.pq_lo, 1)
                        dve.wait_ge(S.kf_done, 5 * c["W"])
                        dve.wait_ge(S.sd_lo, 6 * c["W"])
                        for cc in range(2):
                            re, im = (*it, cc, 0), (*it, cc, 1)
                            dve.wait_ge(*made(im))
                            dve.wait_ge(*made(re))
                            for a, b, d in ((re, 0, 0), (im, 1, 1), (re, 1, 2), (im, 0, 3)):
                                ins = nc.vector.tensor_tensor((tmp_a, tmp_b)[cc][:, d], bank(a, P, NF), kf[:, cc, b], ALU.mult)
                            ins.then_inc(S.z_prod, 1)
                        lo(0)
                        job = (*it, 2, 0)
                        dve.wait_ge(*made(job))
                        nc.vector.tensor_tensor(rem[:], bank(job, P, NF), kf_r[:], ALU.mult).then_inc(S.z_prod, 1)
                        lo(1)
                        dve.wait_ge(S.pq_hi, nth("pq_hi"))
                        rest(sp_s[P // 2:P], rem[P // 2:P], sp_s[P // 2:P]).then_inc(S.pq_lo, 1)
                    if k == "I":
                        for i in range(HALF):
                            j = HALF * it[2] + i
                            job = (*it, i)
                            dve.wait_ge(*made(job))
                            if it[1] == 0:
                                dve.wait_ge(S.hy_done, plan.place(("hy", 16 + j)))
                                dve.wait_ge(S.hy_done, plan.place(("hy", j)))
                            else:
                                dve.wait_ge(S.hy_done, plan.place(("hy", KC + j)))
                            sk = C_SKIP + it[1] * KC + j
                            nc.vector.scalar_tensor_tensor(out=z[:, j], in0=z[:, j], scalar=par[:, sk:sk + 1],
                                                               in1=bank(job), op0=ALU.mult, op1=ALU.add).then_inc(S.inv_read, 1)
                            dve.wait_ge(S.inv_read, nth("inv"))
                            nc.vector.tensor_tensor(z[:, j], z[:, j], (x1, x2)[it[1]][:, j], ALU.mult).then_inc(S.z_done, 1)
                        if it[1] == 1:
                            for i in range(HALF):
                                j = HALF * it[2] + i
                                dve.wait_ge(S.b_hi, j + 1)
                                rest(bl[:, j], z[:, j], bh[:, j]).then_inc(S.b_lo, 1)
                    if k == "nf":
                        n = it[1]
                        dve.wait_ge(S.ms_sum, n + 1)
                        link(nc.vector.tensor_scalar(ms[:], ps[:, BANKS, 0:T], 1.0 / D_MODEL, EPS, ALU.mult, ALU.add))
                        nc.vector.reciprocal(ms[:], ms[:]).then_inc(S.ms_rec, 1)
                    if k == "u":
                        n = it[1]
                        if n:
                            dve.wait_ge(S.rstd_done, n)
                        for j in range(KC + 1):
                            if j < KC:
                                g = (C_N1, C_N2)[n] + j
                                nc.vector.scalar_tensor_tensor(out=utmp[:, j], in0=h[:, j], scalar=par[:, g:g + 1],
                                                                   in1=rstd[:], op0=ALU.mult, op1=ALU.mult).then_inc(S.u_f32, 1)
                            if j:
                                dve.wait_ge(S.u_hi, nth("u"))
                                rest(ul[:, j - 1], utmp[:, j - 1], uh[:, j - 1]).then_inc(S.u_lo, 1)
                    if k == "hy":
                        j = it[1]
                        y, x = hy_dst(j), bank(it)
                        dve.wait_ge(S.hy_tap, plan.place(it))
                        col = C_HW + j
                        link(nc.vector.scalar_tensor_tensor(out=y[:, 1:T], in0=x[:, 0:T - 1], scalar=par[:, col:col + 1],
                                                            in1=y[:, 1:T], op0=ALU.mult, op1=ALU.add))
                        col += 48
                        nc.vector.scalar_tensor_tensor(out=y[:, 0:T - 1], in0=x[:, 1:T], scalar=par[:, col:col + 1],
                                                           in1=y[:, 0:T - 1], op0=ALU.mult, op1=ALU.add).then_inc(S.hy_done, 1)
                    if k == "lx":
                        j = it[1]
                        y, x = xc[:, j], bank(it)
                        dve.wait_ge(S.lx_tap, j + 1)
                        for i, a, b in ((0, 2, 0), (1, 1, 0), (3, 0, 1)):
                            col = C_LW + i * KC + j
                            n = T - max(a, b)
                            ins = nc.vector.scalar_tensor_tensor(out=y[:, a:a + n], in0=x[:, b:b + n],
                                                                 scalar=par[:, col:col + 1], in1=y[:, a:a + n],
                                                                 op0=ALU.mult, op1=ALU.add)
                            if i < 3:
                                link(ins)
                        ins.then_inc(S.lx_done, 1)
                    if k == "LX":
                        f = it[1]
                        dve.wait_ge(S.lx_hi, f + 1)
                        rest(ll[:, 4 * f:4 * f + 4], xc[:, 4 * f:4 * f + 4], lh[:, 4 * f:4 * f + 4]).then_inc(S.lx_lo, 1)
                    if k == "G":
                        split_to(plan.first_slab[it] + 2 + SPL)
                    if k == "Lc":
                        flat = lambda t: t.rearrange("p a b t -> p (a b t)")
                        dve.wait_ge(S.lru_ab, 8 * (it[1] + 1))
                        link(nc.vector.tensor_tensor(la2[:], lr[:], lr[:], ALU.mult))
                        nc.vector.scalar_tensor_tensor(out=flat(lth[:]), in0=flat(la2[:]), scalar=1.0,
                                                           in1=flat(lth[:]), op0=ALU.add, op1=ALU.mult).then_inc(S.lru_th, 1)
                    if k == "Le":
                        dve.wait_ge(S.lru_sq, it[1] + 1)
                        dve.wait_ge(S.lru_ix, 2 * (it[1] + 1))
                        nc.vector.tensor_tensor(li[:], li[:], lth[:], ALU.mult).then_inc(S.lru_b, 1)
                    if k in ("Le", "Lf"):
                        f, d = it[1], "ef".index(k[1])
                        way = (lambda t: t, lambda t: t[:, ::-1])[d]
                        dve.wait_ge(S.lru_b, f + 1)
                        for n in range(HALF):
                            ins = nc.vector.tensor_tensor_scan(way(la2[:, d, n]), way(lr[:, d, n]), way(li[:, d, n]), 0.0,
                                                               ALU.mult, ALU.add)
                        ins.then_inc(S.lru_scan, 1)
                    if k == "Lg":
                        f = it[1]
                        dve.wait_ge(S.lru_scan, 2 * (f + 1))
                        link(nc.vector.tensor_tensor(lth[:, 0], la2[:, 0], la2[:, 1], ALU.add))
                        nc.vector.tensor_tensor(lth[:, 0], lth[:, 0], gl[:, 4 * f:4 * f + 4], ALU.mult).then_inc(S.lru_y, 1)
                        dve.wait_ge(S.l_hi, f + 1)
                        rest(ll[:, 4 * f:4 * f + 4], lth[:, 0], lh[:, 4 * f:4 * f + 4]).then_inc(S.l_lo, 1)
                    if k == "mp":
                        b, j = it[1:]
                        g = plan.place(("mg", b, j))
                        s = sg[:, (g - 1) % SG]
                        dve.wait_ge(S.mg_done, g)
                        dve.wait_ge(*made(it))
                        if b == 0:
                            nc.vector.tensor_tensor(merged[:, j], s, bank(it), ALU.mult).then_inc(S.mp_done, 1)
                        else:
                            dve.wait_ge(S.mp_done, 8 * b)
                            link(nc.vector.tensor_tensor(s, s, bank(it), ALU.mult))
                            nc.vector.tensor_tensor(merged[:, j], merged[:, j], s, ALU.add).then_inc(S.mp_done, 1)
                    if k in ("rq", "rk"):
                        r = rope_place(it)
                        a, b = rot["qk".index(k[1])]
                        split_to(plan.first_slab[it] + 1 + SPL)
                        dve.wait_ge(*made(it))
                        if r > 2:
                            dve.wait_ge(S.rope_lo, r - 2)
                        link(nc.vector.tensor_tensor(a[:], pair(it), cs[:, 0:1].to_broadcast([P, 2, T]), ALU.mult))
                        nc.vector.tensor_tensor(b[:], pair(it), cs[:, 1:2].to_broadcast([P, 2, T]), ALU.mult) \
                            .then_inc(S.rope_ab, 1)
                    if k in ("rv", "rg"):
                        split_to(plan.first_slab[it] + 1 + SPL)
                    if k in ("qlo", "klo"):
                        x = "qk".index(k[0])
                        dve.wait_ge(S.rope_hi, 2 * it[1] + x + 1)
                        rest(qk_l[:, x], rot[x][0][:], qk_h[:, x]).then_inc(S.rope_lo, 1)
                    if k == "RT":
                        for cc, (_, cn) in enumerate(CHUNKS):
                            dve.wait_ge(S.vt_hi, nth("vt"))
                            rest(vt_l[0:cn, cc], bank((*it, cc), cn, 256), vt_h[0:cn, cc]).then_inc(S.vt_lo, 1)
                    if k == "RS":
                        def lo(cc):
                            cn = CHUNKS[cc][1]
                            n = nth("sc_lo")
                            dve.wait_ge(S.sc_hi, n)
                            rest(sc_l[0:cn, cc], sc[0:cn, n % 2], sc_h[0:cn, cc]).then_inc(S.sc_lo, 1)
                        dve.wait_ge(dec_in, 16)
                        for cc, (_, cn) in enumerate(CHUNKS):
                            n = nth("sc")
                            dve.wait_ge(*made((*it, cc)))
                            if n > 2:
                                dve.wait_ge(S.sc_lo, n - 2)
                            nc.vector.tensor_tensor(sc[0:cn, n % 2], bank((*it, cc), cn), dec[0:cn, cc, it[1]],
                                                        ALU.mult).then_inc(S.sc_read, 1)
                            if cc:
                                lo(cc - 1)
                        lo(2)
                    if k == "RM":
                        dve.wait_ge(*made(it))
                        for e in range(2):
                            ins = nc.vector.scalar_tensor_tensor(out=ry[:, e], in0=bank(it), scalar=-1.0 / 256,
                                                                 in1=ry[:, e], op0=ALU.mult, op1=ALU.add)
                            if e == 0:
                                link(ins)
                        ins.then_inc(S.mean_done, 1)
                    if k == "RV":
                        n = it[1]
                        dve.wait_ge(*made(it))
                        link(nc.vector.tensor_scalar(ms[:], bank(it), 1.0 / 256, EPS, ALU.mult, ALU.add))
                        nc.vector.reciprocal(ms[:], ms[:]).then_inc(S.var_rec, 1)
                        dve.wait_ge(S.rstd_r, n + 1)
                        dve.wait_ge(S.rg_done, n + 1)
                        link(nc.vector.tensor_tensor(ry[:], ry[:], gs[:], ALU.mult))
                        nc.vector.tensor_tensor(ry[:], ry[:], rstd[:, None, :].to_broadcast([P, 2, T]), ALU.mult).then_inc(S.yb_done, 1)
                        dve.wait_ge(S.b_hi, KC + n + 1)
                        rest(bl[:, 2 * n:2 * n + 2], ry[:], bh[:, 2 * n:2 * n + 2]).then_inc(S.b_lo, 1)
                    if k == "ms":
                        f = it[1]
                        dve.wait_ge(S.m_hi, f + 1)
                        rest(ll[:, 2 * f:2 * f + 2], merged[:, 2 * f:2 * f + 2], lh[:, 2 * f:2 * f + 2]).then_inc(S.m_lo, 1)
                    if k in ("wo", "dn"):
                        j = it[1]
                        if k == "dn":
                            for m in range(j * FT // KC, (j + 1) * FT // KC):
                                split_to(plan.first_down + m + SPL)
                        dve.wait_ge(*made(it))
                        nc.vector.tensor_tensor(h[:, j], h[:, j], bank(it), ALU.add).then_inc(S.wo_done if k == "wo" else S.dn_done, 1)
                    if k == "fu":
                        i = it[1]
                        s = sg[:, i % SG]
                        dve.wait_ge(S.fg_done, i + 1)
                        dve.wait_ge(*made(it))
                        nc.vector.tensor_tensor(s, s, bank(it), ALU.mult).then_inc(S.hid_f32, 1)
                        dve.wait_ge(S.hid_hi, i + 1)
                        rest(hl[:, i], s, hh[:, i]).then_inc(S.hid_lo, 1)

            @block.tensor
            def _(pe):
                slab_at = [0]

                def free(job):
                    for j in plan.before[job]:
                        reader, n = freed(j)
                        pe.wait_ge(reader, n)

                def passes(dst, tiles):
                    n = len(tiles)
                    for i, (sh, sl, mh, ml) in enumerate(tiles):
                        nc.tensor.matmul(dst, sh, mh, start=(i == 0), stop=False)
                        nc.tensor.matmul(dst, sl, mh, start=False, stop=False)
                        ins = nc.tensor.matmul(dst, sh, ml, start=False, stop=(i == n - 1))
                    return ins

                def weight(slab, t):
                    s = slab % SPL
                    return wh[:, s, t * P:(t + 1) * P], wl[:, s, t * P:(t + 1) * P]

                def project(dst, xh, xl, ready=None):
                    n = slab_at[0]
                    slab_at[0] += 1
                    pe.wait_ge(slab_lo, n + 1)
                    for t in range(KC):
                        if ready:
                            pe.wait_ge(ready[0], ready[1][t])
                        (sh, sl), first = weight(n, t), t == 0
                        nc.tensor.matmul(dst, sh, xh[:, t], start=first, stop=False)
                        nc.tensor.matmul(dst, sl, xh[:, t], start=False, stop=False)
                        ins = nc.tensor.matmul(dst, sh, xl[:, t], start=False, stop=(t == KC - 1))
                    return ins

                def transform(dst, columns, terms):
                    n = len(terms)
                    for i, (vh, vl, vs, at_) in enumerate(terms):
                        cols = slice(columns + at_, columns + at_ + P)
                        for p in range(2):
                            nc.tensor.matmul(dst, fwd_h[:, p, cols], vh(p), start=(i == p == 0), stop=False)
                            nc.tensor.matmul(dst, fwd_l[:, p, cols], vh(p), start=False, stop=False)
                            nc.tensor.matmul(dst, fwd_h[:, p, cols], vl(p), start=False, stop=False)
                        ins = nc.tensor.matmul(dst, fwd_s[:, cols], vs, start=False, stop=(i == n - 1))
                    return ins

                for it in plan.items:
                    k = it[0]
                    if k == "M":
                        i = it[1]
                        if i == 0:
                            w, x = fil[0:EMB, C_W1:C_W1 + HID], zf[:]
                        else:
                            pe.wait_ge(S.mlp_sin, i)
                            w = fil[0:HID, C_W2:C_W2 + HID] if i == 1 else fil[0:HID, C_W3:C_W3 + P]
                            x = mact[0:HID, i - 1]
                        free(it)
                        nc.tensor.matmul(bank(it, HID if i < 2 else P), w, x, start=True, stop=True).then_inc(full[plan.nth[it][0]], 1)
                    if k == "Fs":
                        o, f = it[1:]
                        kn = 2 * o + f
                        pe.wait_ge(S.hdn, 3)
                        if kn:
                            pe.wait_ge(win_in, 32 * kn)
                        for c in range(3):
                            for x in range(2):
                                job = ("Fs", o, f, c, x)
                                w = (hdn_s, hdn_d)[x][:, c * P:(c + 1) * P] if c < 2 else \
                                    hdn_t[:, x].rearrange("p a b -> p (a b)")
                                free(job)
                                nc.tensor.matmul(bank(job, ROWS[c], NF), w, wo_t[:],
                                                 start=True, stop=True).then_inc(full[plan.nth[job][0]], 1)
                    if k == "FK":
                        o, f = it[1:]
                        pe.wait_ge(S.sd_lo, 6 * (2 * o + f + 1))
                        term = [(lambda p, x=x: sp_h[:, p, x], lambda p, x=x: sp_l[:, p, x], sd_s[:, x]) for x in range(2)]
                        for c, x in SPECTRA:
                            job = ("FK", o, f, c, x)
                            free(job)
                            if c < 2:
                                transform(bank(job, P, NF), (2 * x + c) * P, [(*term[x], 0)]) \
                                    .then_inc(full[plan.nth[job][0]], 1)
                            else:
                                transform(bank(job, P, NF), 4 * P, [(*term[0], 0), (*term[1], P)]) \
                                    .then_inc(full[plan.nth[job][0]], 1)
                    if k == "T":
                        o, f = it[1:]
                        if o == 0:
                            pe.wait_ge(S.hy_done, plan.place(("hy", 16 + 4 * f + 3)))
                        else:
                            pe.wait_ge(S.z_done, 4 * f + 4)
                        for c in range(3):
                            job = (*it, c)
                            free(job)
                            if c == 2:
                                pe.wait_ge(S.z_tail, plan.place(it))
                            for i in range(HALF):
                                src = z[:, HALF * f + i, c * P:(c + 1) * P] if c < 2 else \
                                    z_t[:, i].rearrange("p a b -> p (a b)")
                                ins = nc.tensor.transpose(ps[0:ROWS[c], plan.bank[job], i * P:(i + 1) * P], src, ident[:])
                            ins.then_inc(full[plan.nth[job][0]], 1)
                    if k == "W":
                        pe.wait_ge(S.zt_lo, 3 * plan.place(it))
                        for c, x in SPECTRA:
                            job = (*it, c, x)
                            free(job)
                            transform(bank(job, P, NF), (2 * x + c) * P if c < 2 else 6 * P,
                                      [(lambda p: zt_h[:, p], lambda p: zt_l[:, p], zt_s[:], 0)]) \
                                .then_inc(full[plan.nth[job][0]], 1)
                    if k == "I":
                        pe.wait_ge(S.pq_lo, 5 * plan.place(it))
                        for i in range(HALF):
                            job = (*it, i)
                            cols = slice(i * P, (i + 1) * P)
                            free(job)
                            for n in range(4):
                                c, x = n // 2, n % 2
                                nc.tensor.matmul(bank(job), sp_h[:, c, x, cols], inv_h[:, c, x], start=(n == 0), stop=False)
                                nc.tensor.matmul(bank(job), sp_l[:, c, x, cols], inv_h[:, c, x], start=False, stop=False)
                                nc.tensor.matmul(bank(job), sp_h[:, c, x, cols], inv_l[:, c, x], start=False, stop=False)
                            nc.tensor.matmul(bank(job), sp_s[:, cols], inv_s[:], start=False, stop=False)
                            nc.tensor.matmul(bank(job), sp_s[0:P // 2, cols], inv_sl[:], start=False, stop=True) \
                                .then_inc(full[plan.nth[job][0]], 1)
                    if k == "nq":
                        n, j = it[1:]
                        if (n, j) == (1, 0):
                            pe.wait_ge(S.ms_rec, 1)
                        pe.wait_ge(S.sq_done, KC * n + j + 1)
                        ins = nc.tensor.matmul(ps[:, BANKS, 0:T], ones[:], utmp[:, j], start=(j == 0), stop=(j == KC - 1))
                        if j == KC - 1:
                            ins.then_inc(S.ms_sum, 1)
                    if k in ("hy", "lx", "lg", "mg", "fg", "fu"):
                        free(it)
                        ready = None
                        if it in (plan.items[1], ("fg", 0)):
                            n = int(k == "fg")
                            ready = S.u_lo, [KC * n + t + 1 for t in range(KC)]
                        project(bank(it), uh, ul, ready).then_inc(full[plan.nth[it][0]], 1)
                    if k in ("rq", "rk", "rv", "rg"):
                        free(it)
                        project(ps[:, plan.bank[it], 0:T], uh, ul).then_inc(S.pair_slab, 1)
                        project(ps[:, plan.bank[it] + 1, 0:T], uh, ul).then_inc(full[plan.nth[it][0]], 1)
                    if k == "mp":
                        free(it)
                        ready = None
                        if it[2] == 0:
                            ready = [(S.b_lo, [t + 1 for t in range(KC)]), (S.l_lo, [1] * 4 + [2] * 4),
                                     (S.b_lo, [KC + t // 2 + 1 for t in range(KC)])][it[1]]
                        project(bank(it), *((lh, ll) if it[1] == 1 else (bh, bl)), ready).then_inc(full[plan.nth[it][0]], 1)
                    if k == "G":
                        f = it[1]
                        pe.wait_ge(S.lx_lo, f + 1)
                        for n in range(HALF):
                            slab = slab_at[0]
                            if n % 2 == 0:
                                pe.wait_ge(slab_lo, slab + 1)
                            for d in range(2):
                                for g in range(2):
                                    job = ("G", HALF * f + n, d, g)
                                    free(job)
                                    passes(bank(job), [(*weight(slab, (n % 2) * 4 + 2 * d + g),
                                                             lh[:, HALF * f + n], ll[:, HALF * f + n])]).then_inc(full[plan.nth[job][0]], 1)
                            if n % 2 == 1:
                                slab_at[0] += 1
                    if k == "RT":
                        pe.wait_ge(S.rv_done, it[1] + 1)
                        for c, (c0, cn) in enumerate(CHUNKS):
                            job = (*it, c)
                            free(job)
                            for e in range(2):
                                ins = nc.tensor.transpose(ps[0:cn, plan.bank[job], e * P:(e + 1) * P],
                                                          rv[:, e, c0:c0 + cn], ident[:])
                            ins.then_inc(full[plan.nth[job][0]], 1)
                    if k == "RS":
                        pe.wait_ge(S.rope_lo, 2 * (it[1] + 1))
                        for c, (c0, cn) in enumerate(CHUNKS):
                            job = (*it, c)
                            free(job)
                            passes(bank(job, cn), [(qk_h[:, 1, e, c0:c0 + cn], qk_l[:, 1, e, c0:c0 + cn],
                                                         qk_h[:, 0, e], qk_l[:, 0, e]) for e in range(2)]).then_inc(full[plan.nth[job][0]], 1)
                    if k == "RP":
                        pe.wait_ge(S.vt_lo, 3 * (it[1] + 1))
                        pe.wait_ge(S.sc_lo, 3 * (it[1] + 1))
                        free(it)
                        for e in range(2):
                            ins = passes(ps[:, plan.bank[it] + e, 0:T],
                                         [(vt_h[0:n, c, e * P:(e + 1) * P], vt_l[0:n, c, e * P:(e + 1) * P],
                                           sc_h[0:n, c], sc_l[0:n, c]) for c, (_, n) in enumerate(CHUNKS)])
                        ins.then_inc(full[plan.nth[it][0]], 1)
                    if k in ("RM", "RV"):
                        pe.wait_ge(S.y_done if k == "RM" else S.rsq_done, it[1] + 1)
                        free(it)
                        for e in range(2):
                            ins = nc.tensor.matmul(bank(it), ones[:], (ry if k == "RM" else rsq)[:, e],
                                                   start=(e == 0), stop=(e == 1))
                        ins.then_inc(full[plan.nth[it][0]], 1)
                    if k == "wo":
                        free(it)
                        project(bank(it), lh, ll, None if it[1] else (S.m_lo, [t // 2 + 1 for t in range(KC)])).then_inc(full[plan.nth[it][0]], 1)
                    if k == "dn":
                        j = it[1]
                        free(it)
                        for i in range(FT):
                            g = FT * j + i
                            m = g // 8
                            slab = plan.first_down + m
                            if g % 8 == 0 or i == 0:
                                pe.wait_ge(slab_lo, slab + 1)
                            if j == 0:
                                pe.wait_ge(S.hid_lo, i + 1)
                            a, b = weight(slab, g % 8)
                            nc.tensor.matmul(bank(it), a, hh[:, i], start=(i == 0), stop=False)
                            nc.tensor.matmul(bank(it), b, hh[:, i], start=False, stop=False)
                            ins = nc.tensor.matmul(bank(it), a, hl[:, i], start=False, stop=(i == FT - 1))
                            if g % 8 == 7 and i != FT - 1:
                                ins.then_inc(down_slab, 1)
                        ins.then_inc(full[plan.nth[it][0]], 1)

        n_layer = len(sems)
        with nc.Fori(0, DEPTH) as layer:
            with nc.Block() as block:
                layer_body(layer, block)
            nc.all_engine_barrier(sems_to_clear=range(sems[0].num, sems[n_layer - 1].num + 1))

        e_y, e_out = sem("e_y"), sem("e_out")
        with nc.Block() as block:
            @block.vector
            def _(dve):
                for j in range(KC):
                    nc.vector.scalar_tensor_tensor(out=utmp[:, j, N_META:T], in0=h[:, j, N_META:T],
                                                   scalar=finp[:, j:j + 1], in1=rstd[:, N_META:T],
                                                   op0=ALU.mult, op1=ALU.mult).then_inc(e_y, 1)

            @block.sync
            def _(sp):
                for q in range(4):
                    sp.wait_ge(e_y, 2 * q + 2)
                    sp.dma_start(out[:, 2 * q:2 * q + 2], utmp[:, 2 * q:2 * q + 2, N_META:T]).then_inc(e_out, 16)
                sp.wait_ge(e_out, 64)


def constants():
    n2 = 2 * T
    pos = np.arange(T, dtype=np.float64)
    ang = 2 * np.pi * (pos[:, None] + 0.5) * pos[None, :] / n2

    def chunked(a):
        r = np.zeros((CM, 3, *a.shape[1:]), np.float32)
        for c, (c0, cn) in enumerate(CHUNKS):
            r[:cn, c] = a[c0:c0 + cn]
        return r

    def rows(a):
        return np.ascontiguousarray(a[:2 * P].reshape(2, P, -1).transpose(1, 0, 2)).astype(np.float32)

    fc, fs = np.cos(ang.T), -np.sin(ang.T)
    rc, rs, no = fc[:, 2 * P:], fs[:, 2 * P:], np.zeros((T, REM))
    fwd = np.concatenate([fc[:, :2 * P], fs[:, :2 * P]] + 2 * [rc, no, no, rc] + 2 * [no, rs, rs, no]
                         + 4 * [rc, rs], 1)
    tail = fwd[T - TAIL:].copy()
    tail[:TAIL - REM] = 0
    ic, is_ = np.cos(ang) * (2.0 / n2), -np.sin(ang) * (2.0 / n2)
    cinv = rows(np.concatenate([ic, is_], 1)).reshape(P, 2, 2, T)
    cinv_s = np.concatenate(2 * [ic[2 * P:], -ic[2 * P:], is_[2 * P:], is_[2 * P:]]).astype(np.float32)
    half = 128
    inv = np.power(10000.0, -np.linspace(0.0, 1.0, half, dtype=np.float32).astype(np.float64)).astype(np.float32)
    a = (np.arange(T, dtype=np.float32)[None, :] * inv[:, None]).astype(np.float64)
    rope = np.stack([np.cos(a), np.sin(a)], 1).astype(np.float32)
    dist = np.abs(pos[:, None] - pos[None, :])
    lg = np.log1p(-(2.0 ** (-5.0 - np.arange(HEADS))))
    decay = chunked((np.exp(dist[:, None, :] * lg[None, :, None]) / 16.0))
    tn = (np.arange(T, dtype=np.float32) / np.float32(T - 1)).astype(np.float64)
    lo, hi = np.log(1e-2) / 1.5, np.log(1e-2) / 0.3
    deltas = np.abs(np.linspace(lo, hi, D_MODEL).astype(np.float32)).astype(np.float64)
    w = np.exp(-tn[:, None] * deltas[None, :])
    window = np.zeros((P, 3, D_MODEL), np.float32)
    window[:, :2] = rows(w)
    window[:3 * TAIL, 2] = np.concatenate(3 * [w[T - TAIL:]])
    bands = np.linspace(1e-4, BANDS - 1, BANDS).astype(np.float32)
    w = (np.float32(2 * np.pi / T) * np.arange(T, dtype=np.float32)[:, None] * bands[None, :]).astype(np.float64)
    zfeat = np.concatenate([tn[:, None], np.cos(w), np.sin(w)], 1).T.astype(np.float32)
    return {"cfwd": rows(fwd), "cinv": cinv, "cfwd_s": np.concatenate(3 * [tail]).astype(np.float32), "cinv_s": cinv_s, "rope": rope, "decay": decay, "window": window,
            "zfeat": np.ascontiguousarray(zfeat), "ident_in": np.eye(P, dtype=np.float32)}


def lay_out(i):
    f32 = np.float32
    hseq = np.concatenate([i["meta_tokens"], i["x"][0]], 0)
    a = {"h0": hseq.T.reshape(KC, P, T).transpose(1, 0, 2)}

    slabs = np.empty((DEPTH * N_SLAB + RAW, P, KC, P), f32)
    for l in range(DEPTH):
        tiles = lambda w: w.reshape(w.shape[0] // P, P, w.shape[1] // P, P)
        src = {
            "in": tiles(i["w_in"][l]).transpose(2, 1, 0, 3),
            "branch": np.concatenate([tiles(i["w_branch"][l, b]).transpose(2, 1, 0, 3) for b in range(3)]),
            "out": tiles(i["w_out"][l]).transpose(2, 1, 0, 3),
            "gate": i["lru_gate_w"][l].reshape(4, 4, 2, P, P).transpose(1, 3, 2, 0, 4).reshape(4, P, KC, P),
            "gu": tiles(i["ffn_w_gu"][l]).transpose(2, 1, 0, 3),
            "down": tiles(i["ffn_w_down"][l]).transpose(2, 0, 1, 3).reshape(FT, 8, P, P).transpose(0, 2, 1, 3),
        }
        for n, (kind, at) in enumerate(PLAN.slabs):
            slabs[l * N_SLAB + n] = src[kind][at]
    slabs[DEPTH * N_SLAB:] = slabs[:RAW]
    a["slabs"] = slabs.reshape(-1, P, KC * P)

    rows = lambda x: x.reshape(-1, P).T
    ahead = lambda x, n: np.concatenate([x, x[:n]])
    a["params"] = ahead(np.stack([np.concatenate([rows(i[n][l]) for n in (
        "norm1_g", "norm2_g", "hy_conv_w", "hy_conv_b", "hy_skip", "lru_conv_w", "lru_conv_b", "lru_gate_b",
        "lru_lambda")], 1) for l in range(DEPTH)]), 1)
    filt = np.zeros((DEPTH, P, N_FIL), f32)
    for l in range(DEPTH):
        filt[l, :EMB, C_W1:C_W1 + HID] = i["hy_f_w1"][l]
        filt[l, :HID, C_W2:C_W2 + HID] = i["hy_f_w2"][l]
        for s in range(2):
            r = slice(s * HID, (s + 1) * HID)
            filt[l, :HID, C_W3 + s * HID:C_W3 + (s + 1) * HID] = i["hy_f_w3"][l]
            for col, n in ((C_B1, "hy_f_b1"), (C_B2, "hy_f_b2"), (C_B3, "hy_f_b3"), (C_FR, "hy_f_freq")):
                filt[l, r, col] = i[n][l]
        filt[l, :HID, C_SGN] = 1.0
        filt[l, HID:, C_SGN] = -1.0
    a["filt"] = ahead(filt, 1)
    wo = i["hy_f_wout"].reshape(DEPTH, HID, 2, 2, 2, NF).transpose(0, 2, 4, 3, 1, 5)
    a["wout"] = ahead(wo.reshape(DEPTH * 4, P, NF), 1)
    a["fin_g"] = rows(i["final_g"])
    a.update(constants())
    return {n: np.ascontiguousarray(v) for n, v in a.items()}


def kernel(**inputs):
    import concourse.bacc as bacc
    from concourse.bass_utils import run_bass_kernel_spmd as run

    arrays = lay_out({n: np.asarray(v) for n, v in inputs.items()})
    nc = bacc.Bacc("TRN2", target_bir_lowering=False, num_devices=1)
    aps = {n: nc.dram_tensor(n, a.shape, F32, kind="ExternalInput").ap() for n, a in arrays.items()}
    out = nc.dram_tensor("out", (P, KC, SEQ), F32, kind="ExternalOutput").ap()
    build(nc, out=out, **aps)
    r = run(nc, [arrays], core_ids=[0])
    got = r.results[0]["out"]
    return np.ascontiguousarray(got.transpose(2, 1, 0)).reshape(1, SEQ, D_MODEL)
```

```python
from contextlib import ExitStack

import numpy as np
import concourse.bass as bass
from concourse import mybir

P = 128
DEPTH = 2
D_MODEL = 1024
SEQ = 256
N_META = 16
T = SEQ + N_META
EPS = 1e-6
KC = D_MODEL // P
HEADS = 4
D_FF = 2816
FT = D_FF // P
HID = 64
EMB = 33
BANDS = 16
CHUNKS = [(0, 96), (96, 96), (192, 80)]
CM = 96
REM = T - 2 * P
TAIL = 32
ROWS = (P, P, 3 * TAIL)
N_PAT = 3
FW = 2 * 2 * P + N_PAT * P
NF = 512
HALF = 4
RAW = 5
SPL = 4
BANKS = 7
SG = 6

F32 = mybir.dt.float32
F32R = mybir.dt.float32r
ALU = mybir.AluOpType
ACT = mybir.ActivationFunctionType

C_N1, C_N2 = 0, 8
C_HW, C_HB = 16, 88
C_SKIP = 112
C_LW, C_LB = 128, 160
C_GB = 168
C_LAM = 200
N_PAR = 216
C_W1, C_W2, C_W3 = 0, 64, 128
C_B1, C_B2, C_B3, C_FR, C_SGN = 256, 257, 258, 259, 260
N_FIL = 261


def schedule():
    hy = lambda *js: [("hy", j) for j in js]
    lx = lambda *js: [("lx", j) for j in js]
    lg = lambda *js: [("lg", j) for j in js]
    s = [("u", 0)] + [("H",)] + hy(16, 17, 18, 19, 20, 21) + [("Fs", 0, 0)] + hy(22, 23, 0) + [("FK", 0, 0), ("T", 0, 0)]
    s += hy(1) + [("W", 0, 0)] + hy(2) + [("c8",)] + hy(3)
    s += [("I", 0, 0), ("Fs", 0, 1)] + hy(4, 5, 6) + [("FK", 0, 1), ("T", 0, 1)] + hy(7, 8) + [("W", 0, 1)] + hy(9, 10)
    s += [("I", 0, 1), ("Fs", 1, 0)] + hy(11, 12) + [("FK", 1, 0), ("T", 1, 0)] + hy(13, 14) + [("W", 1, 0)]
    s += hy(15) + lx(0, 1) + [("I", 1, 0), ("Fs", 1, 1)] + lx(2, 3) + [("FK", 1, 1), ("T", 1, 1)] + lx(4, 5)
    s += [("W", 1, 1)] + lx(6, 7) + lg(0) + [("I", 1, 1)] + lg(1, 2, 3, 4) + [("LX", 0)] + lg(5) + [("LX", 1)] + lg(6, 7) + [("G", 0)]
    m = [(k, 0, j) for j in range(8) for k in ("mg", "mp")] + [("mg", 1, j) for j in range(6)]
    lru = lambda f: [("La", f), ("Lb", f), ("Lc", f), 3, ("Lt", f), 1, ("Ld", f), 1, ("Le", f), 1, ("Lf", f), ("Lg", f), 2,
                     ("Lh", f)]
    chain = [2] + lru(0)[:-2] + [1, ("G", 1), ("Lh", 0), 2] + lru(1) + [3]
    for c in chain:
        if isinstance(c, tuple):
            s += [c]
        else:
            s, m = s + m[:c], m[c:]
    assert not m
    for j in range(8):
        s += [("mp", 1, j)]
        if j + 6 < 8:
            s += [("mg", 1, j + 6)]
    s += [("rq", 0), ("rk", 0), ("qlo", 0), ("klo", 0), ("rv", 0)]
    for h in range(HEADS):
        s += [("RS", h), ("RT", h)] + ([("RQ", h - 1), ("RN", h - 1)] if h else []) + [("rg", h), ("RP", h)]
        if h + 1 < HEADS:
            s += [("rq", h + 1), ("RM", h), ("qlo", h + 1), ("rk", h + 1), ("klo", h + 1), ("RV", h), ("rv", h + 1)]
        else:
            s += [("mg", 2, 0), ("mg", 2, 1), ("RM", h), ("mg", 2, 2), ("mg", 2, 3), ("RV", h), ("RQ", h), ("RN", h),
                  ("mg", 2, 4), ("mg", 2, 5)]
    s += [("mp", 2, 0), ("mp", 2, 1), ("mg", 2, 6), ("mg", 2, 7), ("mp", 2, 2), ("ms", 0), ("mp", 2, 3), ("mp", 2, 4),
          ("ms", 1), ("mp", 2, 5), ("mp", 2, 6), ("ms", 2), ("mp", 2, 7), ("ms", 3)]
    for k, n in (("wo", 0), ("dn", 1)):
        for j in range(KC):
            s += [(k, j)] + ([("nq", n, j - 1)] if j else [])
            if (k, j) in (("dn", 1), ("dn", 3), ("dn", 5)):
                s += [("M", j // 2)]
        s += [("nq", n, KC - 1), ("nf", n)]
        if n == 0:
            s += [("u", 1)]
            for i in range(FT):
                s += [("fg", i), ("fu", i)]
    return s


def item_slabs(it):
    k = it[0]
    if k == "hy":
        return [("in", it[1])]
    if k == "lx":
        return [("in", 24 + it[1])]
    if k == "lg":
        return [("in", 32 + it[1])]
    if k in ("rq", "rk", "rv", "rg"):
        first = {"rq": 40, "rk": 48, "rv": 56, "rg": 64}[k] + 2 * it[1]
        return [("in", first), ("in", first + 1)]
    if k == "mg":
        return [("in", 72 + 8 * it[1] + it[2])]
    if k == "mp":
        return [("branch", 8 * it[1] + it[2])]
    if k == "G":
        return [("gate", 2 * it[1]), ("gate", 2 * it[1] + 1)]
    if k == "wo":
        return [("out", it[1])]
    if k == "fg":
        return [("gu", it[1])]
    if k == "fu":
        return [("gu", FT + it[1])]
    return []


SPECTRA = [(0, 0), (0, 1), (1, 0), (1, 1), (2, 0)]


def item_jobs(it):
    k = it[0]
    if k == "Fs":
        return [((k, *it[1:], c, x), 1) for c in range(3) for x in range(2)]
    if k in ("FK", "W"):
        return [((k, *it[1:], c, x), 1) for c, x in SPECTRA]
    if k == "T":
        return [(("T", *it[1:], c), 1) for c in range(3)]
    if k == "I":
        return [(("I", *it[1:], i), 1) for i in range(HALF)]
    if k == "G":
        return [(("G", 4 * it[1] + n, d, g), 1) for n in range(HALF) for d in range(2) for g in range(2)]
    if k in ("rq", "rk", "rv", "rg", "RP"):
        return [(it, 2)]
    if k == "RS":
        return [((k, it[1], c), 1) for c in range(3)]
    if k == "RT":
        return [((k, it[1], c), 1) for c in range(2)]
    if k in ("u", "La", "Lb", "Lc", "Lt", "Ld", "Le", "Lf", "Lg", "Lh", "LX", "RQ", "RN", "qlo", "klo", "ms", "nq", "nf", "c8",
             "H"):
        return []
    return [(it, 1)]


class Plan:

    def __init__(self):
        self.items = schedule()
        self.slabs, self.first_slab = [], {}
        self.bank, self.nth = {}, {}
        self.jobs = []
        self.before = {}
        self.order = {}
        used, owner, at = [0] * BANKS, [None] * BANKS, 0
        slab_job, self.pairs = [], 0
        for it in self.items:
            self.first_slab[it] = len(self.slabs) - (not item_jobs(it) and len(self.slabs) > 0)
            self.order.setdefault(it[0], []).append(it)
            mine = item_slabs(it)
            self.slabs += mine
            for job, n in item_jobs(it):
                if at + n > BANKS:
                    at = 0
                self.bank[job] = at
                self.before[job] = [owner[b] for b in range(at, at + n) if owner[b] is not None]
                for b in range(at, at + n):
                    owner[b] = job
                used[at + n - 1] += 1
                self.nth[job] = (at + n - 1, used[at + n - 1])
                self.jobs.append(job)
                if job[0] != it[0] or job != it:
                    self.order.setdefault(("job", job[0]), []).append(job)
                at = (at + n) % BANKS
            if it[0] == "G":
                g = [j for j, _ in item_jobs(it)]
                slab_job += [g[7], g[15]]
            elif len(mine) == 2:
                self.pairs = self.pairs + 1
                slab_job += [self.pairs, it]
            elif mine:
                slab_job += [it]
        self.first_down = len(self.slabs)
        self.slabs += [("down", n) for n in range(FT)]
        self.slab_job = slab_job

    def place(self, it):
        return self.order[it[0]].index(it) + 1

    def jplace(self, job):
        return self.order[("job", job[0])].index(job) + 1


def place(n):
    return n if n < GAP else n + PAD


PLAN = Plan()
N_SLAB = len(PLAN.slabs)
PAD = -N_SLAB % (RAW * SPL)
GAP = PLAN.first_slab[("dn", 0)] + 8
SPLITS = range(SPL, N_SLAB + SPL)
BY_VECTOR = [m for f in range(2) for m in range(PLAN.first_slab[("G", f)] + SPL, PLAN.first_slab[("Lt", f)] + SPL)]
TOGETHER = {("hy", 16): [("hy", 17), ("hy", 18)],
            ("fg", 0): [("fu", 0), ("fg", 1)]}
U = KC * T * 4


class Signals:

    def __init__(self, sem):
        self.mlp_arg = sem("mlp_arg")
        self.mlp_sin = sem("mlp_sin")
        self.hdn = sem("hdn")
        self.sd_win = sem("sd_win")
        self.sd_hi = sem("sd_hi")
        self.sd_lo = sem("sd_lo")
        self.kf_done = sem("kf_done")
        self.zt_hi = sem("zt_hi")
        self.zt_lo = sem("zt_lo")
        self.z_prod = sem("z_prod")
        self.pq = sem("pq")
        self.pq_hi = sem("pq_hi")
        self.pq_lo = sem("pq_lo")
        self.inv_read = sem("inv_read")
        self.z_done = sem("z_done")
        self.z_tail = sem("z_tail")
        self.b_hi = sem("b_hi")
        self.b_lo = sem("b_lo")
        self.sq_done = sem("sq_done")
        self.sq_sum = sem("sq_sum")
        self.ms_sum = sem("ms_sum")
        self.ms_rec = sem("ms_rec")
        self.rstd_done = sem("rstd_done")
        self.u_f32 = sem("u_f32")
        self.u_hi = sem("u_hi")
        self.u_lo = sem("u_lo")
        self.hy_tap = sem("hy_tap")
        self.hy_done = sem("hy_done")
        self.lx_tap = sem("lx_tap")
        self.lx_done = sem("lx_done")
        self.lg_done = sem("lg_done")
        self.lx_hi = sem("lx_hi")
        self.lx_lo = sem("lx_lo")
        self.gate_done = sem("gate_done")
        self.lru_tanh = sem("lru_tanh")
        self.lru_ab = sem("lru_ab")
        self.lru_ix = sem("lru_ix")
        self.lru_a2 = sem("lru_a2")
        self.lru_b1 = sem("lru_b1")
        self.lru_th = sem("lru_th")
        self.lru_sq = sem("lru_sq")
        self.lru_b = sem("lru_b")
        self.lru_scan = sem("lru_scan")
        self.lru_sum = sem("lru_sum")
        self.lru_y = sem("lru_y")
        self.l_hi = sem("l_hi")
        self.l_lo = sem("l_lo")
        self.mg_done = sem("mg_done")
        self.mp_done = sem("mp_done")
        self.rv_done = sem("rv_done")
        self.rope_ab = sem("rope_ab")
        self.rope_f = sem("rope_f")
        self.rope_hi = sem("rope_hi")
        self.rope_lo = sem("rope_lo")
        self.rg_done = sem("rg_done")
        self.vt_hi = sem("vt_hi")
        self.vt_lo = sem("vt_lo")
        self.sc_read = sem("sc_read")
        self.sc_hi = sem("sc_hi")
        self.sc_lo = sem("sc_lo")
        self.y_done = sem("y_done")
        self.mean_done = sem("mean_done")
        self.rsq_done = sem("rsq_done")
        self.rsq_sum = sem("rsq_sum")
        self.y_sum = sem("y_sum")
        self.var_in = sem("var_in")
        self.var_rec = sem("var_rec")
        self.rstd_r = sem("rstd_r")
        self.yb_done = sem("yb_done")
        self.m_hi = sem("m_hi")
        self.m_lo = sem("m_lo")
        self.wo_done = sem("wo_done")
        self.fg_done = sem("fg_done")
        self.hid_f32 = sem("hid_f32")
        self.hid_hi = sem("hid_hi")
        self.hid_lo = sem("hid_lo")
        self.dn_done = sem("dn_done")
        self.lam_exp = sem("lam_exp")
        self.c8_done = sem("c8_done")
        self.pair_slab = sem("pair_slab")
        self.par_next = sem("par_next")
        self.win_next = sem("win_next")


def build(nc, h0, slabs, params, filt, wout, fin_g, cfwd, cinv, cfwd_s, cinv_s, rope, decay, window, zfeat, ident_in, out):
    plan = PLAN
    sems = []

    with ExitStack() as ctx:
        def sem(name):
            s = ctx.enter_context(nc.semaphore(name))
            sems.append(s)
            return s

        top = [(nc.sbuf_base + 31) // 32 * 32]

        def at(name, shape, offset, dt=F32):
            size = 4 * int(np.prod(shape[1:]))
            assert offset + size <= nc.sbuf_usable_end, (name, offset, size)
            return nc.alloc_sbuf_tensor_at(name, shape, dt, offset=offset)

        def sb(name, shape, dt=F32):
            t = at(name, shape, top[0], dt)
            top[0] += (4 * int(np.prod(shape[1:])) + 31) // 32 * 32
            return t

        h = sb("h", [P, KC, T])
        uh = sb("uh", [P, KC, T], F32R)
        ul = sb("ul", [P, KC, T], F32R)
        wl = sb("wl", [P, RAW, KC * P], F32R)
        raw = at("raw", [P, RAW, KC * P], top[0] - 4 * RAW * KC * P)
        wh = sb("wh", [P, SPL, KC * P], F32R)
        warm = sb("warm", [P, 1])[:]
        fwd_h = sb("fwd_h", [P, 2, FW], F32R)
        fwd_l = sb("fwd_l", [P, 2, FW], F32R)
        fwd_s = sb("fwd_s", [3 * TAIL, FW], F32R)
        inv_h = sb("inv_h", [P, 2, 2, T], F32R)
        inv_l = sb("inv_l", [P, 2, 2, T], F32R)
        inv_s = sb("inv_s", [P, T], F32R)
        inv_sl = sb("inv_sl", [P // 2, T], F32R)
        cs = sb("cs", [P, 2, T])
        ones = sb("ones", [P, P])
        ident = sb("ident", [P, P])
        zf = sb("zf", [EMB, T])
        par = sb("par", [P, N_PAR])
        fil = sb("fil", [P, N_FIL])
        c8 = sb("c8", [P, 2, 2 * KC])
        hdn_s = sb("hdn_s", [P, T])
        hdn_d = sb("hdn_d", [P, T])
        rstd = sb("rstd", [P, T])
        ms = sb("ms", [P, T])
        finp = sb("finp", [P, KC])
        U0 = top[0]
        utmp = at("utmp", [P, KC, T], U0)
        tmp_b = at("tmp_b", [P, 4, NF], U0)
        A0 = U0 + U

        oA, oB, oC, oD, oG, oX, oL, oE = (A0 + x for x in (0, U, 2 * U, 3 * U, 3 * U + 12288, 3 * U + 24576,
                                                           4 * U + 24576, 5 * U + 24576))
        oT = oE + 24576
        x1 = at("x1", [P, KC, T], oA)
        x2 = at("x2", [P, KC, T], oB)
        z = at("z", [P, KC, T], oC)
        zt_h = at("zt_h", [P, 2, NF], oD, F32R)
        zt_l = at("zt_l", [P, 2, NF], oD + 4096, F32R)
        zt_s = at("zt_s", [3 * TAIL, NF], oD + 8192, F32R)
        hdn_t = at("hdn_t", [P, 2, 3, TAIL], oD + 10240)
        lsp = at("lsp", [P, 5, 2 * KC], oD + 11008)
        kf = at("kf", [P, 2, 2, NF], oG)
        kf_r = at("kf_r", [P, NF], oG + 8192)
        sp_h = at("sp_h", [P, 2, 2, NF], oE, F32R)
        sp_l = at("sp_l", [P, 2, 2, NF], oE + 8192, F32R)
        sd_s = at("sd_s", [3 * TAIL, 2, NF], oE + 16384, F32R)
        sp_s = at("sp_s", [P, NF], oE + 16384, F32R)
        rem = at("rem", [P, NF], oE + 20480)
        z_t = at("z_t", [P, HALF, 3, TAIL], oE + 22528)
        tmp_a = at("tmp_a", [P, 4, NF], oT)
        win = at("win", [P, 3, NF], oL)
        wo_t = at("wo_t", [P, NF], oL + 6144)
        marg = at("marg", [P, 3, T], oT)
        mact = at("mact", [P, 2, T], oT + 3264)
        bh = at("bh", [P, KC, T], oA, F32R)
        bl = at("bl", [P, KC, T], oB, F32R)
        xc = at("xc", [P, KC, T], oX)
        gl = at("gl", [P, KC, T], oL)
        lh = at("lh", [P, KC, T], oE, F32R)
        ll = at("ll", [P, KC, T], oE + U, F32R)
        lth = at("lth", [P, 2, HALF, T], oC)
        lr = at("lr", [P, 2, HALF, T], oD)
        li = at("li", [P, 2, HALF, T], oG)
        la2 = at("la2", [P, 2, HALF, T], U0)
        merged = at("merged", [P, KC, T], oT)
        sg = at("sg", [P, SG, T], oE + 2 * U)
        dec = at("dec", [CM, 3, HEADS, T], oC)
        o = oC + 3 * HEADS * T * 4
        qk_h = at("qk_h", [P, 2, 2, T], o, F32R)
        qk_l = at("qk_l", [P, 2, 2, T], o + 4352, F32R)
        rv = at("rv", [P, 2, T], o + 8704)
        vt_h = at("vt_h", [CM, 3, 256], o + 10880, F32R)
        vt_l = at("vt_l", [CM, 3, 256], o + 13952, F32R)
        rot = [[at(f"rot_{x}{y}", [P, 2, T], base + 2176 * "cs".index(y)) for y in "cs"]
               for x, base in (("q", o + 17024), ("k", U0))]
        sc = at("sc", [CM, 2, T], o + 21376)
        sc_h = at("sc_h", [CM, 3, T], o + 23552, F32R)
        sc_l = at("sc_l", [CM, 3, T], o + 26816, F32R)
        ry = at("ry", [P, 2, T], o + 30080)
        rsq = at("rsq", [P, 2, T], o + 32256)
        gs = at("gs", [P, 2, T], o + 34432)
        ysum = at("ysum", [P, T], U0 + 4352)
        hh = at("hh", [P, FT, T], oA, F32R)
        hl = at("hl", [P, FT, T], oA + FT * T * 4, F32R)
        raw_fwd, raw_inv = at("raw_fwd", [P, 2, FW], oA), at("raw_inv", [P, 2, 2, T], oA + 8 * FW)
        raw_fs, raw_is = at("raw_fs", [3 * TAIL, FW], oA + 32768), at("raw_is", [P, T], oA + 32768 + 4 * FW)

        ps = ctx.enter_context(nc.psum_tensor("ps", [P, BANKS + 1, 512], F32))

        full = [sem(f"bank_full{b}") for b in range(BANKS)]
        raw_in = [sem(f"raw_in{r}") for r in range(RAW)]
        slab_hi, slab_hi_v, slab_lo, down_slab = sem("slab_hi"), sem("slab_hi_v"), sem("slab_lo"), sem("down_slab")
        win_in, dec_in = sem("win_in"), sem("dec_in")
        dve_step, act_step = sem("dve_step"), sem("act_step")
        S = Signals(sem)

        def made(job):
            b, n = plan.nth[job]
            return full[b], n

        def freed(job):
            k = job[0]
            jp = plan.jplace if ("job", k) in plan.order else None
            if k == "M":
                return S.mlp_arg, job[1] + 1
            if k in ("Fs", "FK", "T", "I", "G", "RS"):
                return {"Fs": S.sd_win, "FK": S.kf_done, "T": S.zt_lo, "I": S.inv_read, "G": S.gate_done,
                        "RS": S.sc_read}[k], jp(job)
            if k == "RT":
                return S.vt_lo, 3 * job[1] + 2 + job[2]
            if k == "W":
                return S.z_prod, 3 * ((jp(job) - 1) // 5) + job[4 - 1] + 1
            if k in ("rq", "rk"):
                return S.rope_ab, rope_place(job)
            return {"hy": S.hy_done, "lx": S.lx_done, "lg": S.lg_done, "mg": S.mg_done, "mp": S.mp_done,
                    "rv": S.rv_done, "rg": S.rg_done, "RP": S.y_done, "RM": S.mean_done, "RV": S.var_in,
                    "wo": S.wo_done, "fg": S.fg_done, "fu": S.hid_f32, "dn": S.dn_done}[k], plan.place(job)

        def rope_place(it):
            return [i for i in plan.items if i[0] in ("rq", "rk")].index(it) + 1

        def slab_used(n):
            if n < plan.first_down:
                job = plan.slab_job[n]
                return (S.pair_slab, job) if isinstance(job, int) else made(job)
            m = n - plan.first_down + 1
            if (8 * m) % FT == 0:
                return made(("dn", 8 * m // FT - 1))
            return down_slab, m - m // 11

        def last_in_slot(n, slots):
            m = place(n) - slots
            while GAP <= m < GAP + PAD:
                m -= slots
            return None if m < 0 else m if m < GAP else m - PAD

        def raw_slot(n):
            return place(n) % RAW

        def hi_slot(n):
            return place(n) % SPL

        def hy_dst(j):
            return (x1, x2, z)[j // KC][:, j % KC]

        def bank(job, m=P, n=T):
            return ps[0:m, plan.bank[job], 0:n]

        def values(it, c):
            at_ = c % 2 * 256
            return ps[0:CHUNKS[c][1], plan.bank[(*it, c // 2)], at_:at_ + 256]

        def pair(job):
            b = plan.bank[job]
            return ps[:, b:b + 2, 0:T]

        def load_params(eng, layer):
            return eng.dma_start(par[:], params[bass.ds(layer, 1)].rearrange("a p n -> p (a n)"))

        def load_fil(eng, layer):
            return eng.dma_start(fil[:], filt[bass.ds(layer, 1)].rearrange("a p n -> p (a n)"))

        def load_window(eng, f):
            return eng.dma_start(win[:], window[:, :, f * NF:(f + 1) * NF])

        def load_wout(eng, k):
            return eng.dma_start(wo_t[:], wout[bass.ds(k, 1)].rearrange("a p n -> p (a n)"))

        TWO_PI = 2 * np.pi
        PI_A = 6.28125
        PI_B = float(np.float32(TWO_PI - PI_A))
        PI_C = float(TWO_PI - PI_A - PI_B)
        PI_LE = 3.1415925
        MAGIC = 1.5 * 2.0 ** 23

        def mlp_argument(i, src, link):
            m = HID if i < 2 else P
            a, b, t = marg[0:m, 0], marg[0:m, 1], marg[0:m, 2]
            col = (C_B1, C_B2, C_B3)[i]
            link(nc.vector.tensor_scalar(t, src, fil[0:m, col:col + 1], fil[0:m, C_FR:C_FR + 1], ALU.add, ALU.mult))
            link(nc.vector.tensor_scalar(b, t, 1 / TWO_PI, MAGIC, ALU.mult, ALU.add))
            link(nc.vector.tensor_scalar(b, b, MAGIC, None, ALU.subtract))
            for p_ in (PI_A, PI_B, PI_C):
                link(nc.vector.scalar_tensor_tensor(out=t, in0=b, scalar=-p_, in1=t, op0=ALU.mult, op1=ALU.add))
            return nc.vector.tensor_scalar(a, t, PI_LE, -PI_LE, ALU.min, ALU.max)

        def mlp_sine(i):
            dst = (mact[0:HID, 0], mact[0:HID, 1], hdn_s[:])[i]
            return nc.scalar.activation(dst, marg[0:HID, 0] if i < 2 else marg[:, 0], ACT.Sin)

        def mlp_product(i, dst):
            w = (fil[0:EMB, C_W1:C_W1 + HID], fil[0:HID, C_W2:C_W2 + HID], fil[0:HID, C_W3:C_W3 + P])[i]
            return nc.tensor.matmul(dst[0:HID if i < 2 else P, 0:T], w, mact[0:HID, i - 1] if i else zf[:],
                                    start=True, stop=True)

        def features(link):
            link(nc.vector.memset(hdn_s[HID:P, 0:1], 0.0))
            return nc.vector.tensor_scalar(hdn_d[:], hdn_s[:], fil[:, C_SGN:C_SGN + 1], None, ALU.mult)

        c_h, c_net, c_rest = sem("c_h"), sem("c_net"), sem("c_rest")
        c_slab, c_mat = [sem(f"c_slab{n}") for n in range(SPL)], [sem(f"c_mat{n}") for n in range(4)]
        c_ones, c_sq, c_ms, c_rec, c_rstd = sem("c_ones"), sem("c_sq"), sem("c_ms"), sem("c_rec"), sem("c_rstd")
        c_mlp, c_arg, c_sin, c_feat, c_step = sem("c_mlp"), sem("c_arg"), sem("c_sin"), sem("c_feat"), sem("c_step")
        c_wh, c_wl, c_hi, c_lo, c_lo_p = sem("c_wh"), sem("c_wl"), sem("c_hi"), sem("c_lo"), sem("c_lo_p")
        with nc.Block() as block:
            @block.sync
            def _(sp):
                sp.dma_start(zf[:], zfeat).then_inc(c_net, 16)
                load_fil(sp, 0).then_inc(c_net, 16)
                sp.dma_start(h[:, 0:4], h0[:, 0:4]).then_inc(c_h, 16)
                sp.dma_start(h[:, 4:8], h0[:, 4:8]).then_inc(c_h, 16)
                for n in range(SPL):
                    sp.dma_start(raw[:, n], slabs[n]).then_inc(c_slab[n], 16)
                sp.dma_start(raw_fwd[:], cfwd).then_inc(c_mat[0], 16)
                sp.dma_start(raw_inv[:], cinv).then_inc(c_mat[1], 16)
                sp.dma_start(raw_fs[:], cfwd_s).then_inc(c_mat[2], 16)
                sp.dma_start(raw_is[:], cinv_s).then_inc(c_mat[3], 16)
                load_params(sp, 0).then_inc(c_rest, 16)
                load_window(sp, 0).then_inc(c_rest, 16)
                load_wout(sp, 0).then_inc(c_rest, 16)
                sp.dma_start(cs[:], rope).then_inc(c_rest, 16)
                sp.dma_start(ident[:], ident_in).then_inc(c_rest, 16)
                sp.dma_start(finp[:], fin_g).then_inc(c_rest, 16)
                sp.wait_ge(c_rest, 16 * 6)

            @block.scalar
            def _(act):
                def slab_hi_part(n):
                    act.wait_ge(c_slab[n], 16)
                    nc.scalar.activation(wh[:, n], raw[:, n], ACT.Copy).then_inc(c_wh, 1)

                def sine(i):
                    act.wait_ge(c_arg, i + 1)
                    mlp_sine(i).then_inc(c_sin, 1)

                sine(0)
                act.wait_ge(c_h, 32)
                for j in range(KC):
                    nc.scalar.activation(utmp[:, j], h[:, j], ACT.Square).then_inc(c_sq, 1)
                sine(1)
                for n in range(SPL):
                    slab_hi_part(n)
                sine(2)
                for n, (hi, src) in enumerate(((fwd_h, raw_fwd), (inv_h, raw_inv), (fwd_s, raw_fs), (inv_s, raw_is))):
                    act.wait_ge(c_mat[n], 16)
                    nc.scalar.activation(hi[:], src[:], ACT.Copy).then_inc(c_hi, 1)
                act.wait_ge(c_rec, 1)
                nc.scalar.activation(rstd[:], ms[:], ACT.Sqrt).then_inc(c_rstd, 1)
                act.wait_ge(c_rstd, 1)
                act.wait_ge(c_hi, 4)

            @block.tensor
            def _(pe):
                pe.wait_ge(c_net, 32)
                mlp_product(0, ps[:, 0]).then_inc(c_mlp, 1)
                pe.wait_ge(c_sin, 1)
                mlp_product(1, ps[:, 1]).then_inc(c_mlp, 1)
                pe.wait_ge(c_ones, 1)
                for j in range(KC):
                    pe.wait_ge(c_sq, j + 1)
                    ins = nc.tensor.matmul(ps[:, BANKS, 0:T], ones[:], utmp[:, j], start=(j == 0), stop=(j == KC - 1))
                ins.then_inc(c_ms, 1)
                pe.wait_ge(c_sin, 2)
                mlp_product(2, ps[:, 2]).then_inc(c_mlp, 1)

            @block.vector
            def _(dve):
                steps = [0]

                def link(ins):
                    steps[0] += 1
                    ins.then_inc(c_step, 1)
                    dve.wait_ge(c_step, steps[0])

                nc.vector.memset(ones[:], 1.0).then_inc(c_ones, 1)
                def argument(i):
                    dve.wait_ge(c_mlp, i + 1)
                    mlp_argument(i, ps[0:HID if i < 2 else P, i, 0:T], link).then_inc(c_arg, 1)

                def slab_lo_part(n):
                    dve.wait_ge(c_wh, n + 1)
                    nc.vector.tensor_tensor(wl[:, n], raw[:, n], wh[:, n].bitcast(F32), ALU.subtract).then_inc(c_wl, 1)

                argument(0)
                argument(1)
                slab_lo_part(0)
                dve.wait_ge(c_ms, 1)
                link(nc.vector.tensor_scalar(ms[:], ps[:, BANKS, 0:T], 1.0 / D_MODEL, EPS, ALU.mult, ALU.add))
                argument(2)
                nc.vector.reciprocal(ms[:], ms[:]).then_inc(c_rec, 1)
                dve.wait_ge(c_sin, 3)
                features(link).then_inc(c_feat, 1)
                for n in range(1, SPL):
                    slab_lo_part(n)
                dve.wait_ge(c_hi, 1)
                nc.vector.tensor_tensor(fwd_l[:], raw_fwd[:], fwd_h[:].bitcast(F32), ALU.subtract).then_inc(c_lo, 1)
                dve.wait_ge(c_hi, 3)
                mid = slice(TAIL, 2 * TAIL)
                nc.vector.tensor_tensor(fwd_s[mid], raw_fs[mid], fwd_s[mid].bitcast(F32), ALU.subtract).then_inc(c_lo, 1)
                dve.wait_ge(c_hi, 4)
                nc.vector.tensor_tensor(inv_sl[:], raw_is[0:P // 2], inv_s[0:P // 2].bitcast(F32),
                                        ALU.subtract).then_inc(c_lo, 1)
                dve.wait_ge(c_feat, 1)
                dve.wait_ge(c_wl, SPL)
                dve.wait_ge(c_lo, 3)

            @block.gpsimd
            def _(pool):
                pool.wait_ge(c_hi, 2)
                nc.gpsimd.tensor_tensor(inv_l[:], raw_inv[:], inv_h[:].bitcast(F32), ALU.subtract).then_inc(c_lo_p, 1)
                pool.wait_ge(c_lo_p, 1)

        def layer_body(layer, block):
            @block.sync
            def _(sp):
                for n in SPLITS:
                    if last_in_slot(n, RAW) is not None:
                        sp.wait_ge(*slab_used(last_in_slot(n, RAW)))
                    sp.dma_start(raw[:, raw_slot(n)], slabs[bass.ds(layer * N_SLAB + n, 1)].rearrange("a p n -> p (a n)")) \
                        .then_inc(raw_in[raw_slot(n)], 16)
                    if n == plan.first_slab[("fg", 8)]:
                        sp.wait_ge(S.u_f32, 2 * KC)
                        load_params(sp, layer + 1).then_inc(S.par_next, 16)
                        load_fil(sp, layer + 1).then_inc(S.par_next, 16)
                sp.wait_ge(S.par_next, 32)

            @block.gpsimd
            def _(pool):
                n = 0
                for it in plan.items:
                    if it[0] == "W":
                        for c in range(2):
                            t = (tmp_a, tmp_b)[c]
                            pool.wait_ge(S.z_prod, 3 * n + c + 1)
                            nc.gpsimd.tensor_tensor(t[:, 0], t[:, 0], t[:, 1], ALU.subtract).then_inc(S.pq, 1)
                            nc.gpsimd.tensor_tensor(t[:, 2], t[:, 2], t[:, 3], ALU.add).then_inc(S.pq, 1)
                        n += 1
                    if it[0] == "La":
                        f = it[1]
                        pool.wait_ge(S.gate_done, 16 * (f + 1))
                        for d in range(2):
                            nc.gpsimd.tensor_tensor(li[:, d], li[:, d], xc[:, 4 * f:4 * f + 4], ALU.mult).then_inc(S.lru_ix, 1)
                    if it[0] == "nq" and 0 < it[2] < KC - 1:
                        m, j = it[1:]
                        pool.wait_ge(S.sq_done, KC * m + j + 1)
                        if j > 1:
                            pool.wait_ge(S.sq_sum, (KC - 2) * m + j - 1)
                        nc.gpsimd.tensor_tensor(utmp[:, j], utmp[:, j - 1], utmp[:, j], ALU.add).then_inc(S.sq_sum, 1)
                    if it[0] == "RP":
                        pool.wait_ge(S.y_done, it[1] + 1)
                        if it[1]:
                            pool.wait_ge(*made(("RM", it[1] - 1)))
                        nc.gpsimd.tensor_tensor(ysum[:], ry[:, 0], ry[:, 1], ALU.add).then_inc(S.y_sum, 1)
                    if it[0] == "RM":
                        pool.wait_ge(S.rsq_done, it[1] + 1)
                        nc.gpsimd.tensor_tensor(rsq[:, 0], rsq[:, 0], rsq[:, 1], ALU.add).then_inc(S.rsq_sum, 1)
                    if it[0] == "Lc":
                        pool.wait_ge(S.lru_ab, 8 * (it[1] + 1))
                        for d in range(2):
                            nc.gpsimd.tensor_tensor(la2[:, d], lr[:, d], lr[:, d], ALU.mult).then_inc(S.lru_a2, 1)
                    if it[0] == "Le":
                        pool.wait_ge(S.lru_sq, 2 * (it[1] + 1))
                        nc.gpsimd.tensor_tensor(li[:, 1], li[:, 1], lth[:, 1], ALU.mult).then_inc(S.lru_b1, 1)
                    if it[0] == "Lg":
                        f = it[1]
                        pool.wait_ge(S.lru_sum, f + 1)
                        nc.gpsimd.tensor_tensor(lth[:, 0], lth[:, 0], gl[:, 4 * f:4 * f + 4], ALU.mult).then_inc(S.lru_y, 1)
                    if it[0] in ("rq", "rk"):
                        a, b = rot["qk".index(it[0][1])]
                        pool.wait_ge(S.rope_ab, rope_place(it))
                        nc.gpsimd.tensor_tensor(a[:, 0], a[:, 0], b[:, 1], ALU.subtract).then_inc(S.rope_f, 1)
                        nc.gpsimd.tensor_tensor(a[:, 1], a[:, 1], b[:, 0], ALU.add).then_inc(S.rope_f, 1)

            @block.scalar
            def _(act):
                steps = [0]
                splits = [0]

                def link(ins):
                    steps[0] += 1
                    ins.then_inc(act_step, 1)
                    act.wait_ge(act_step, steps[0])

                def split_to(n):
                    while splits[0] < min(n - SPL, len(SPLITS)):
                        m = SPLITS[splits[0]]
                        splits[0] += 1
                        if m in BY_VECTOR:
                            continue
                        act.wait_ge(raw_in[raw_slot(m)], 16 * sum(raw_slot(q) == raw_slot(m) for q in range(SPL, m + 1)))
                        act.wait_ge(*slab_used(last_in_slot(m, SPL)))
                        nc.scalar.activation(wh[:, hi_slot(m)], raw[:, raw_slot(m)], ACT.Copy).then_inc(slab_hi, 1)

                def rnd(dst, src):
                    return nc.scalar.activation(dst, src, ACT.Copy)

                def load_filter(k):
                    act.wait_ge(S.sd_win, 6 * k)
                    act.wait_ge(*made(("Fs", (k - 1) // 2, (k - 1) % 2, 2, 1)))
                    load_window(act, k % 2).then_inc(win_in, 16)
                    load_wout(act, layer * 4 + k).then_inc(win_in, 16)

                c = {}

                def nth(name):
                    c[name] = c.get(name, 0) + 1
                    return c[name]

                for it in plan.items:
                    k = it[0]
                    split_to(plan.first_slab[it] + SPL)
                    if k == "M":
                        act.wait_ge(S.mlp_arg, it[1] + 1)
                        mlp_sine(it[1]).then_inc(S.mlp_sin, 1)
                    if k == "Fs":
                        for n in range(6):
                            cc, x = n // 2, n % 2
                            cn = ROWS[cc]
                            act.wait_ge(S.sd_win, nth("sd"))
                            rnd(sp_h[:, cc, x] if cc < 2 else sd_s[:, x], tmp_a[0:cn, n % 4]).then_inc(S.sd_hi, 1)
                    if k == "FK":
                        for cc, x in SPECTRA:
                            job = ("FK", it[1], it[2], cc, x)
                            act.wait_ge(*made(job))
                            if (cc, x) == (0, 0) and c.get("W"):
                                act.wait_ge(S.z_prod, 3 * c["W"])
                            nc.scalar.copy(kf[:, cc, x] if cc < 2 else kf_r[:], bank(job, P, NF)).then_inc(S.kf_done, 1)
                    if k == "FK" and it[1:] != (1, 1):
                        load_filter(2 * it[1] + it[2] + 1)
                    if k == "c8":
                        lam = par[:, C_LAM:C_LAM + 2 * KC]
                        link(nc.scalar.activation(lsp[:, 0], lam, ACT.Abs))
                        nc.scalar.activation(lsp[:, 1], lsp[:, 0], ACT.Exp, scale=-1.0).then_inc(S.lam_exp, 1)
                    if it == ("fg", 4):
                        load_window(act, 0).then_inc(S.win_next, 16)
                        load_wout(act, (layer + 1) * 4).then_inc(S.win_next, 16)
                    if k == "nf":
                        nc.scalar.activation(warm, ones[:, 0:1], ACT.Sqrt)
                    if it == ("nf", 1):
                        act.wait_ge(S.win_next, 32)
                        split_to(N_SLAB + SPL)
                    if it == ("mp", 1, 0):
                        act.wait_ge(S.l_lo, 2)
                        act.dma_start(dec[:], decay).then_inc(dec_in, 16)
                    if k == "T":
                        for cc in range(3):
                            job = (*it, cc)
                            act.wait_ge(*made(job))
                            rnd(zt_h[:, cc] if cc < 2 else zt_s[:], bank(job, ROWS[cc], NF)).then_inc(S.zt_hi, 1)
                    if k == "W":
                        nth("W")
                        for cc in range(2):
                            for x in range(2):
                                act.wait_ge(S.pq, nth("pq"))
                                rnd(sp_h[:, cc, x], (tmp_a, tmp_b)[cc][:, 2 * x]).then_inc(S.pq_hi, 1)
                        act.wait_ge(S.z_prod, 3 * c["W"])
                        rnd(sp_s[:], rem[:]).then_inc(S.pq_hi, 1)
                    if k == "I" and it[1] == 1:
                        for i in range(HALF):
                            j = HALF * it[2] + i
                            act.wait_ge(S.z_done, 8 + j + 1)
                            rnd(bh[:, j], z[:, j]).then_inc(S.b_hi, 1)
                    if k == "nq":
                        n, j = it[1:]
                        act.wait_ge((S.wo_done, S.dn_done)[n], j + 1)
                        nc.scalar.activation(utmp[:, j], h[:, j], ACT.Square).then_inc(S.sq_done, 1)
                    if k == "nf":
                        act.wait_ge(S.ms_rec, it[1] + 1)
                        nc.scalar.activation(rstd[:], ms[:], ACT.Sqrt).then_inc(S.rstd_done, 1)
                    if k == "u":
                        for j in range(KC):
                            act.wait_ge(S.u_f32, nth("u"))
                            rnd(uh[:, j], utmp[:, j]).then_inc(S.u_hi, 1)
                    if k == "hy":
                        j = it[1]
                        act.wait_ge(*made(it))
                        nc.scalar.activation(hy_dst(j), bank(it), ACT.Identity,
                                                 bias=par[:, C_HB + j:C_HB + j + 1],
                                                 scale=par[:, C_HW + 24 + j:C_HW + 25 + j]).then_inc(S.hy_tap, 1)
                    if k == "lx":
                        j = it[1]
                        act.wait_ge(*made(it))
                        nc.scalar.activation(xc[:, j], bank(it), ACT.Identity,
                                                 bias=par[:, C_LB + j:C_LB + j + 1],
                                                 scale=par[:, C_LW + 16 + j:C_LW + 17 + j]).then_inc(S.lx_tap, 1)
                    if k == "lg":
                        act.wait_ge(*made(it))
                        if it[1] == 0:
                            act.wait_ge(S.sd_win, 24)
                            act.wait_ge(*made(("Fs", 1, 1, 2, 1)))
                        nc.scalar.activation(gl[:, it[1]], bank(it), ACT.Gelu_apprx_tanh).then_inc(S.lg_done, 1)
                    if k == "LX":
                        f = it[1]
                        if f == 0:
                            act.wait_ge(S.lx_done, KC)
                            act.wait_ge(*made(("I", 1, 1, HALF - 1)))
                        rnd(lh[:, 4 * f:4 * f + 4], xc[:, 4 * f:4 * f + 4]).then_inc(S.lx_hi, 1)
                    if k == "G":
                        f = it[1]
                        if f == 1:
                            act.wait_ge(S.lru_scan, 2)
                        else:
                            act.wait_ge(S.b_lo, KC)
                        for n in range(HALF):
                            for d in range(2):
                                for g in range(2):
                                    job = ("G", 4 * f + n, d, g)
                                    col = C_GB + (2 * d + g) * KC + 4 * f + n
                                    act.wait_ge(*made(job))
                                    nc.scalar.activation((lr, li)[g][:, d, n], bank(job), ACT.Sigmoid,
                                                             bias=par[:, col:col + 1]).then_inc(S.gate_done, 1)
                                if n % 2 == 1 and d == 1:
                                    split_to(plan.first_slab[it] + n // 2 + 1 + SPL)
                    if k in ("La", "Lb"):
                        f = it[1]
                        if k == "La":
                            act.wait_ge(S.gate_done, 16 * (f + 1))
                            act.wait_ge(S.c8_done, 2)
                            if f:
                                act.wait_ge(S.l_lo, f)
                        else:
                            act.wait_ge(S.lru_tanh, 8 * (f + 1))
                        for d in range(2):
                            for n in range(HALF):
                                col = d * KC + HALF * f + n
                                if k == "La":
                                    nc.scalar.activation(lth[:, d, n], lr[:, d, n], ACT.Tanh,
                                                             scale=c8[:, 0, col:col + 1]).then_inc(S.lru_tanh, 1)
                                else:
                                    nc.scalar.activation(lr[:, d, n], lr[:, d, n], ACT.Exp,
                                                             scale=c8[:, 1, col:col + 1]).then_inc(S.lru_ab, 1)
                    if k == "Ld":
                        for d in range(2):
                            act.wait_ge(S.lru_th, 2 * it[1] + d + 1)
                            nc.scalar.activation(lth[:, d], lth[:, d], ACT.Sqrt).then_inc(S.lru_sq, 1)
                    if k == "Lh":
                        f = it[1]
                        act.wait_ge(S.lru_y, f + 1)
                        rnd(lh[:, 4 * f:4 * f + 4], lth[:, 0]).then_inc(S.l_hi, 1)
                    if k == "mg":
                        s = (plan.place(it) - 1) % SG
                        act.wait_ge(*made(it))
                        if plan.place(it) == 1:
                            act.wait_ge(*made(("I", 1, 1, HALF - 1)))
                        if plan.place(it) > SG:
                            act.wait_ge(S.mp_done, plan.place(it) - SG)
                        nc.scalar.activation(sg[:, s], bank(it), ACT.Sigmoid).then_inc(S.mg_done, 1)
                    if k == "rv":
                        split_to(plan.first_slab[it] + 1 + SPL)
                        act.wait_ge(*made(it))
                        if it[1] == 0:
                            act.wait_ge(S.l_lo, 2)
                        nc.scalar.copy(rv[:], pair(it)).then_inc(S.rv_done, 1)
                    if k in ("rq", "rk"):
                        split_to(plan.first_slab[it] + 1 + SPL)
                    if k in ("qlo", "klo"):
                        x = "qk".index(k[0])
                        act.wait_ge(S.rope_f, 2 * (2 * it[1] + x + 1))
                        if it[1]:
                            act.wait_ge(*made(("RS", it[1] - 1, 2)))
                        rnd(qk_h[:, x], rot[x][0][:]).then_inc(S.rope_hi, 1)
                    if k == "rg":
                        split_to(plan.first_slab[it] + 1 + SPL)
                        act.wait_ge(*made(it))
                        if it[1]:
                            act.wait_ge(S.yb_done, it[1])
                        nc.scalar.activation(gs[:], pair(it), ACT.Silu).then_inc(S.rg_done, 1)
                    if k == "RT":
                        for cc, (_, cn) in enumerate(CHUNKS):
                            act.wait_ge(*made((*it, cc // 2)))
                            rnd(vt_h[0:cn, cc], values(it, cc)).then_inc(S.vt_hi, 1)
                    if k == "RS":
                        for cc, (_, cn) in enumerate(CHUNKS):
                            act.wait_ge(S.sc_read, nth("sc"))
                            rnd(sc_h[0:cn, cc], sc[0:cn, c["sc"] % 2]).then_inc(S.sc_hi, 1)
                    if k == "RP":
                        act.wait_ge(*made(it))
                        if it[1]:
                            act.wait_ge(S.b_lo, KC + it[1])
                        nc.scalar.copy(ry[:], pair(it)).then_inc(S.y_done, 1)
                    if k == "RM":
                        nc.scalar.activation(warm, ones[:, 0:1], ACT.Sqrt)
                        act.wait_ge(S.mean_done, it[1] + 1)
                        nc.scalar.activation(rsq[:], ry[:], ACT.Square).then_inc(S.rsq_done, 1)
                    if k == "RQ":
                        act.wait_ge(S.var_rec, it[1] + 1)
                        nc.scalar.activation(rstd[:], ms[:], ACT.Sqrt).then_inc(S.rstd_r, 1)
                    if k == "RN":
                        act.wait_ge(S.yb_done, it[1] + 1)
                        rnd(bh[:, 2 * it[1]:2 * it[1] + 2], ry[:]).then_inc(S.b_hi, 1)
                    if k == "ms":
                        f = it[1]
                        act.wait_ge(S.mp_done, 16 + 2 * f + 2)
                        if f == 0:
                            act.wait_ge(*made(("mp", 1, 7)))
                        rnd(lh[:, 2 * f:2 * f + 2], merged[:, 2 * f:2 * f + 2]).then_inc(S.m_hi, 1)
                    if k == "fg":
                        i = it[1]
                        act.wait_ge(*made(it))
                        if i >= SG:
                            act.wait_ge(S.hid_lo, i - SG + 1)
                        nc.scalar.activation(sg[:, i % SG], bank(it), ACT.Silu).then_inc(S.fg_done, 1)
                    if k == "fu":
                        i = it[1]
                        act.wait_ge(S.hid_f32, i + 1)
                        rnd(hh[:, i], sg[:, i % SG]).then_inc(S.hid_hi, 1)
                    if k == "dn":
                        for m in range(it[1] * FT // KC, (it[1] + 1) * FT // KC):
                            split_to(plan.first_down + m + SPL)

            @block.vector
            def _(dve):
                steps = [0]
                splits = [0]

                def link(ins):
                    steps[0] += 1
                    ins.then_inc(dve_step, 1)
                    dve.wait_ge(dve_step, steps[0])

                def split_to(n):
                    while splits[0] < min(n - SPL, len(SPLITS)):
                        m = SPLITS[splits[0]]
                        rounded = [q for q in BY_VECTOR if q <= m]
                        if m in rounded:
                            dve.wait_ge(raw_in[raw_slot(m)], 16 * sum(raw_slot(q) == raw_slot(m) for q in range(SPL, m + 1)))
                            dve.wait_ge(*slab_used(last_in_slot(m, SPL)))
                            nc.vector.tensor_copy(wh[:, hi_slot(m)], raw[:, raw_slot(m)]).then_inc(slab_hi_v, 1)
                            dve.wait_ge(slab_hi_v, len(rounded))
                        else:
                            dve.wait_ge(slab_hi, splits[0] + 1 - len(rounded))
                        nc.vector.tensor_tensor(wl[:, raw_slot(m)], raw[:, raw_slot(m)], wh[:, hi_slot(m)].bitcast(F32),
                                                ALU.subtract).then_inc(slab_lo, 1)
                        splits[0] += 1

                def rest(dst, src, hi):
                    return nc.vector.tensor_tensor(dst, src, hi.bitcast(F32), ALU.subtract)

                c = {}

                def nth(name):
                    c[name] = c.get(name, 0) + 1
                    return c[name]

                last3 = slice(2 * TAIL, 3 * TAIL)
                for it in plan.items:
                    k = it[0]
                    if k not in ("RS", "RT"):
                        split_to(plan.first_slab[it] + SPL)
                    if k == "c8":
                        dve.wait_ge(S.lam_exp, 1)
                        e, s, s2, r = lsp[:, 1], lsp[:, 2], lsp[:, 3], lsp[:, 4]
                        link(nc.vector.tensor_scalar(s2, e, 2.0, None, ALU.add))
                        link(nc.vector.reciprocal(s, s2))
                        link(nc.vector.tensor_tensor(s, e, s, ALU.mult))
                        link(nc.vector.tensor_tensor(s2, s, s, ALU.mult))
                        link(nc.vector.tensor_scalar(r, s2, 1.0 / 15, None, ALU.mult))
                        for q in (13, 11, 9, 7, 5, 3):
                            link(nc.vector.scalar_tensor_tensor(out=r, in0=r, scalar=1.0 / q, in1=s2, op0=ALU.add, op1=ALU.mult))
                        link(nc.vector.scalar_tensor_tensor(out=r, in0=r, scalar=1.0, in1=s, op0=ALU.add, op1=ALU.mult))
                        link(nc.vector.tensor_scalar(s, par[:, C_LAM:C_LAM + 2 * KC], -1.0, 0.0, ALU.mult, ALU.max))
                        link(nc.vector.scalar_tensor_tensor(out=s, in0=r, scalar=2.0, in1=s, op0=ALU.mult, op1=ALU.add))
                        nc.vector.tensor_scalar(c8[:, 0], s, 8.0, None, ALU.mult).then_inc(S.c8_done, 1)
                        nc.vector.tensor_scalar(c8[:, 1], s, -8.0, None, ALU.mult).then_inc(S.c8_done, 1)
                    if k == "M":
                        dve.wait_ge(*made(it))
                        mlp_argument(it[1], bank(it, HID if it[1] < 2 else P), link).then_inc(S.mlp_arg, 1)
                    if it == ("dn", 7):
                        dve.wait_ge(S.mlp_sin, 3)
                        link(features(link))
                    if k == "H":
                        for x in range(2):
                            nc.vector.tensor_copy(hdn_t[:, x], (hdn_s, hdn_d)[x][:, None, T - TAIL:T].to_broadcast([P, 3, TAIL])) \
                                .then_inc(S.hdn, 1)
                    if k == "Fs":
                        def lo(n):
                            cc, x = n // 2, n % 2
                            dve.wait_ge(S.sd_hi, nth("sd_hi"))
                            if cc < 2:
                                rest(sp_l[:, cc, x], tmp_a[:, n % 4], sp_h[:, cc, x]).then_inc(S.sd_lo, 1)
                            else:
                                rest(sd_s[last3, x], tmp_a[last3, n % 4], sd_s[last3, x]).then_inc(S.sd_lo, 1)
                        nth("F")
                        if c["F"] > 1:
                            dve.wait_ge(win_in, 32 * (c["F"] - 1))
                        if c.get("pq_hi"):
                            dve.wait_ge(S.pq_lo, c["pq_hi"])
                            dve.wait_ge(S.z_done, 4 * c["F"] - 4)
                        for n in range(6):
                            cc, x = n // 2, n % 2
                            cn = ROWS[cc]
                            job = ("Fs", it[1], it[2], cc, x)
                            dve.wait_ge(*made(job))
                            if n >= 4:
                                dve.wait_ge(S.sd_lo, 6 * c["F"] - 6 + n - 3)
                            nc.vector.tensor_tensor(tmp_a[0:cn, n % 4], bank(job, cn, NF), win[0:cn, cc], ALU.mult).then_inc(S.sd_win, 1)
                            if n:
                                lo(n - 1)
                        lo(5)
                    if k == "T":
                        o, f = it[1:]
                        if o == 0:
                            dve.wait_ge(S.hy_done, plan.place(("hy", 16 + 4 * f + 3)))
                        else:
                            dve.wait_ge(S.z_done, 4 * f + 4)
                        if plan.place(it) > 1:
                            dve.wait_ge(*made((*plan.order["T"][plan.place(it) - 2], 2)))
                        nc.vector.tensor_copy(z_t[:], z[:, HALF * f:HALF * (f + 1), None, T - TAIL:T]
                                              .to_broadcast([P, HALF, 3, TAIL])).then_inc(S.z_tail, 1)
                        for cc in range(3):
                            dve.wait_ge(S.zt_hi, nth("zt"))
                            if cc < 2:
                                rest(zt_l[:, cc], bank((*it, cc), P, NF), zt_h[:, cc]).then_inc(S.zt_lo, 1)
                            else:
                                rest(zt_s[last3], ps[last3, plan.bank[(*it, cc)], 0:NF], zt_s[last3]).then_inc(S.zt_lo, 1)
                    if k == "W":
                        nth("W")

                        def lo(cc):
                            for x in range(2):
                                dve.wait_ge(S.pq_hi, nth("pq_hi"))
                                rest(sp_l[:, cc, x], (tmp_a, tmp_b)[cc][:, 2 * x], sp_h[:, cc, x]).then_inc(S.pq_lo, 1)
                        dve.wait_ge(S.kf_done, 5 * c["W"])
                        dve.wait_ge(S.sd_lo, 6 * c["W"])
                        for cc in range(2):
                            re, im = (*it, cc, 0), (*it, cc, 1)
                            dve.wait_ge(*made(im))
                            dve.wait_ge(*made(re))
                            for a, b, d in ((re, 0, 0), (im, 1, 1), (re, 1, 2), (im, 0, 3)):
                                ins = nc.vector.tensor_tensor((tmp_a, tmp_b)[cc][:, d], bank(a, P, NF), kf[:, cc, b], ALU.mult)
                            ins.then_inc(S.z_prod, 1)
                        lo(0)
                        job = (*it, 2, 0)
                        dve.wait_ge(*made(job))
                        nc.vector.tensor_tensor(rem[:], bank(job, P, NF), kf_r[:], ALU.mult).then_inc(S.z_prod, 1)
                        lo(1)
                        dve.wait_ge(S.pq_hi, nth("pq_hi"))
                        rest(sp_s[P // 2:P], rem[P // 2:P], sp_s[P // 2:P]).then_inc(S.pq_lo, 1)
                    if k == "I":
                        for i in range(HALF):
                            j = HALF * it[2] + i
                            job = (*it, i)
                            dve.wait_ge(*made(job))
                            if it[1] == 0:
                                dve.wait_ge(S.hy_done, plan.place(("hy", 16 + j)))
                                dve.wait_ge(S.hy_done, plan.place(("hy", j)))
                            else:
                                dve.wait_ge(S.hy_done, plan.place(("hy", KC + j)))
                            sk = C_SKIP + it[1] * KC + j
                            nc.vector.scalar_tensor_tensor(out=z[:, j], in0=z[:, j], scalar=par[:, sk:sk + 1],
                                                               in1=bank(job), op0=ALU.mult, op1=ALU.add).then_inc(S.inv_read, 1)
                            dve.wait_ge(S.inv_read, nth("inv"))
                            nc.vector.tensor_tensor(z[:, j], z[:, j], (x1, x2)[it[1]][:, j], ALU.mult).then_inc(S.z_done, 1)
                        if it[1] == 1:
                            for i in range(HALF):
                                j = HALF * it[2] + i
                                dve.wait_ge(S.b_hi, j + 1)
                                rest(bl[:, j], z[:, j], bh[:, j]).then_inc(S.b_lo, 1)
                    if k == "nf":
                        n = it[1]
                        dve.wait_ge(S.ms_sum, n + 1)
                        link(nc.vector.tensor_scalar(ms[:], ps[:, BANKS, 0:T], 1.0 / D_MODEL, EPS, ALU.mult, ALU.add))
                        nc.vector.reciprocal(ms[:], ms[:]).then_inc(S.ms_rec, 1)
                        if n:
                            split_to(N_SLAB + SPL)
                            dve.wait_ge(slab_lo, len(SPLITS))
                    if k == "u":
                        n = it[1]
                        if n:
                            dve.wait_ge(S.rstd_done, n)
                        for j in range(KC + 1):
                            if j < KC:
                                g = (C_N1, C_N2)[n] + j
                                nc.vector.scalar_tensor_tensor(out=utmp[:, j], in0=h[:, j], scalar=par[:, g:g + 1],
                                                                   in1=rstd[:], op0=ALU.mult, op1=ALU.mult).then_inc(S.u_f32, 1)
                            if j:
                                dve.wait_ge(S.u_hi, nth("u"))
                                rest(ul[:, j - 1], utmp[:, j - 1], uh[:, j - 1]).then_inc(S.u_lo, 1)
                    if k == "hy":
                        j = it[1]
                        y, x = hy_dst(j), bank(it)
                        dve.wait_ge(S.hy_tap, plan.place(it))
                        col = C_HW + j
                        link(nc.vector.scalar_tensor_tensor(out=y[:, 1:T], in0=x[:, 0:T - 1], scalar=par[:, col:col + 1],
                                                            in1=y[:, 1:T], op0=ALU.mult, op1=ALU.add))
                        col += 48
                        nc.vector.scalar_tensor_tensor(out=y[:, 0:T - 1], in0=x[:, 1:T], scalar=par[:, col:col + 1],
                                                           in1=y[:, 0:T - 1], op0=ALU.mult, op1=ALU.add).then_inc(S.hy_done, 1)
                    if k == "lx":
                        j = it[1]
                        y, x = xc[:, j], bank(it)
                        dve.wait_ge(S.lx_tap, j + 1)
                        for i, a, b in ((0, 2, 0), (1, 1, 0), (3, 0, 1)):
                            col = C_LW + i * KC + j
                            n = T - max(a, b)
                            ins = nc.vector.scalar_tensor_tensor(out=y[:, a:a + n], in0=x[:, b:b + n],
                                                                 scalar=par[:, col:col + 1], in1=y[:, a:a + n],
                                                                 op0=ALU.mult, op1=ALU.add)
                            if i < 3:
                                link(ins)
                        ins.then_inc(S.lx_done, 1)
                    if k == "LX":
                        f = it[1]
                        dve.wait_ge(S.lx_hi, f + 1)
                        rest(ll[:, 4 * f:4 * f + 4], xc[:, 4 * f:4 * f + 4], lh[:, 4 * f:4 * f + 4]).then_inc(S.lx_lo, 1)
                    if k == "G":
                        split_to(plan.first_slab[it] + 2 + SPL)
                    if k == "Lb":
                        split_to(plan.first_slab[it] + 2 + SPL)
                    if k == "Lt":
                        for d in range(2):
                            dve.wait_ge(S.lru_a2, 2 * it[1] + d + 1)
                            nc.vector.scalar_tensor_tensor(out=lth[:, d], in0=la2[:, d], scalar=1.0, in1=lth[:, d],
                                                           op0=ALU.add, op1=ALU.mult).then_inc(S.lru_th, 1)
                    if k == "Le":
                        dve.wait_ge(S.lru_sq, 2 * it[1] + 1)
                        dve.wait_ge(S.lru_ix, 2 * it[1] + 1)
                        nc.vector.tensor_tensor(li[:, 0], li[:, 0], lth[:, 0], ALU.mult).then_inc(S.lru_b, 1)
                    if k in ("Le", "Lf"):
                        f, d = it[1], "ef".index(k[1])
                        way = (lambda t: t, lambda t: t[:, ::-1])[d]
                        dve.wait_ge((S.lru_b, S.lru_b1)[d], f + 1)
                        for n in range(HALF):
                            ins = nc.vector.tensor_tensor_scan(way(la2[:, d, n]), way(lr[:, d, n]), way(li[:, d, n]), 0.0,
                                                               ALU.mult, ALU.add)
                        ins.then_inc(S.lru_scan, 1)
                        if d == 1:
                            dve.wait_ge(S.lru_scan, 2 * (f + 1))
                            nc.vector.tensor_tensor(lth[:, 0], la2[:, 0], la2[:, 1], ALU.add).then_inc(S.lru_sum, 1)
                    if k == "Lh":
                        f = it[1]
                        dve.wait_ge(S.l_hi, f + 1)
                        rest(ll[:, 4 * f:4 * f + 4], lth[:, 0], lh[:, 4 * f:4 * f + 4]).then_inc(S.l_lo, 1)
                    if k == "mp":
                        b, j = it[1:]
                        g = plan.place(("mg", b, j))
                        s = sg[:, (g - 1) % SG]
                        dve.wait_ge(S.mg_done, g)
                        dve.wait_ge(*made(it))
                        if b == 0:
                            nc.vector.tensor_tensor(merged[:, j], s, bank(it), ALU.mult).then_inc(S.mp_done, 1)
                        else:
                            dve.wait_ge(S.mp_done, 8 * b)
                            link(nc.vector.tensor_tensor(s, s, bank(it), ALU.mult))
                            nc.vector.tensor_tensor(merged[:, j], merged[:, j], s, ALU.add).then_inc(S.mp_done, 1)
                    if k in ("rq", "rk"):
                        r = rope_place(it)
                        a, b = rot["qk".index(k[1])]
                        split_to(plan.first_slab[it] + 1 + SPL)
                        dve.wait_ge(*made(it))
                        if r > 2:
                            dve.wait_ge(S.rope_lo, r - 2)
                        link(nc.vector.tensor_tensor(a[:], pair(it), cs[:, 0:1].to_broadcast([P, 2, T]), ALU.mult))
                        nc.vector.tensor_tensor(b[:], pair(it), cs[:, 1:2].to_broadcast([P, 2, T]), ALU.mult) \
                            .then_inc(S.rope_ab, 1)
                    if k in ("rv", "rg"):
                        split_to(plan.first_slab[it] + 1 + SPL)
                    if k in ("qlo", "klo"):
                        x = "qk".index(k[0])
                        dve.wait_ge(S.rope_hi, 2 * it[1] + x + 1)
                        rest(qk_l[:, x], rot[x][0][:], qk_h[:, x]).then_inc(S.rope_lo, 1)
                    if k == "RT":
                        for cc, (_, cn) in enumerate(CHUNKS):
                            dve.wait_ge(S.vt_hi, 3 * it[1] + max(cc + 1, 2))
                            rest(vt_l[0:cn, cc], values(it, cc), vt_h[0:cn, cc]).then_inc(S.vt_lo, 1)
                    if k == "RS":
                        def lo(cc):
                            cn = CHUNKS[cc][1]
                            n = nth("sc_lo")
                            dve.wait_ge(S.sc_hi, n)
                            rest(sc_l[0:cn, cc], sc[0:cn, n % 2], sc_h[0:cn, cc]).then_inc(S.sc_lo, 1)
                        dve.wait_ge(dec_in, 16)
                        for cc, (_, cn) in enumerate(CHUNKS):
                            n = nth("sc")
                            dve.wait_ge(*made((*it, cc)))
                            if n > 2:
                                dve.wait_ge(S.sc_lo, n - 2)
                            nc.vector.tensor_tensor(sc[0:cn, n % 2], bank((*it, cc), cn), dec[0:cn, cc, it[1]],
                                                        ALU.mult).then_inc(S.sc_read, 1)
                            if cc:
                                lo(cc - 1)
                        lo(2)
                    if k == "RM":
                        dve.wait_ge(*made(it))
                        for e in range(2):
                            ins = nc.vector.scalar_tensor_tensor(out=ry[:, e], in0=bank(it), scalar=-1.0 / 256,
                                                                 in1=ry[:, e], op0=ALU.mult, op1=ALU.add)
                            if e == 0:
                                link(ins)
                        ins.then_inc(S.mean_done, 1)
                    if k == "RV":
                        n = it[1]
                        dve.wait_ge(*made(it))
                        nc.vector.tensor_scalar(ms[:], bank(it), 1.0 / 256, EPS, ALU.mult, ALU.add).then_inc(S.var_in, 1)
                        dve.wait_ge(S.var_in, n + 1)
                        nc.vector.reciprocal(ms[:], ms[:]).then_inc(S.var_rec, 1)
                    if k == "RQ":
                        n = it[1]
                        dve.wait_ge(S.rstd_r, n + 1)
                        dve.wait_ge(S.rg_done, n + 1)
                        link(nc.vector.tensor_tensor(ry[:], ry[:], gs[:], ALU.mult))
                        nc.vector.tensor_tensor(ry[:], ry[:], rstd[:, None, :].to_broadcast([P, 2, T]), ALU.mult).then_inc(S.yb_done, 1)
                    if k == "RN":
                        n = it[1]
                        dve.wait_ge(S.b_hi, KC + n + 1)
                        rest(bl[:, 2 * n:2 * n + 2], ry[:], bh[:, 2 * n:2 * n + 2]).then_inc(S.b_lo, 1)
                    if k == "ms":
                        f = it[1]
                        dve.wait_ge(S.m_hi, f + 1)
                        rest(ll[:, 2 * f:2 * f + 2], merged[:, 2 * f:2 * f + 2], lh[:, 2 * f:2 * f + 2]).then_inc(S.m_lo, 1)
                    if k in ("wo", "dn"):
                        j = it[1]
                        if k == "dn":
                            for m in range(j * FT // KC, (j + 1) * FT // KC):
                                split_to(plan.first_down + m + SPL)
                        dve.wait_ge(*made(it))
                        nc.vector.tensor_tensor(h[:, j], h[:, j], bank(it), ALU.add).then_inc(S.wo_done if k == "wo" else S.dn_done, 1)
                    if k == "fu":
                        i = it[1]
                        s = sg[:, i % SG]
                        dve.wait_ge(S.fg_done, i + 1)
                        dve.wait_ge(*made(it))
                        nc.vector.tensor_tensor(s, s, bank(it), ALU.mult).then_inc(S.hid_f32, 1)
                        dve.wait_ge(S.hid_hi, i + 1)
                        rest(hl[:, i], s, hh[:, i]).then_inc(S.hid_lo, 1)

            @block.tensor
            def _(pe):
                slab_at = [0]

                def free(job):
                    for j in plan.before[job]:
                        reader, n = freed(j)
                        pe.wait_ge(reader, n)

                def passes(dst, tiles):
                    n = len(tiles)
                    for i, (sh, sl, mh, ml) in enumerate(tiles):
                        nc.tensor.matmul(dst, sh, mh, start=(i == 0), stop=False)
                        nc.tensor.matmul(dst, sl, mh, start=False, stop=False)
                        ins = nc.tensor.matmul(dst, sh, ml, start=False, stop=(i == n - 1))
                    return ins

                def weight(slab, t):
                    return wh[:, hi_slot(slab), t * P:(t + 1) * P], wl[:, raw_slot(slab), t * P:(t + 1) * P]

                def wait_split(n):
                    if n >= SPL:
                        pe.wait_ge(slab_lo, n - SPL + 1)

                def project(dst, xh, xl, ready=None):
                    n = slab_at[0]
                    slab_at[0] += 1
                    wait_split(n)
                    for t in range(KC):
                        if ready:
                            pe.wait_ge(ready[0], ready[1][t])
                        (sh, sl), first = weight(n, t), t == 0
                        nc.tensor.matmul(dst, sh, xh[:, t], start=first, stop=False)
                        nc.tensor.matmul(dst, sl, xh[:, t], start=False, stop=False)
                        ins = nc.tensor.matmul(dst, sh, xl[:, t], start=False, stop=(t == KC - 1))
                    return ins

                def transform(dst, columns, terms):
                    n = len(terms)
                    for i, (vh, vl, vs, at_) in enumerate(terms):
                        cols = slice(columns + at_, columns + at_ + P)
                        for p in range(2):
                            nc.tensor.matmul(dst, fwd_h[:, p, cols], vh(p), start=(i == p == 0), stop=False)
                            nc.tensor.matmul(dst, fwd_l[:, p, cols], vh(p), start=False, stop=False)
                            nc.tensor.matmul(dst, fwd_h[:, p, cols], vl(p), start=False, stop=False)
                        ins = nc.tensor.matmul(dst, fwd_s[:, cols], vs, start=False, stop=(i == n - 1))
                    return ins

                for it in plan.items:
                    k = it[0]
                    if k == "M":
                        if it[1]:
                            pe.wait_ge(S.mlp_sin, it[1])
                        else:
                            pe.wait_ge(S.par_next, 32)
                        free(it)
                        mlp_product(it[1], ps[:, plan.bank[it]]).then_inc(full[plan.nth[it][0]], 1)
                    if k == "Fs":
                        o, f = it[1:]
                        kn = 2 * o + f
                        pe.wait_ge(S.hdn, 2)
                        if kn:
                            pe.wait_ge(win_in, 32 * kn)
                        for c in range(3):
                            for x in range(2):
                                job = ("Fs", o, f, c, x)
                                w = (hdn_s, hdn_d)[x][:, c * P:(c + 1) * P] if c < 2 else \
                                    hdn_t[:, x].rearrange("p a b -> p (a b)")
                                free(job)
                                nc.tensor.matmul(bank(job, ROWS[c], NF), w, wo_t[:],
                                                 start=True, stop=True).then_inc(full[plan.nth[job][0]], 1)
                    if k == "FK":
                        o, f = it[1:]
                        pe.wait_ge(S.sd_lo, 6 * (2 * o + f + 1))
                        term = [(lambda p, x=x: sp_h[:, p, x], lambda p, x=x: sp_l[:, p, x], sd_s[:, x]) for x in range(2)]
                        for c, x in SPECTRA:
                            job = ("FK", o, f, c, x)
                            free(job)
                            if c < 2:
                                transform(bank(job, P, NF), (2 * x + c) * P, [(*term[x], 0)]) \
                                    .then_inc(full[plan.nth[job][0]], 1)
                            else:
                                transform(bank(job, P, NF), 4 * P, [(*term[0], 0), (*term[1], P)]) \
                                    .then_inc(full[plan.nth[job][0]], 1)
                    if k == "T":
                        o, f = it[1:]
                        if o == 0:
                            pe.wait_ge(S.hy_done, plan.place(("hy", 16 + 4 * f + 3)))
                        else:
                            pe.wait_ge(S.z_done, 4 * f + 4)
                        for c in range(3):
                            job = (*it, c)
                            free(job)
                            if c == 2:
                                pe.wait_ge(S.z_tail, plan.place(it))
                            for i in range(HALF):
                                src = z[:, HALF * f + i, c * P:(c + 1) * P] if c < 2 else \
                                    z_t[:, i].rearrange("p a b -> p (a b)")
                                ins = nc.tensor.transpose(ps[0:ROWS[c], plan.bank[job], i * P:(i + 1) * P], src, ident[:])
                            ins.then_inc(full[plan.nth[job][0]], 1)
                    if k == "W":
                        pe.wait_ge(S.zt_lo, 3 * plan.place(it))
                        for c, x in SPECTRA:
                            job = (*it, c, x)
                            free(job)
                            transform(bank(job, P, NF), (2 * x + c) * P if c < 2 else 6 * P,
                                      [(lambda p: zt_h[:, p], lambda p: zt_l[:, p], zt_s[:], 0)]) \
                                .then_inc(full[plan.nth[job][0]], 1)
                    if k == "I":
                        pe.wait_ge(S.pq_lo, 5 * plan.place(it))
                        for i in range(HALF):
                            job = (*it, i)
                            cols = slice(i * P, (i + 1) * P)
                            free(job)
                            for n in range(4):
                                c, x = n // 2, n % 2
                                nc.tensor.matmul(bank(job), sp_h[:, c, x, cols], inv_h[:, c, x], start=(n == 0), stop=False)
                                nc.tensor.matmul(bank(job), sp_l[:, c, x, cols], inv_h[:, c, x], start=False, stop=False)
                                nc.tensor.matmul(bank(job), sp_h[:, c, x, cols], inv_l[:, c, x], start=False, stop=False)
                            nc.tensor.matmul(bank(job), sp_s[:, cols], inv_s[:], start=False, stop=False)
                            nc.tensor.matmul(bank(job), sp_s[0:P // 2, cols], inv_sl[:], start=False, stop=True) \
                                .then_inc(full[plan.nth[job][0]], 1)
                    if k == "nq" and it[2] == KC - 1:
                        n, j = it[1:]
                        if n == 1:
                            pe.wait_ge(S.ms_rec, 1)
                        pe.wait_ge(S.sq_sum, (KC - 2) * (n + 1))
                        nc.tensor.matmul(ps[:, BANKS, 0:T], ones[:], utmp[:, j - 1], start=True, stop=False)
                        pe.wait_ge(S.sq_done, KC * (n + 1))
                        nc.tensor.matmul(ps[:, BANKS, 0:T], ones[:], utmp[:, j], start=False, stop=True).then_inc(S.ms_sum, 1)
                    if it in TOGETHER:
                        group = [it] + TOGETHER[it]
                        for j in group:
                            free(j)
                        for t in range(KC):
                            pe.wait_ge(S.u_lo, KC * (k == "fg") + t + 1)
                            for n, j in enumerate(group):
                                wait_split(slab_at[0] + n)
                                sh, sl = weight(slab_at[0] + n, t)
                                nc.tensor.matmul(bank(j), sh, uh[:, t], start=(t == 0), stop=False)
                                nc.tensor.matmul(bank(j), sl, uh[:, t], start=False, stop=False)
                                ins = nc.tensor.matmul(bank(j), sh, ul[:, t], start=False, stop=(t == KC - 1))
                                if t == KC - 1:
                                    ins.then_inc(full[plan.nth[j][0]], 1)
                        slab_at[0] += len(group)
                    elif k in ("hy", "lx", "lg", "mg", "fg", "fu") and not any(it in g for g in TOGETHER.values()):
                        free(it)
                        project(bank(it), uh, ul).then_inc(full[plan.nth[it][0]], 1)
                    if k in ("rq", "rk", "rv", "rg"):
                        free(it)
                        project(ps[:, plan.bank[it], 0:T], uh, ul).then_inc(S.pair_slab, 1)
                        project(ps[:, plan.bank[it] + 1, 0:T], uh, ul).then_inc(full[plan.nth[it][0]], 1)
                    if k == "mp":
                        free(it)
                        ready = None
                        if it[2] == 0:
                            ready = [(S.b_lo, [t + 1 for t in range(KC)]), (S.l_lo, [1] * 4 + [2] * 4),
                                     (S.b_lo, [KC + t // 2 + 1 for t in range(KC)])][it[1]]
                        project(bank(it), *((lh, ll) if it[1] == 1 else (bh, bl)), ready).then_inc(full[plan.nth[it][0]], 1)
                    if k == "G":
                        f = it[1]
                        pe.wait_ge(S.lx_lo, f + 1)
                        for n in range(HALF):
                            slab = slab_at[0]
                            if n % 2 == 0:
                                wait_split(slab)
                            for d in range(2):
                                for g in range(2):
                                    job = ("G", HALF * f + n, d, g)
                                    free(job)
                                    passes(bank(job), [(*weight(slab, (n % 2) * 4 + 2 * d + g),
                                                             lh[:, HALF * f + n], ll[:, HALF * f + n])]).then_inc(full[plan.nth[job][0]], 1)
                            if n % 2 == 1:
                                slab_at[0] += 1
                    if k == "RT":
                        pe.wait_ge(S.rv_done, it[1] + 1)
                        for c, (c0, cn) in enumerate(CHUNKS):
                            job = (*it, c // 2)
                            if c != 1:
                                free(job)
                            for e in range(2):
                                ins = nc.tensor.transpose(values(it, c)[:, e * P:(e + 1) * P],
                                                          rv[:, e, c0:c0 + cn], ident[:])
                            if c != 0:
                                ins.then_inc(full[plan.nth[job][0]], 1)
                    if k == "RS":
                        pe.wait_ge(S.rope_lo, 2 * (it[1] + 1))
                        for c, (c0, cn) in enumerate(CHUNKS):
                            job = (*it, c)
                            free(job)
                            passes(bank(job, cn), [(qk_h[:, 1, e, c0:c0 + cn], qk_l[:, 1, e, c0:c0 + cn],
                                                         qk_h[:, 0, e], qk_l[:, 0, e]) for e in range(2)]).then_inc(full[plan.nth[job][0]], 1)
                    if k == "RP":
                        free(it)
                        for e in range(2):
                            for c, (_, n) in enumerate(CHUNKS):
                                if e == 0:
                                    pe.wait_ge(S.vt_lo, 3 * it[1] + c + 1)
                                    pe.wait_ge(S.sc_lo, 3 * it[1] + c + 1)
                                dst, vh = ps[:, plan.bank[it] + e, 0:T], vt_h[0:n, c, e * P:(e + 1) * P]
                                nc.tensor.matmul(dst, vh, sc_h[0:n, c], start=(c == 0), stop=False)
                                nc.tensor.matmul(dst, vt_l[0:n, c, e * P:(e + 1) * P], sc_h[0:n, c], start=False, stop=False)
                                ins = nc.tensor.matmul(dst, vh, sc_l[0:n, c], start=False, stop=(c == 2))
                        ins.then_inc(full[plan.nth[it][0]], 1)
                    if k == "RM":
                        pe.wait_ge(S.y_sum, it[1] + 1)
                        free(it)
                        nc.tensor.matmul(bank(it), ones[:], ysum[:], start=True, stop=True).then_inc(full[plan.nth[it][0]], 1)
                    if k == "RV":
                        pe.wait_ge(S.rsq_sum, it[1] + 1)
                        free(it)
                        nc.tensor.matmul(bank(it), ones[:], rsq[:, 0], start=True, stop=True).then_inc(full[plan.nth[it][0]], 1)
                    if k == "wo":
                        free(it)
                        project(bank(it), lh, ll, None if it[1] else (S.m_lo, [t // 2 + 1 for t in range(KC)])).then_inc(full[plan.nth[it][0]], 1)
                    if k == "dn":
                        j = it[1]
                        free(it)
                        for i in range(FT):
                            g = FT * j + i
                            m = g // 8
                            slab = plan.first_down + m
                            if g % 8 == 0 or i == 0:
                                wait_split(slab)
                            if j == 0:
                                pe.wait_ge(S.hid_lo, i + 1)
                            a, b = weight(slab, g % 8)
                            nc.tensor.matmul(bank(it), a, hh[:, i], start=(i == 0), stop=False)
                            nc.tensor.matmul(bank(it), b, hh[:, i], start=False, stop=False)
                            ins = nc.tensor.matmul(bank(it), a, hl[:, i], start=False, stop=(i == FT - 1))
                            if g % 8 == 7 and i != FT - 1:
                                ins.then_inc(down_slab, 1)
                        ins.then_inc(full[plan.nth[it][0]], 1)

        n_layer = len(sems)
        with nc.Fori(0, DEPTH) as layer:
            with nc.Block() as block:
                layer_body(layer, block)
            nc.all_engine_barrier(sems_to_clear=range(sems[0].num, sems[n_layer - 1].num + 1))

        e_y, e_out = sem("e_y"), sem("e_out")
        with nc.Block() as block:
            @block.vector
            def _(dve):
                for j in range(KC):
                    nc.vector.scalar_tensor_tensor(out=utmp[:, j, N_META:T], in0=h[:, j, N_META:T],
                                                   scalar=finp[:, j:j + 1], in1=rstd[:, N_META:T],
                                                   op0=ALU.mult, op1=ALU.mult).then_inc(e_y, 1)

            @block.sync
            def _(sp):
                for q in range(4):
                    sp.wait_ge(e_y, 2 * q + 2)
                    sp.dma_start(out[:, 2 * q:2 * q + 2], utmp[:, 2 * q:2 * q + 2, N_META:T]).then_inc(e_out, 16)
                sp.wait_ge(e_out, 64)


def constants():
    n2 = 2 * T
    pos = np.arange(T, dtype=np.float64)
    ang = 2 * np.pi * (pos[:, None] + 0.5) * pos[None, :] / n2

    def chunked(a):
        r = np.zeros((CM, 3, *a.shape[1:]), np.float32)
        for c, (c0, cn) in enumerate(CHUNKS):
            r[:cn, c] = a[c0:c0 + cn]
        return r

    def rows(a):
        return np.ascontiguousarray(a[:2 * P].reshape(2, P, -1).transpose(1, 0, 2)).astype(np.float32)

    fc, fs = np.cos(ang.T), -np.sin(ang.T)
    rc, rs, no = fc[:, 2 * P:], fs[:, 2 * P:], np.zeros((T, REM))
    fwd = np.concatenate([fc[:, :2 * P], fs[:, :2 * P]] + 2 * [rc, no, no, rc] + 2 * [no, rs, rs, no]
                         + 4 * [rc, rs], 1)
    tail = fwd[T - TAIL:].copy()
    tail[:TAIL - REM] = 0
    ic, is_ = np.cos(ang) * (2.0 / n2), -np.sin(ang) * (2.0 / n2)
    cinv = rows(np.concatenate([ic, is_], 1)).reshape(P, 2, 2, T)
    cinv_s = np.concatenate(2 * [ic[2 * P:], -ic[2 * P:], is_[2 * P:], is_[2 * P:]]).astype(np.float32)
    half = 128
    inv = np.power(10000.0, -np.linspace(0.0, 1.0, half, dtype=np.float32).astype(np.float64)).astype(np.float32)
    a = (np.arange(T, dtype=np.float32)[None, :] * inv[:, None]).astype(np.float64)
    rope = np.stack([np.cos(a), np.sin(a)], 1).astype(np.float32)
    dist = np.abs(pos[:, None] - pos[None, :])
    lg = np.log1p(-(2.0 ** (-5.0 - np.arange(HEADS))))
    decay = chunked((np.exp(dist[:, None, :] * lg[None, :, None]) / 16.0))
    tn = (np.arange(T, dtype=np.float32) / np.float32(T - 1)).astype(np.float64)
    lo, hi = np.log(1e-2) / 1.5, np.log(1e-2) / 0.3
    deltas = np.abs(np.linspace(lo, hi, D_MODEL).astype(np.float32)).astype(np.float64)
    w = np.exp(-tn[:, None] * deltas[None, :])
    window = np.zeros((P, 3, D_MODEL), np.float32)
    window[:, :2] = rows(w)
    window[:3 * TAIL, 2] = np.concatenate(3 * [w[T - TAIL:]])
    bands = np.linspace(1e-4, BANDS - 1, BANDS).astype(np.float32)
    w = (np.float32(2 * np.pi / T) * np.arange(T, dtype=np.float32)[:, None] * bands[None, :]).astype(np.float64)
    zfeat = np.concatenate([tn[:, None], np.cos(w), np.sin(w)], 1).T.astype(np.float32)
    return {"cfwd": rows(fwd), "cinv": cinv, "cfwd_s": np.concatenate(3 * [tail]).astype(np.float32), "cinv_s": cinv_s, "rope": rope, "decay": decay, "window": window,
            "zfeat": np.ascontiguousarray(zfeat), "ident_in": np.eye(P, dtype=np.float32)}


def lay_out(i):
    f32 = np.float32
    hseq = np.concatenate([i["meta_tokens"], i["x"][0]], 0)
    a = {"h0": hseq.T.reshape(KC, P, T).transpose(1, 0, 2)}

    slabs = np.empty((DEPTH * N_SLAB + SPL, P, KC, P), f32)
    for l in range(DEPTH):
        tiles = lambda w: w.reshape(w.shape[0] // P, P, w.shape[1] // P, P)
        src = {
            "in": tiles(i["w_in"][l]).transpose(2, 1, 0, 3),
            "branch": np.concatenate([tiles(i["w_branch"][l, b]).transpose(2, 1, 0, 3) for b in range(3)]),
            "out": tiles(i["w_out"][l]).transpose(2, 1, 0, 3),
            "gate": i["lru_gate_w"][l].reshape(4, 4, 2, P, P).transpose(1, 3, 2, 0, 4).reshape(4, P, KC, P),
            "gu": tiles(i["ffn_w_gu"][l]).transpose(2, 1, 0, 3),
            "down": tiles(i["ffn_w_down"][l]).transpose(2, 0, 1, 3).reshape(FT, 8, P, P).transpose(0, 2, 1, 3),
        }
        for n, (kind, at) in enumerate(PLAN.slabs):
            slabs[l * N_SLAB + n] = src[kind][at]
    slabs[DEPTH * N_SLAB:] = slabs[:SPL]
    a["slabs"] = slabs.reshape(-1, P, KC * P)

    rows = lambda x: x.reshape(-1, P).T
    ahead = lambda x, n: np.concatenate([x, x[:n]])
    a["params"] = ahead(np.stack([np.concatenate([rows(i[n][l]) for n in (
        "norm1_g", "norm2_g", "hy_conv_w", "hy_conv_b", "hy_skip", "lru_conv_w", "lru_conv_b", "lru_gate_b",
        "lru_lambda")], 1) for l in range(DEPTH)]), 1)
    filt = np.zeros((DEPTH, P, N_FIL), f32)
    for l in range(DEPTH):
        filt[l, :EMB, C_W1:C_W1 + HID] = i["hy_f_w1"][l]
        filt[l, :HID, C_W2:C_W2 + HID] = i["hy_f_w2"][l]
        for s in range(2):
            r = slice(s * HID, (s + 1) * HID)
            filt[l, :HID, C_W3 + s * HID:C_W3 + (s + 1) * HID] = i["hy_f_w3"][l]
            for col, n in ((C_B1, "hy_f_b1"), (C_B2, "hy_f_b2"), (C_B3, "hy_f_b3"), (C_FR, "hy_f_freq")):
                filt[l, r, col] = i[n][l]
        filt[l, :HID, C_SGN] = 1.0
        filt[l, HID:, C_SGN] = -1.0
    a["filt"] = ahead(filt, 1)
    wo = i["hy_f_wout"].reshape(DEPTH, HID, 2, 2, 2, NF).transpose(0, 2, 4, 3, 1, 5)
    a["wout"] = ahead(wo.reshape(DEPTH * 4, P, NF), 1)
    a["fin_g"] = rows(i["final_g"])
    a.update(constants())
    return {n: np.ascontiguousarray(v) for n, v in a.items()}


def kernel(**inputs):
    import concourse.bacc as bacc
    from concourse.bass_utils import run_bass_kernel_spmd as run

    arrays = lay_out({n: np.asarray(v) for n, v in inputs.items()})
    nc = bacc.Bacc("TRN2", target_bir_lowering=False, num_devices=1)
    aps = {n: nc.dram_tensor(n, a.shape, F32, kind="ExternalInput").ap() for n, a in arrays.items()}
    out = nc.dram_tensor("out", (P, KC, SEQ), F32, kind="ExternalOutput").ap()
    build(nc, out=out, **aps)
    r = run(nc, [arrays], core_ids=[0])
    got = r.results[0]["out"]
    return np.ascontiguousarray(got.transpose(2, 1, 0)).reshape(1, SEQ, D_MODEL)
```
